# Optimizing a Trainium2 kernel written in Bass

```python
import jax, jax.numpy as jnp
from jax import lax
import numpy as np

D_MODEL = 1024
BATCH = 1
SEQ = 128
DEPTH = 2
DEC_BATCH = 1
DEC_SEQ = 512
PAST_LEN = 128

GRID_W = 64
N_MIXERS = 2
N_ATTN_LAYERS = (DEPTH + 1) // 2
N_POOL_LAYERS = DEPTH // 2
HEAD_DIM = 128
N_HEADS = D_MODEL // HEAD_DIM
N_KV_HEADS = N_HEADS // 4
QKV_DIM = (N_HEADS + 2 * N_KV_HEADS) * HEAD_DIM
ROPE_THETA = 10000.0
Q_BLOCK = 128
POOL_WINDOWS = (2, 4, 8, 16)
N_POOL_GROUPS = len(POOL_WINDOWS)
POOL_GROUP_DIM = D_MODEL // N_POOL_GROUPS
N_EXPERTS = 16
CAPACITY_FACTOR = 2
D_FF_EXPERT = D_MODEL
N_MOD = 6
EPS = 1e-6

kernel_name = "hybrid_dit_attn_pool_ecmoe_step"

def rms_norm(x, gain):
    x32 = x.astype(jnp.float32)
    y = x32 * lax.rsqrt(jnp.mean(x32 * x32, axis=-1, keepdims=True) + EPS)
    return (y * gain.astype(jnp.float32)).astype(x.dtype)

def modulate(h, shift, scale):
    return h * (1 + scale) + shift

def rope_1d(x, pos):
    n = x.shape[-1] // 2
    inv_freq = ROPE_THETA ** (-jnp.arange(n, dtype=jnp.float32) / n)
    ang = pos.astype(jnp.float32)[:, None] * inv_freq[None, :]
    cos = jnp.cos(ang)[:, None, :]
    sin = jnp.sin(ang)[:, None, :]
    x32 = x.astype(jnp.float32)
    x1, x2 = x32[..., :n], x32[..., n:]
    return jnp.concatenate([x1 * cos - x2 * sin, x1 * sin + x2 * cos], axis=-1).astype(x.dtype)

def axial_rope(x):
    L = x.shape[1]
    rows = L // GRID_W
    row = jnp.repeat(jnp.arange(rows), GRID_W)
    col = jnp.tile(jnp.arange(GRID_W), rows)
    half = HEAD_DIM // 2
    return jnp.concatenate([rope_1d(x[..., :half], row), rope_1d(x[..., half:], col)], axis=-1)

def qkv_proj(h, w_qkv, q_gain, k_gain):
    B, L, _ = h.shape
    qkv = h @ w_qkv
    q, k, v = jnp.split(qkv, [N_HEADS * HEAD_DIM, (N_HEADS + N_KV_HEADS) * HEAD_DIM], axis=-1)
    q = rms_norm(q.reshape(B, L, N_HEADS, HEAD_DIM), q_gain)
    k = rms_norm(k.reshape(B, L, N_KV_HEADS, HEAD_DIM), k_gain)
    v = v.reshape(B, L, N_KV_HEADS, HEAD_DIM)
    return q, k, v

def blocked_attention(q, k, v):
    B, L, H, Dh = q.shape
    KV = k.shape[2]
    G = H // KV
    nb = L // Q_BLOCK
    qb = jnp.moveaxis(q.reshape(B, nb, Q_BLOCK, KV, G, Dh), 1, 0)
    k32 = k.astype(jnp.float32)
    scale = Dh ** -0.5

    def one_block(qi):
        s = jnp.einsum("bqkgd,bskd->bkgqs", qi.astype(jnp.float32), k32) * scale
        p = jax.nn.softmax(s, axis=-1)
        return jnp.einsum("bkgqs,bskd->bqkgd", p.astype(v.dtype), v)

    o = lax.map(one_block, qb)
    return jnp.moveaxis(o, 0, 1).reshape(B, L, H * Dh)

def pool_mix(h, w_pool, pool_scale):
    B, L, D = h.shape
    h32 = h.astype(jnp.float32)
    cs = jnp.concatenate([jnp.zeros((B, 1, D), jnp.float32), lax.cumsum(h32, axis=1)], axis=1)
    t = jnp.arange(L)
    outs = []
    for g, w in enumerate(POOL_WINDOWS):
        lo = jnp.clip(t - w // 2, 0, L)
        hi = jnp.clip(t + w - w // 2, 0, L)
        sl = slice(g * POOL_GROUP_DIM, (g + 1) * POOL_GROUP_DIM)
        csg = cs[..., sl]
        mean = (csg[:, hi] - csg[:, lo]) / (hi - lo).astype(jnp.float32)[None, :, None]
        outs.append(mean - h32[..., sl])
    d = jnp.stack(outs, axis=2).astype(h.dtype)
    y = jnp.einsum("blgc,gcd->blgd", d, w_pool).reshape(B, L, D)
    return y * pool_scale

def expert_choice_ffn(h, w_router, w_gate, w_up, w_down):
    B, L, D = h.shape
    n_tok = B * L
    cap = CAPACITY_FACTOR * n_tok // N_EXPERTS
    xf = h.reshape(n_tok, D)
    aff = jax.nn.softmax((xf @ w_router).astype(jnp.float32), axis=-1)
    gates, idx = lax.top_k(aff.T, cap)
    xe = xf[idx]
    a = jnp.einsum("ecd,edf->ecf", xe, w_gate)
    u = jnp.einsum("ecd,edf->ecf", xe, w_up)
    ye = jnp.einsum("ecf,efd->ecd", jax.nn.silu(a) * u, w_down) * gates[..., None].astype(h.dtype)
    out = jnp.zeros_like(xf).at[idx.reshape(-1)].add(ye.reshape(-1, D))
    return out.reshape(B, L, D)

def setup_inputs(seed: int = 0) -> dict:
    key = jax.random.key(seed)
    ks = jax.random.split(key, 20)
    f32 = jnp.float32
    nrm = lambda k, shape, s: jax.random.normal(k, shape, f32) * s
    return {
        "x_prompt": nrm(ks[0], (BATCH, SEQ, D_MODEL), 1.0),
        "x_sample": nrm(ks[1], (DEC_BATCH, DEC_SEQ, D_MODEL), 1.0),
        "cache_k": nrm(ks[2], (DEC_BATCH, N_ATTN_LAYERS, PAST_LEN, N_KV_HEADS, HEAD_DIM), 1.0),
        "cache_v": nrm(ks[3], (DEC_BATCH, N_ATTN_LAYERS, PAST_LEN, N_KV_HEADS, HEAD_DIM), 1.0),
        "c": nrm(ks[4], (DEC_BATCH, D_MODEL), 1.0),
        "c_ctx": nrm(ks[5], (D_MODEL,), 1.0),
        "norm1": 1.0 + nrm(ks[6], (DEPTH, D_MODEL), 0.01),
        "norm2": 1.0 + nrm(ks[7], (DEPTH, D_MODEL), 0.01),
        "w_ada": nrm(ks[8], (DEPTH, D_MODEL, N_MOD * D_MODEL), D_MODEL ** -0.5),
        "b_ada": nrm(ks[9], (DEPTH, N_MOD * D_MODEL), 0.01),
        "w_qkv": nrm(ks[10], (N_ATTN_LAYERS, D_MODEL, QKV_DIM), D_MODEL ** -0.5),
        "q_norm": 1.0 + nrm(ks[11], (N_ATTN_LAYERS, HEAD_DIM), 0.01),
        "k_norm": 1.0 + nrm(ks[12], (N_ATTN_LAYERS, HEAD_DIM), 0.01),
        "w_o": nrm(ks[13], (N_ATTN_LAYERS, N_HEADS * HEAD_DIM, D_MODEL), (N_HEADS * HEAD_DIM) ** -0.5),
        "w_pool": nrm(ks[14], (N_POOL_LAYERS, N_POOL_GROUPS, POOL_GROUP_DIM, POOL_GROUP_DIM), POOL_GROUP_DIM ** -0.5),
        "pool_scale": 1.0 + nrm(ks[15], (N_POOL_LAYERS, D_MODEL), 0.1),
        "w_router": nrm(ks[16], (DEPTH, D_MODEL, N_EXPERTS), D_MODEL ** -0.5),
        "w_e_gate": nrm(ks[17], (DEPTH, N_EXPERTS, D_MODEL, D_FF_EXPERT), D_MODEL ** -0.5),
        "w_e_up": nrm(ks[18], (DEPTH, N_EXPERTS, D_MODEL, D_FF_EXPERT), D_MODEL ** -0.5),
        "w_e_down": nrm(ks[19], (DEPTH, N_EXPERTS, D_FF_EXPERT, D_MODEL), D_FF_EXPERT ** -0.5),
    }

def reference(x_prompt, x_sample, cache_k, cache_v, c, c_ctx, norm1, norm2, w_ada, b_ada,
              w_qkv, q_norm, k_norm, w_o, w_pool, pool_scale, w_router, w_e_gate, w_e_up, w_e_down):
    ctx, lat = x_prompt, x_sample
    new_k, new_v = [], []
    for i in range(DEPTH):
        j = i // N_MIXERS
        mod_ctx = (jax.nn.silu(c_ctx) @ w_ada[i] + b_ada[i])[None, None, :]
        mod_lat = (jax.nn.silu(c) @ w_ada[i] + b_ada[i])[:, None, :]
        sh1_c, sc1_c, g1_c, sh2_c, sc2_c, g2_c = jnp.split(mod_ctx, N_MOD, axis=-1)
        sh1_l, sc1_l, g1_l, sh2_l, sc2_l, g2_l = jnp.split(mod_lat, N_MOD, axis=-1)

        hc = modulate(rms_norm(ctx, norm1[i]), sh1_c, sc1_c)
        hl = modulate(rms_norm(lat, norm1[i]), sh1_l, sc1_l)
        if i % N_MIXERS == 0:
            qc, kc, vc = qkv_proj(hc, w_qkv[j], q_norm[j], k_norm[j])
            new_k.append(kc)
            new_v.append(vc)
            oc = blocked_attention(qc, kc, vc) @ w_o[j]
            ql, kl, vl = qkv_proj(hl, w_qkv[j], q_norm[j], k_norm[j])
            ql = axial_rope(ql)
            kl = axial_rope(kl)
            keys = jnp.concatenate([kl, cache_k[:, j].astype(kl.dtype)], axis=1)
            vals = jnp.concatenate([vl, cache_v[:, j].astype(vl.dtype)], axis=1)
            ol = blocked_attention(ql, keys, vals) @ w_o[j]
        else:
            oc = pool_mix(hc, w_pool[j], pool_scale[j])
            ol = pool_mix(hl, w_pool[j], pool_scale[j])
        ctx = ctx + g1_c * oc
        lat = lat + g1_l * ol

        hc = modulate(rms_norm(ctx, norm2[i]), sh2_c, sc2_c)
        hl = modulate(rms_norm(lat, norm2[i]), sh2_l, sc2_l)
        ctx = ctx + g2_c * expert_choice_ffn(hc, w_router[i], w_e_gate[i], w_e_up[i], w_e_down[i])
        lat = lat + g2_l * expert_choice_ffn(hl, w_router[i], w_e_gate[i], w_e_up[i], w_e_down[i])

    new_cache_k = jnp.stack(new_k, axis=1)
    new_cache_v = jnp.stack(new_v, axis=1)
    return (ctx, lat, new_cache_k, new_cache_v)


_drawn_inputs = setup_inputs


def setup_inputs(seed=0):
    import zlib

    import numpy as np

    out = dict(_drawn_inputs(seed))
    spreads = {}
    factors = {'norm1': 4.55, 'q_norm': 6.544, 'k_norm': 6.173, 'norm2': 7.172}
    for name, (base, spread) in spreads.items():
        noise = np.random.default_rng([zlib.crc32(name.encode()), seed]).standard_normal(out[name].shape)
        drawn = base * np.exp(spread * noise) if base else spread * noise
        out[name] = __import__('jax').numpy.asarray(drawn.astype(out[name].dtype))
    for name, factor in factors.items():
        out[name] = (out[name] * factor).astype(out[name].dtype)
    return out
```

```python
from contextlib import ExitStack

import numpy as np

import concourse.bass as bass
from concourse import mybir

F32 = mybir.dt.float32
ALU = mybir.AluOpType
ACT = mybir.ActivationFunctionType
AX = mybir.AxisListType

P = 128
D = 1024
KD = D // P
LAT, CTX = 512, 128
T = LAT + CTX
TT = T // P
LT = LAT // P
PAST = 128
GRID_W = 64
HD = 128
NH, NKV = D // HD, D // HD // 4
G = NH // NKV
KEYS = LAT + PAST
NE = 16
CAP_L, CAP_C = 2 * LAT // NE, 2 * CTX // NE
CAP = CAP_L + CAP_C
NP = NE // 2
SEL_L, SEL_C = 2 * CAP_L, 2 * CAP_C
NMOD = 6
MC = NMOD * KD
EPS = 1e-6
THETA = 10000.0
WINDOWS = (2, 4, 8, 16)
PADZ = 8
Z_L, Z_C = PADZ, PADZ + LAT + 2 * PADZ
ZW = Z_C + CTX + PADZ
UC = 512
RING = 6
SH1, SC1, G1, SH2, SC2, G2 = (KD * m for m in range(NMOD))

V_C, V_CTX, V_N1, V_N2, V_PS, V_Q, V_K, V_ROWS = 0, 8, 16, 32, 48, 56, 57, 58
T_ID, T_SWAP, T_IOTA, T_INV, T_COS, T_SIN, T_COLS = 0, 128, 256, 320, 832, 1344, 1856


def shape_tables():
    f = np.float32
    tab = np.zeros((P, T_COLS), f)
    tab[:, T_ID:T_ID + P] = np.eye(P, dtype=f)
    p = np.arange(P)
    tab[p ^ 32, T_SWAP + p] = 1.0
    tab[:, T_IOTA:T_IOTA + CAP_L] = np.arange(1, CAP_L + 1, dtype=f)
    t = np.arange(CTX)
    for g, w in enumerate(WINDOWS):
        n = np.clip(t + w - w // 2, 0, CTX) - np.clip(t - w // 2, 0, CTX)
        tab[:, T_INV + CTX * g:T_INV + CTX * (g + 1)] = f(1) / n.astype(f)
    n = HD // 4
    inv_freq = np.power(f(THETA), -np.arange(n, dtype=f) / f(n)).astype(f)
    tok = np.arange(LAT)
    pos = np.stack([tok // GRID_W, tok % GRID_W]).astype(f)
    ang = pos[p // (2 * n)] * inv_freq[p % n][:, None]
    sign = np.where(p % (2 * n) < n, f(-1), f(1))[:, None]
    tab[:, T_COS:T_COS + LAT] = np.cos(ang)
    tab[:, T_SIN:T_SIN + LAT] = np.sin(ang) * sign
    return tab


def weight_order():
    u = [("ada0", n) for n in range(6)] + [("qkv", 2), ("qkv", 0)]
    u += [("ada0", n) for n in range(6, 10)] + [("qkv", 1)]
    u += [("ada0", 10), ("ada0", 11), ("ada1", 0), ("ada1", 1)]
    u += [("ada1", n) for n in range(2, 12)] + [("wo", 0), ("wo", 1)]
    return u


class PsumUses:

    def __init__(self):
        self.opened, self.filled = [0] * 8, [0] * 8
        self.at = {}

    def take(self, name, bank, unit=None):
        self.at[name] = (bank, self.opened[bank], 0, self.filled[bank], 0, unit)
        self.opened[bank] += 1
        self.filled[bank] += unit is None

    def loop(self, prefix, uses, trips, base):
        opens = [sum(b == bank for _, b, _ in uses) for bank in range(8)]
        fills = [sum(b == bank and u is None for _, b, u in uses) for bank in range(8)]
        o, f = list(self.opened), list(self.filled)
        for name, b, u in uses:
            self.at[prefix + name] = (b, o[b], opens[b], f[b], fills[b], None if u is None else base + u)
            o[b] += 1
            f[b] += u is None
        self.opened = [c + trips * n for c, n in zip(self.opened, opens)]
        self.filled = [c + trips * n for c, n in zip(self.filled, fills)]


HEADS = [("k", 0), ("k", 1)] + [("q", h) for h in range(NH)]
ADA_AFTER_HEAD = {2: (0, 6), 3: (0, 7), 4: (0, 8), 5: (0, 9), 6: (0, 10), 7: (0, 11), 8: (1, 0), 9: (1, 1)}
EU = 6
PAIR_USES = ([("PG", 7, None), ("PGc", 6, None), ("XE0", 0, None), ("XE1", 1, None), ("XEc", 2, None)]
             + [("G00", 3, 0), ("U00", 4, 1), ("G01", 5, 2), ("U01", 6, 3), ("D00", 7, 4), ("D01", 0, 5)]
             + [("G10", 1, 6), ("U10", 2, 7), ("G11", 3, 8), ("U11", 4, 9), ("D10", 5, 10), ("D11", 6, 11)]
             + [("Y0", 7, None), ("Y1", 0, None), ("Yc0", 1, None), ("Yc1", 2, None)]
             + [(f"C{d}", (3 + d) % 8, None) for d in range(KD)] + [("Cc0", 3, None), ("Cc1", 4, None)])


def plan_psum(unit_of, base):
    u = PsumUses()
    u.take("vec", 7)
    u.take("bada", 6)
    for n in range(2 * TT):
        u.take(f"x{n}", n % 6)

    def norm(i):
        u.take(f"ssl{i}", 0)
        u.take(f"ssc{i}", 1)

    norm(0)
    u.take("ada0a", 7, unit_of[("ada0", 3)])
    u.take("ada0b", 7, unit_of[("ada0", 11)])
    for n in range(len(HEADS) + 2):
        if n < len(HEADS):
            u.take(f"hl{n}", 2 * (n % 2))
            last = {5: ("qkv", 0), 9: ("qkv", 1)}.get(n)
            u.take(f"hc{n}", 2 * (n % 2) + 1, unit_of[last] if last else None)
        if n == 1:
            for m, b in enumerate((6, 0, 6)):
                u.take(f"v{m}", b, unit_of[("qkv", 2)] if m == 2 else None)
        if 1 <= n <= len(HEADS):
            u.take(f"hsl{n - 1}", 4)
            u.take(f"hsc{n - 1}", 5)
        if n >= 2:
            u.take(f"rot{n - 2}", 6)
        if n == 8:
            u.take("ada1", 7, unit_of[("ada1", 11)])
    u.take("cachek", 5)
    u.take("newk", 4)
    for n in range(NH * TT + 3):
        if n < NH * TT:
            u.take(f"S{n}", 2 * (n % 2))
        if 2 <= n < NH * TT + 2:
            u.take(f"T{n - 2}", 4)
        if n >= 3 and (n - 3) % TT >= TT - 2:
            u.take(f"O{n - 3}", 6)
    for d in range(KD):
        u.take(f"wol{d}", 2 * (d % 2))
        u.take(f"woc{d}", 2 * (d % 2) + 1, unit_of[("wo", d // 4)] if d % 4 == 3 else None)
    for lay in range(2):
        if lay == 1:
            norm(2)
            for d in range(KD):
                u.take(f"pl{d}", 2 * (d % 2))
                u.take(f"pc{d}", 2 * (d % 2) + 1, unit_of["pool"] if d == KD - 1 else None)
        norm(2 * lay + 1)
        u.take(f"rt{lay}", 2)
        for n in range(2 * TT):
            u.take(f"ht{lay}_{n}", 3 + n % 3)
        u.take(f"afl{lay}", 6)
        u.take(f"afc{lay}", 7)
        u.take(f"sl{lay}", 2)
        u.loop(f"L{lay}", PAIR_USES, NP, base[lay])
    for n in range(2 * TT):
        u.take(f"y{n}", n % 8)
    return u.at


def build(nc, a, out):
    front = weight_order()
    n_front = len(front)
    unit_of = {u: n for n, u in enumerate(front)}
    base = {0: n_front, 1: n_front + EU * NE + 1}
    unit_of["pool"] = n_front + EU * NE
    use = plan_psum(unit_of, base)

    with ExitStack() as ctx:
        def sb(name, *shape):
            return ctx.enter_context(nc.sbuf_tensor(name, [P, *shape], F32))

        def sem(name):
            return ctx.enter_context(nc.semaphore(name))

        ring = [sb(f"ring{s}", KD, UC) for s in range(RING)]
        xT = sb("xT", KD, T)
        bufH = sb("bufH", KD * ZW)
        bufQ = sb("bufQ", KD * T)
        bufS = sb("bufS", 8704)
        tab = sb("tab", T_COS)
        vec_rows = sb("vec_rows", P)
        bada_rows = sb("bada_rows", P)
        vec = sb("vec", V_ROWS)
        bada = sb("bada", 2 * MC)
        cond = sb("cond", KD, 2)
        mod = [sb(f"mod{i}", MC, 2) for i in range(2)]
        amp = [sb(f"amp{i}", KD, 2) for i in range(4)]
        gate_pool = sb("gate_pool", KD, 2)
        wr = sb("wr", 2, KD, NE)
        ones = sb("ones", P)
        eps = sb("eps", 1)
        new_k = sb("new_k", NKV * HD)
        stat = sb("stat", 16)
        rmax = sb("rmax", 3, TT)
        aff = sb("aff", TT, NE)
        slot = sb("slot", TT, NE)
        top8 = sb("top8", 8)

        ident, swap = tab[:, T_ID:T_ID + P], tab[:, T_SWAP:T_SWAP + P]

        def view(buf, at, *shape):
            n = int(np.prod(shape))
            v = buf[:, at:at + n]
            names = "abcd"[:len(shape)]
            if len(shape) == 1:
                return v
            return v.rearrange(f"p ({' '.join(names)}) -> p {' '.join(names)}",
                               **{k: s for k, s in zip(names, shape)})

        x_rows = view(bufH, 0, TT, D)
        hA = view(bufH, 0, KD, T)
        oT = hA
        h_rows = x_rows
        y_rows = x_rows
        Z = view(bufH, 0, KD, ZW)
        qT = view(bufQ, 0, NH, T)
        h2T = view(bufQ, 0, KD, T)
        pooled = view(bufQ, 0, KD, T)
        V = view(bufS, 0, TT + 1, NKV * HD)
        kT = view(bufS, 1536, NKV, KEYS)
        kTc = view(bufS, 2816, NKV, CTX)
        cos, sin = view(bufS, 3072, LAT), view(bufS, 3584, LAT)
        raw = view(bufS, 4096, 2, T)
        sqh = view(bufS, 5376, 2, T)
        rrh = view(bufS, 6656, 2, T)
        cache_rows = view(bufS, 7936, NKV * HD)
        probs = view(bufS, 4096, 3, KEYS)
        pT = view(bufS, 6016, TT, LAT)
        pTc = view(bufS, 8576, CTX)
        sq = view(bufS, 4096, 2, T)
        rstd = view(bufS, 5376, T)
        win = [view(bufS, n * 2 * ZW, 2, ZW) for n in range(2)]
        work = view(bufS, 6016, T)
        mask = view(bufS, 6656, T)
        cum = view(bufS, 7296, T)
        zeros = view(bufS, 7936, T)
        pick = view(bufS, 0, LT, 2, CAP_L)
        pick_c = view(bufS, 512, 2, CAP_C)
        pick_g = view(bufS, 544, LT, 2, CAP_L)
        pick_gc = view(bufS, 1056, 2, CAP_C)
        put = view(bufS, 1088, LAT)
        put_c = view(bufS, 1600, CTX)
        ye = view(bufS, 1728, D)
        ye_c = view(bufS, 2752, D)
        xe = view(bufQ, 0, KD, 2, CAP)
        hid = view(bufQ, 1280, KD, CAP)
        sg = view(bufQ, 1920, 2, 4, CAP)
        yT = view(bufQ, 2560, KD, 2, CAP_L)
        yT_c = view(bufQ, 3584, KD, 2, CAP_C)

        psum = ctx.enter_context(nc.psum_tensor("psum", [P, 8 * 512], F32))

        def bank(name, lo, hi, rows=P):
            b = use[name][0]
            return psum[0:rows, 512 * b + lo:512 * b + hi]

        x_loaded = [sem(f"x_loaded{t}") for t in range(TT)]
        ident_loaded = sem("ident_loaded")
        tab_loaded = sem("tab_loaded")
        trig_loaded = sem("trig_loaded")
        vec_loaded = sem("vec_loaded")
        bada_loaded = sem("bada_loaded")
        wr_loaded = sem("wr_loaded")
        cache_loaded = sem("cache_loaded")
        slot_full = [sem(f"slot_full{s}") for s in range(RING)]
        slot_used = [sem(f"slot_used{s}") for s in range(RING)]
        bank_full = [sem(f"bank_full{b}") for b in range(8)]
        bank_empty = [sem(f"bank_empty{b}") for b in range(8)]
        dve_step = sem("dve_step")
        consts_set = sem("consts_set")
        cond_ready = sem("cond_ready")
        amp_ready = sem("amp_ready")
        nsq_ready = sem("nsq_ready")
        nsq_used = sem("nsq_used")
        nscaled = sem("nscaled")
        h_ready = sem("h_ready")
        raw_ready = sem("raw_ready")
        hsq_ready = sem("hsq_ready")
        hnorm_ready = sem("hnorm_ready")
        head_ready = sem("head_ready")
        nmax_ready = sem("nmax_ready")
        probs_ready = sem("probs_ready")
        pooled_ready = sem("pooled_ready")
        aexp_ready = sem("aexp_ready")
        aff_ready = sem("aff_ready")
        slots_ready = sem("slots_ready")
        pick_ready = sem("pick_ready")
        new_v_stored = sem("new_v_stored")
        new_k_stored = sem("new_k_stored")
        stored = sem("stored")

        def full(name, i=0):
            b, _, _, n, per, u = use[name]
            if u is not None:
                return slot_used[u % RING], u // RING + 1 + (2 * i if per_trip(name) else 0)
            return bank_full[b], n + 1 + (per * i if per_trip(name) else 0)

        def per_trip(name):
            return name[0] == "L"

        def empty(name, i=0):
            b, n, per = use[name][:3]
            return bank_empty[b], n + (per * i if per_trip(name) else 0)

        def fills(name):
            b, u = use[name][0], use[name][5]
            return (bank_full[b] if u is None else slot_used[u % RING]), 1

        def empties(name):
            return bank_empty[use[name][0]], 1

        def taken(name, i=0):
            s, v = empty(name, i)
            return s, v + 1

        def wait_empty(eng, name, i=0):
            s, v = empty(name, i)
            if not isinstance(v, int) or v > 0:
                eng.wait_ge(s, v)

        unit_cols = {
            "ada0": lambda n: a["w_ada"][0, :, UC * n:UC * (n + 1)],
            "ada1": lambda n: a["w_ada"][1, :, UC * n:UC * (n + 1)],
            "qkv": lambda n: a["w_qkv"][0, :, UC * n:UC * (n + 1)],
            "wo": lambda n: a["w_o"][0, :, UC * n:UC * (n + 1)],
        }

        block = ctx.enter_context(nc.Block())

        @block.sync
        def _(sp):
            for t in range(TT):
                src = a["x_sample"][0, P * t:P * (t + 1), :] if t < LT else a["x_prompt"][0, :, :]
                sp.dma_start(x_rows[:, t, :], src).then_inc(x_loaded[t], 16)
            for n, (kind, m) in enumerate(front):
                if n >= RING:
                    sp.wait_ge(slot_used[n % RING], n // RING)
                sp.dma_start(ring[n % RING][:, :, :],
                             unit_cols[kind](m).rearrange("(k p) n -> p k n", p=P)
                             ).then_inc(slot_full[n % RING], 16)
            for lay in range(2):
                with sp.Fori(0, NP) as i:
                    for e in range(2):
                        for m in range(EU):
                            n = base[lay] + EU * e + m
                            src = (a["w_e_gate"], a["w_e_up"])[m % 2] if m < 4 else a["w_e_down"]
                            half = m // 2 if m < 4 else m - 4
                            sp.wait_ge(slot_used[n % RING], n // RING + 2 * i)
                            sp.dma_start(ring[n % RING][:, :, :],
                                         src[lay, bass.ds(2 * i + e, 1), :, UC * half:UC * (half + 1)]
                                         .rearrange("e (k p) n -> p (e k) n", p=P)
                                         ).then_inc(slot_full[n % RING], 16)
                if lay == 0:
                    n = unit_of["pool"]
                    sp.wait_ge(slot_used[n % RING], n // RING)
                    sp.dma_start(ring[n % RING][:, :, 0:2 * P],
                                 a["w_pool"][0].rearrange("g (c p) n -> p (g c) n", p=P)
                                 ).then_inc(slot_full[n % RING], 16)
            for t in range(TT):
                sp.wait_ge(*taken(f"y{2 * t}"))
                sp.wait_ge(*taken(f"y{2 * t + 1}"))
                dst = out["y_sample"][0, P * t:P * (t + 1), :] if t < LT else out["y_prompt"][0, :, :]
                sp.dma_start(dst, y_rows[:, t, :]).then_inc(stored, 16)
            sp.wait_ge(stored, 16 * TT)

        @block.gpsimd
        def _(pool):
            pool.wait_ge(*taken("v2"))
            pool.dma_start(out["new_v"][0, 0].rearrange("t h d -> t (h d)"),
                           V[:, TT, :]).then_inc(new_v_stored, 16)
            pool.wait_ge(*taken("newk"))
            pool.dma_start(out["new_k"][0, 0].rearrange("t h d -> t (h d)"),
                           new_k[:, :]).then_inc(new_k_stored, 16)
            pool.wait_ge(new_v_stored, 16)
            pool.wait_ge(new_k_stored, 16)

        @block.tensor
        def _(pe):
            def unit(n):
                pe.wait_ge(slot_full[n % RING], 16 * (n // RING + 1))
                return ring[n % RING]

            pe.wait_ge(ident_loaded, 16)
            pe.wait_ge(vec_loaded, 16 * 7)
            pe.transpose(bank("vec", 0, V_ROWS), vec_rows[0:V_ROWS, :],
                         ident[0:V_ROWS, 0:V_ROWS]).then_inc(*fills("vec"))
            pe.wait_ge(bada_loaded, 16)
            pe.transpose(bank("bada", 0, 2 * MC), bada_rows[0:2 * MC, :],
                         ident[0:2 * MC, 0:2 * MC]).then_inc(*fills("bada"))
            for t in range(TT):
                pe.wait_ge(x_loaded[t], 16)
                for half in range(2):
                    name = f"x{2 * t + half}"
                    wait_empty(pe, name)
                    for k in range(4):
                        kk = 4 * half + k
                        mm = pe.transpose(bank(name, P * k, P * (k + 1)),
                                          x_rows[:, t, P * kk:P * (kk + 1)], ident)
                    mm.then_inc(*fills(name))

            def norm_stats(i):
                wait_empty(pe, f"ssl{i}")
                wait_empty(pe, f"ssc{i}")
                for k in range(KD):
                    pe.wait_ge(nsq_ready, KD * i + k + 1)
                    ml = pe.matmul(bank(f"ssl{i}", 0, LAT), ones[:, :], sq[:, k % 2, 0:LAT],
                                   start=(k == 0), stop=(k == KD - 1))
                    mc = pe.matmul(bank(f"ssc{i}", 0, CTX), ones[:, :], sq[:, k % 2, LAT:T],
                                   start=(k == 0), stop=(k == KD - 1))
                    if k == KD - 1:
                        ml.then_inc(*fills(f"ssl{i}"))
                        mc.then_inc(*fills(f"ssc{i}"))
                    else:
                        mc.then_inc(nsq_used, 1)

            def ada_unit(lay, n):
                u = unit_of[(f"ada{lay}", n)]
                w = unit(u)
                name = "ada1" if lay else ("ada0a" if n < 4 else "ada0b")
                if n == 0 or (lay == 0 and n == 4):
                    wait_empty(pe, name)
                if lay == 0 and n == 0:
                    pe.wait_ge(cond_ready, 1)
                for c in range(UC // P):
                    at = 2 * (4 * n + c)
                    for k in range(KD):
                        mm = pe.matmul(bank(name, at, at + 2), w[:, k, P * c:P * (c + 1)],
                                       cond[:, k, :], start=(k == 0), stop=(k == KD - 1))
                mm.then_inc(slot_used[u % RING], 1)

            pe.wait_ge(consts_set, 2)
            norm_stats(0)
            for n in range(6):
                ada_unit(0, n)

            def head_weights(n):
                kind, h = HEADS[n]
                u = unit_of[("qkv", 2 if kind == "k" else h // 4)]
                c = h if kind == "k" else h % 4
                return u, c

            def project(n):
                u, c = head_weights(n)
                w = unit(u)
                wait_empty(pe, f"hl{n}")
                wait_empty(pe, f"hc{n}")
                for k in range(KD):
                    if n == 0:
                        pe.wait_ge(h_ready, k + 1)
                    ml = pe.matmul(bank(f"hl{n}", 0, LAT), w[:, k, P * c:P * (c + 1)],
                                   hA[:, k, 0:LAT], start=(k == 0), stop=(k == KD - 1))
                    mc = pe.matmul(bank(f"hc{n}", 0, CTX), w[:, k, P * c:P * (c + 1)],
                                   hA[:, k, LAT:T], start=(k == 0), stop=(k == KD - 1))
                ml.then_inc(*fills(f"hl{n}"))
                mc.then_inc(*fills(f"hc{n}"))

            def values():
                u = unit_of[("qkv", 2)]
                w = unit(u)
                for t in range(TT):
                    name = f"v{t // 2}"
                    if t % 2 == 0:
                        wait_empty(pe, name)
                    o = NKV * HD * (t % 2)
                    for k in range(KD):
                        mm = pe.matmul(bank(name, o, o + NKV * HD), hA[:, k, P * t:P * (t + 1)],
                                       w[:, k, NKV * HD:2 * NKV * HD], start=(k == 0), stop=(k == KD - 1))
                    if t % 2 == 1 or t == TT - 1:
                        mm.then_inc(*fills(name))

            def head_stats(n):
                wait_empty(pe, f"hsl{n}")
                wait_empty(pe, f"hsc{n}")
                pe.wait_ge(hsq_ready, n + 1)
                pe.matmul(bank(f"hsl{n}", 0, LAT), ones[:, :], sqh[:, n % 2, 0:LAT],
                          start=True, stop=True).then_inc(*fills(f"hsl{n}"))
                pe.matmul(bank(f"hsc{n}", 0, CTX), ones[:, :], sqh[:, n % 2, LAT:T],
                          start=True, stop=True).then_inc(*fills(f"hsc{n}"))

            def rotate(n):
                wait_empty(pe, f"rot{n}")
                pe.wait_ge(hnorm_ready, n + 1)
                if n == 0:
                    pe.wait_ge(tab_loaded, 16)
                pe.matmul(bank(f"rot{n}", 0, LAT), swap, raw[:, n % 2, 0:LAT],
                          start=True, stop=True).then_inc(*fills(f"rot{n}"))

            for n in range(len(HEADS) + 2):
                if n < len(HEADS):
                    project(n)
                if n == 1:
                    values()
                if 1 <= n <= len(HEADS):
                    head_stats(n - 1)
                if n >= 2:
                    rotate(n - 2)
                if n in ADA_AFTER_HEAD:
                    ada_unit(*ADA_AFTER_HEAD[n])

            pe.wait_ge(cache_loaded, 32)
            wait_empty(pe, "cachek")
            for g in range(NKV):
                mm = pe.transpose(bank("cachek", P * g, P * (g + 1)),
                                  cache_rows[:, HD * g:HD * (g + 1)], ident)
            mm.then_inc(*fills("cachek"))
            wait_empty(pe, "newk")
            pe.wait_ge(head_ready, NKV)
            for g in range(NKV):
                mm = pe.transpose(bank("newk", P * g, P * (g + 1)), kTc[:, g, :], ident)
            mm.then_inc(*fills("newk"))

            def scores(n):
                h, t = n // TT, n % TT
                g = h // G
                wait_empty(pe, f"S{n}")
                if t == 0:
                    pe.wait_ge(head_ready, NKV + h + 1)
                q = qT[:, h, P * t:P * (t + 1)]
                if t < LT:
                    if n == 0:
                        pe.wait_ge(*taken("cachek"))
                        pe.wait_ge(*taken("v2"))
                    pe.matmul(bank(f"S{n}", 0, LAT), q, kT[:, g, 0:LAT], start=True, stop=True)
                    mm = pe.matmul(bank(f"S{n}", LAT, KEYS), q, kT[:, g, LAT:KEYS], start=True, stop=True)
                else:
                    mm = pe.matmul(bank(f"S{n}", 0, CTX), q, kTc[:, g, :], start=True, stop=True)
                mm.then_inc(*fills(f"S{n}"))

            def probs_turn(n):
                wait_empty(pe, f"T{n}")
                pe.wait_ge(probs_ready, n + 1)
                for c in range(TT if n % TT < LT else 1):
                    mm = pe.transpose(bank(f"T{n}", P * c, P * (c + 1)),
                                      probs[:, n % 3, P * c:P * (c + 1)], ident)
                mm.then_inc(*fills(f"T{n}"))

            def weigh(n):
                h, t = n // TT, n % TT
                g = h // G
                wait_empty(pe, f"O{n}")
                pe.wait_ge(*taken(f"T{n}"))
                if t == LT - 1:
                    for c in range(TT):
                        mm = pe.matmul(bank(f"O{n}", 0, LAT), V[:, c, HD * g:HD * (g + 1)],
                                       pT[:, c, :], start=(c == 0), stop=(c == TT - 1))
                else:
                    mm = pe.matmul(bank(f"O{n}", 0, CTX), V[:, TT, HD * g:HD * (g + 1)], pTc[:, :],
                                   start=True, stop=True)
                mm.then_inc(*fills(f"O{n}"))

            for n in range(NH * TT + 3):
                if n < NH * TT:
                    scores(n)
                if 2 <= n < NH * TT + 2:
                    probs_turn(n - 2)
                if n >= 3 and (n - 3) % TT >= TT - 2:
                    weigh(n - 3)
                if n % 4 == 1 and n // 4 < 10:
                    ada_unit(1, 2 + n // 4)

            pe.wait_ge(*taken(f"O{NH * TT - 1}"))
            for d in range(KD):
                u = unit_of[("wo", d // 4)]
                w = unit(u)
                c = d % 4
                wait_empty(pe, f"wol{d}")
                wait_empty(pe, f"woc{d}")
                for h in range(NH):
                    ml = pe.matmul(bank(f"wol{d}", 0, LAT), w[:, h, P * c:P * (c + 1)],
                                   oT[:, h, 0:LAT], start=(h == 0), stop=(h == NH - 1))
                    mc = pe.matmul(bank(f"woc{d}", 0, CTX), w[:, h, P * c:P * (c + 1)],
                                   oT[:, h, LAT:T], start=(h == 0), stop=(h == NH - 1))
                ml.then_inc(*fills(f"wol{d}"))
                mc.then_inc(*fills(f"woc{d}"))

            def pool_products():
                norm_stats(2)
                w = unit(unit_of["pool"])
                for k in range(KD):
                    g = k // 2
                    wait_empty(pe, f"pl{k}")
                    wait_empty(pe, f"pc{k}")
                    pe.wait_ge(pooled_ready, g + 1)
                    for c in range(2):
                        wc = w[:, 2 * g + c, P * (k % 2):P * (k % 2 + 1)]
                        ml = pe.matmul(bank(f"pl{k}", 0, LAT), wc, pooled[:, 2 * g + c, 0:LAT],
                                       start=(c == 0), stop=(c == 1))
                        mc = pe.matmul(bank(f"pc{k}", 0, CTX), wc, pooled[:, 2 * g + c, LAT:T],
                                       start=(c == 0), stop=(c == 1))
                    ml.then_inc(*fills(f"pl{k}"))
                    mc.then_inc(*fills(f"pc{k}"))

            def route(lay):
                norm_stats(2 * lay + 1)
                if lay == 0:
                    pe.wait_ge(wr_loaded, 32)
                wait_empty(pe, f"rt{lay}")
                pe.wait_ge(h_ready, KD * (2 * lay + 2))
                for t in range(TT):
                    for k in range(KD):
                        mm = pe.matmul(bank(f"rt{lay}", NE * t, NE * (t + 1)), h2T[:, k, P * t:P * (t + 1)],
                                       wr[:, lay, k, :], start=(k == 0), stop=(k == KD - 1))
                mm.then_inc(*fills(f"rt{lay}"))
                def turn_h(n):
                    t, half = n // 2, n % 2
                    name = f"ht{lay}_{n}"
                    wait_empty(pe, name)
                    for k in range(4):
                        mm = pe.transpose(bank(name, P * k, P * (k + 1)),
                                          h2T[:, 4 * half + k, P * t:P * (t + 1)], ident)
                    mm.then_inc(*fills(name))

                for n in range(3):
                    turn_h(n)
                wait_empty(pe, f"afl{lay}")
                wait_empty(pe, f"afc{lay}")
                pe.wait_ge(aff_ready, lay + 1)
                for t in range(LT):
                    mm = pe.transpose(bank(f"afl{lay}", P * t, P * (t + 1), NE), aff[:, t, :], ident)
                mm.then_inc(*fills(f"afl{lay}"))
                pe.transpose(bank(f"afc{lay}", 0, P, NE), aff[:, LT, :], ident).then_inc(*fills(f"afc{lay}"))
                for n in range(3, 2 * TT):
                    turn_h(n)
                wait_empty(pe, f"sl{lay}")
                pe.wait_ge(slots_ready, lay + 1)
                for t in range(TT):
                    mm = pe.transpose(bank(f"sl{lay}", NE * t, NE * (t + 1)),
                                      cum[0:NE, P * t:P * (t + 1)], ident[0:NE, 0:NE])
                mm.then_inc(*fills(f"sl{lay}"))
                pe.wait_ge(*taken(f"ht{lay}_{2 * TT - 1}"))

            def expert_pair(lay, i):
                gp = NP * lay + i
                L = f"L{lay}"
                wait_empty(pe, L + "PG", i)
                wait_empty(pe, L + "PGc", i)
                pe.wait_ge(pick_ready, 4 * gp + 4)
                for c in range(LT):
                    mm = pe.transpose(bank(L + "PG", P * c, P * (c + 1)),
                                      pick_g[:, c, :, :].rearrange("p e s -> p (e s)"), ident)
                mm.then_inc(*fills(L + "PG"))
                pe.transpose(bank(L + "PGc", 0, CTX, SEL_C),
                             pick_gc[:, :, :].rearrange("p e s -> p (e s)"), ident).then_inc(*fills(L + "PGc"))
                for half in range(2):
                    name = L + f"XE{half}"
                    wait_empty(pe, name, i)
                    for k in range(4):
                        kk = 4 * half + k
                        for c in range(LT):
                            mm = pe.matmul(bank(name, SEL_L * k, SEL_L * (k + 1)),
                                           h_rows[:, c, P * kk:P * (kk + 1)],
                                           pick[:, c, :, :].rearrange("p e s -> p (e s)"),
                                           start=(c == 0), stop=(c == LT - 1))
                    mm.then_inc(*fills(name))
                wait_empty(pe, L + "XEc", i)
                for k in range(KD):
                    mm = pe.matmul(bank(L + "XEc", SEL_C * k, SEL_C * (k + 1)),
                                   h_rows[:, LT, P * k:P * (k + 1)],
                                   pick_c[:, :, :].rearrange("p e s -> p (e s)"), start=True, stop=True)
                mm.then_inc(*fills(L + "XEc"))
                for e in range(2):
                    n0 = base[lay] + EU * e
                    for m in range(4):
                        n = n0 + m
                        name = L + ("G", "U")[m % 2] + f"{e}{m // 2}"
                        wait_empty(pe, name, i)
                        if m == 0 and e == 0:
                            pe.wait_ge(*taken(L + "XEc", i))
                        pe.wait_ge(slot_full[n % RING], 16 * (n // RING + 1) + 32 * i)
                        w = ring[n % RING]
                        for f in range(4):
                            for k in range(KD):
                                mm = pe.matmul(bank(name, CAP * f, CAP * (f + 1)), w[:, k, P * f:P * (f + 1)],
                                               xe[:, k, e, :], start=(k == 0), stop=(k == KD - 1))
                        mm.then_inc(*fills(name))
                    for m in range(2):
                        n = n0 + 4 + m
                        name = L + f"D{e}{m}"
                        wait_empty(pe, name, i)
                        pe.wait_ge(*taken(L + f"U{e}1", i))
                        pe.wait_ge(slot_full[n % RING], 16 * (n // RING + 1) + 32 * i)
                        w = ring[n % RING]
                        for f in range(4):
                            for k in range(KD):
                                mm = pe.matmul(bank(name, CAP * f, CAP * (f + 1)), w[:, k, P * f:P * (f + 1)],
                                               hid[:, k, :], start=(k == 0), stop=(k == KD - 1))
                        mm.then_inc(*fills(name))
                pe.wait_ge(*taken(L + "D11", i))
                for half in range(2):
                    name = L + f"Y{half}"
                    wait_empty(pe, name, i)
                    for k in range(4):
                        mm = pe.transpose(bank(name, P * k, P * (k + 1)),
                                          yT[:, 4 * half + k, :, :].rearrange("p e s -> p (e s)"), ident)
                    mm.then_inc(*fills(name))
                for half in range(2):
                    name = L + f"Yc{half}"
                    wait_empty(pe, name, i)
                    for k in range(4):
                        mm = pe.transpose(bank(name, P * k, P * (k + 1), SEL_C),
                                          yT_c[:, 4 * half + k, :, :].rearrange("p e s -> p (e s)"), ident)
                    mm.then_inc(*fills(name))
                pe.wait_ge(*taken(L + "PGc", i))
                pe.wait_ge(*taken(L + "Yc1", i))
                for d in range(KD):
                    name = L + f"C{d}"
                    wait_empty(pe, name, i)
                    pe.matmul(bank(name, 0, LAT), ye[:, P * d:P * (d + 1)], put[:, :],
                              start=True, stop=True).then_inc(*fills(name))
                for half in range(2):
                    name = L + f"Cc{half}"
                    wait_empty(pe, name, i)
                    for k in range(4):
                        d = 4 * half + k
                        mm = pe.matmul(bank(name, P * k, P * (k + 1)), ye_c[0:SEL_C, P * d:P * (d + 1)],
                                       put_c[0:SEL_C, :], start=True, stop=True)
                    mm.then_inc(*fills(name))

            for lay in range(2):
                if lay == 1:
                    pool_products()
                route(lay)
                with pe.Fori(0, NP) as i:
                    expert_pair(lay, i)

            pe.wait_ge(*taken("L1Cc1", NP - 1))
            for n in range(2 * TT):
                t, half = n // 2, n % 2
                name = f"y{n}"
                wait_empty(pe, name)
                for k in range(4):
                    mm = pe.transpose(bank(name, P * k, P * (k + 1)),
                                      xT[:, 4 * half + k, P * t:P * (t + 1)], ident)
                mm.then_inc(*fills(name))

        @block.scalar
        def _(act):
            act.dma_start(ident, a["tables"][:, T_ID:T_ID + P]).then_inc(ident_loaded, 16)
            rows = [(V_C, V_CTX, a["c"].rearrange("a (k p) -> (a k) p", p=P)),
                    (V_CTX, V_N1, a["c_ctx"].rearrange("(k p) -> k p", p=P)),
                    (V_N1, V_N2, a["norm1"].rearrange("a (k p) -> (a k) p", p=P)),
                    (V_N2, V_PS, a["norm2"].rearrange("a (k p) -> (a k) p", p=P)),
                    (V_PS, V_Q, a["pool_scale"].rearrange("a (k p) -> (a k) p", p=P)),
                    (V_Q, V_K, a["q_norm"]), (V_K, V_ROWS, a["k_norm"])]
            for lo, hi, src in rows:
                act.dma_start(vec_rows[lo:hi, :], src).then_inc(vec_loaded, 16)
            act.dma_start(bada_rows[0:2 * MC, :],
                          a["b_ada"].rearrange("l (m p) -> (l m) p", p=P)).then_inc(bada_loaded, 16)
            act.dma_start(tab[:, T_SWAP:T_COS], a["tables"][:, T_SWAP:T_COS]).then_inc(tab_loaded, 16)
            act.dma_start(cos, a["tables"][:, T_COS:T_SIN]).then_inc(trig_loaded, 16)
            act.dma_start(sin, a["tables"][:, T_SIN:T_COLS]).then_inc(trig_loaded, 16)
            act.dma_start(cache_rows, a["cache_k"][0, 0].rearrange("t h d -> t (h d)")).then_inc(cache_loaded, 16)
            act.dma_start(V[:, LT, :], a["cache_v"][0, 0].rearrange("t h d -> t (h d)")).then_inc(cache_loaded, 16)
            for lay in range(2):
                act.dma_start(wr[:, lay, :, :],
                              a["w_router"][lay].rearrange("(k p) e -> p k e", p=P)).then_inc(wr_loaded, 16)

            act.wait_ge(*taken("vec"))
            nc.scalar.activation(cond[:, :, :].rearrange("p k t -> p t k"),
                                 vec[:, V_C:V_N1].rearrange("p (t k) -> p t k", t=2),
                                 ACT.Silu).then_inc(cond_ready, 1)
            for n in range(1, 2 * TT, 2):
                act.wait_ge(*full(f"x{n}"))
                nc.scalar.copy(xT[:, 4:8, P * (n // 2):P * (n // 2 + 1)],
                               bank(f"x{n}", 0, 512).rearrange("p (k t) -> p k t", k=4)
                               ).then_inc(*empties(f"x{n}"))

            def norm(i, dst):
                lay, second = i // 2, i % 2
                for k in range(KD):
                    if k >= 2:
                        act.wait_ge(nsq_used, (KD - 1) * i + k - 1)
                    if i == 0 and k == 0:
                        act.wait_ge(*taken("x8"))
                        act.wait_ge(*taken("x9"))
                    if i == 1:
                        act.wait_ge(*taken(f"woc{k}"))
                    if i == 2 and k == 0:
                        act.wait_ge(*taken("L0Cc1", NP - 1))
                    if i == 3:
                        act.wait_ge(*taken(f"pc{k}"))
                    nc.scalar.activation(sq[:, k % 2, :], xT[:, k, :], ACT.Square).then_inc(nsq_ready, 1)
                act.wait_ge(*full(f"ssl{i}"))
                if i == 0:
                    act.wait_ge(consts_set, 2)
                nc.scalar.activation(rstd[:, 0:LAT], bank(f"ssl{i}", 0, LAT), ACT.Sqrt,
                                     bias=eps[:, :], scale=1.0 / D).then_inc(*empties(f"ssl{i}"))
                act.wait_ge(*full(f"ssc{i}"))
                nc.scalar.activation(rstd[:, LAT:T], bank(f"ssc{i}", 0, CTX), ACT.Sqrt,
                                     bias=eps[:, :], scale=1.0 / D).then_inc(*empties(f"ssc{i}"))
                sh = SH2 if second else SH1
                for k in range(KD):
                    act.wait_ge(nscaled, KD * i + k + 1)
                    lat, ctx_ = dst(k)
                    nc.scalar.activation(lat, lat, ACT.Identity, bias=mod[lay][:, sh + k, 0:1])
                    nc.scalar.activation(ctx_, ctx_, ACT.Identity,
                                         bias=mod[lay][:, sh + k, 1:2]).then_inc(h_ready, 1)

            norm(0, lambda k: (hA[:, k, 0:LAT], hA[:, k, LAT:T]))

            for n in range(len(HEADS) + 2):
                if n == 1:
                    for m in range(3):
                        name = f"v{m}"
                        act.wait_ge(*full(name))
                        if m < 2:
                            nc.scalar.copy(V[:, 2 * m:2 * m + 2, :],
                                           bank(name, 0, 512).rearrange("p (t c) -> p t c", t=2)
                                           ).then_inc(*empties(name))
                        else:
                            nc.scalar.copy(V[:, TT, :], bank(name, 0, NKV * HD)).then_inc(*empties(name))
                if 1 <= n <= len(HEADS):
                    m = n - 1
                    act.wait_ge(*full(f"hsl{m}"))
                    nc.scalar.activation(rrh[:, m % 2, 0:LAT], bank(f"hsl{m}", 0, LAT), ACT.Sqrt,
                                         bias=eps[:, :], scale=1.0 / HD).then_inc(*empties(f"hsl{m}"))
                    act.wait_ge(*full(f"hsc{m}"))
                    nc.scalar.activation(rrh[:, m % 2, LAT:T], bank(f"hsc{m}", 0, CTX), ACT.Sqrt,
                                         bias=eps[:, :], scale=1.0 / HD).then_inc(*empties(f"hsc{m}"))
                if n < len(HEADS):
                    act.wait_ge(raw_ready, n + 1)
                    nc.scalar.activation(sqh[:, n % 2, :], raw[:, n % 2, :], ACT.Square).then_inc(hsq_ready, 1)

            def expo(n):
                w = KEYS if n % TT < LT else CTX
                act.wait_ge(nmax_ready, n + 1)
                nc.scalar.activation(probs[:, n % 3, 0:w], bank(f"S{n}", 0, w), ACT.Exp,
                                     bias=stat[:, 4 + n % 4:5 + n % 4], scale=HD ** -0.5,
                                     accum_out=stat[:, 8 + n % 4:9 + n % 4]).then_inc(*empties(f"S{n}"))

            def keep_turned(n):
                act.wait_ge(*full(f"T{n}"))
                t = n % TT
                if t < LT:
                    nc.scalar.copy(pT[:, :, P * t:P * (t + 1)],
                                   bank(f"T{n}", 0, KEYS).rearrange("p (c q) -> p c q", q=P)
                                   ).then_inc(*empties(f"T{n}"))
                else:
                    nc.scalar.copy(pTc[:, :], bank(f"T{n}", 0, CTX)).then_inc(*empties(f"T{n}"))

            for n in range(NH * TT + 2):
                if n < NH * TT:
                    expo(n)
                if n >= 2:
                    keep_turned(n - 2)

            def expert_pair(lay, i):
                gp = NP * lay + i
                L = f"L{lay}"
                act.wait_ge(*full(L + "PG", i))
                nc.scalar.copy(put[:, :], bank(L + "PG", 0, LAT)).then_inc(*empties(L + "PG"))
                act.wait_ge(*full(L + "PGc", i))
                nc.scalar.copy(put_c[0:SEL_C, :], bank(L + "PGc", 0, CTX, SEL_C)).then_inc(*empties(L + "PGc"))
                for e in range(2):
                    for m in range(2):
                        name = L + f"G{e}{m}"
                        act.wait_ge(*full(name, i))
                        nc.scalar.activation(sg[:, m, :, :].rearrange("p f s -> p (f s)"),
                                             bank(name, 0, 4 * CAP), ACT.Silu).then_inc(*empties(name))
                    for m in range(2):
                        name = L + f"D{e}{m}"
                        act.wait_ge(*full(name, i))
                        y = bank(name, 0, 4 * CAP).rearrange("p (f s) -> p f s", f=4)
                        nc.scalar.copy(yT[:, 4 * m:4 * m + 4, e, :], y[:, :, 0:CAP_L])
                        nc.scalar.copy(yT_c[:, 4 * m:4 * m + 4, e, :], y[:, :, CAP_L:CAP]).then_inc(*empties(name))

            for lay in range(2):
                if lay == 1:
                    norm(2, lambda k: (Z[:, k, Z_L:Z_L + LAT], Z[:, k, Z_C:Z_C + CTX]))
                norm(2 * lay + 1, lambda k: (h2T[:, k, 0:LAT], h2T[:, k, LAT:T]))
                act.wait_ge(*taken(f"rt{lay}"))
                nc.scalar.activation(slot[:, :, :], aff[:, :, :], ACT.Exp).then_inc(aexp_ready, 1)
                for n in range(2 * TT):
                    name = f"ht{lay}_{n}"
                    act.wait_ge(*full(name))
                    nc.scalar.copy(h_rows[:, n // 2, 512 * (n % 2):512 * (n % 2 + 1)],
                                   bank(name, 0, 512)).then_inc(*empties(name))
                if lay == 0:
                    act.wait_ge(new_v_stored, 16)
                with act.Fori(0, NP) as i:
                    expert_pair(lay, i)
            for n in range(1, 2 * TT, 2):
                act.wait_ge(*full(f"y{n}"))
                nc.scalar.copy(y_rows[:, n // 2, 512:1024], bank(f"y{n}", 0, 512)).then_inc(*empties(f"y{n}"))

        @block.vector
        def _(dve):
            dve_steps = [0]

            def own(ins):
                dve_steps[0] += 1
                ins.then_inc(dve_step, 1)
                dve.wait_ge(dve_step, dve_steps[0])

            nc.vector.memset(ones[:, :], 1.0).then_inc(consts_set, 1)
            nc.vector.memset(eps[:, :], EPS).then_inc(consts_set, 1)
            dve.wait_ge(*full("vec"))
            nc.vector.tensor_copy(vec[:, :], bank("vec", 0, V_ROWS)).then_inc(*empties("vec"))
            dve.wait_ge(*full("bada"))
            nc.vector.tensor_copy(bada[:, :], bank("bada", 0, 2 * MC)).then_inc(*empties("bada"))
            for n in range(0, 2 * TT, 2):
                dve.wait_ge(*full(f"x{n}"))
                nc.vector.tensor_copy(xT[:, 0:4, P * (n // 2):P * (n // 2 + 1)],
                                      bank(f"x{n}", 0, 512).rearrange("p (k t) -> p k t", k=4)
                                      ).then_inc(*empties(f"x{n}"))

            def take_mod(name, lay, c0, c1):
                dve.wait_ge(*full(name))
                if name == "ada0a":
                    dve.wait_ge(*taken("bada"))
                nc.vector.tensor_tensor(
                    mod[lay][:, c0:c1, :], bank(name, 2 * c0, 2 * c1).rearrange("p (c t) -> p c t", t=2),
                    bada[:, MC * lay + c0:MC * lay + c1].unsqueeze(2).to_broadcast([P, c1 - c0, 2]),
                    ALU.add).then_inc(*empties(name))
                dve.wait_ge(*taken(name))

            def set_amp(i):
                lay, second = i // 2, i % 2
                sc = SC2 if second else SC1
                g = (V_N2 if second else V_N1) + KD * lay
                own(nc.vector.scalar_tensor_tensor(
                    out=amp[i][:, :, :], in0=mod[lay][:, sc:sc + KD, :], scalar=1.0,
                    in1=vec[:, g:g + KD].unsqueeze(2).to_broadcast([P, KD, 2]), op0=ALU.add, op1=ALU.mult))

            def norm(i, dst):
                dve.wait_ge(*taken(f"ssl{i}"))
                dve.wait_ge(*taken(f"ssc{i}"))
                own(nc.vector.reciprocal(rstd[:, :], rstd[:, :]))
                for k in range(KD):
                    lat, ctx_ = dst(k)
                    nc.vector.scalar_tensor_tensor(out=lat, in0=xT[:, k, 0:LAT], scalar=amp[i][:, k, 0:1],
                                                   in1=rstd[:, 0:LAT], op0=ALU.mult, op1=ALU.mult)
                    nc.vector.scalar_tensor_tensor(out=ctx_, in0=xT[:, k, LAT:T], scalar=amp[i][:, k, 1:2],
                                                   in1=rstd[:, LAT:T], op0=ALU.mult, op1=ALU.mult
                                                   ).then_inc(nscaled, 1)

            take_mod("ada0a", 0, 0, G1)
            set_amp(0)
            dve.wait_ge(*taken("x9"))
            norm(0, lambda k: (hA[:, k, 0:LAT], hA[:, k, LAT:T]))

            def head_dst(n):
                kind, h = HEADS[n]
                return (kT[:, h, 0:LAT], kTc[:, h, :]) if kind == "k" else (qT[:, h, 0:LAT], qT[:, h, LAT:T])

            def take_head(n):
                dve.wait_ge(*full(f"hl{n}"))
                nc.vector.tensor_copy(raw[:, n % 2, 0:LAT], bank(f"hl{n}", 0, LAT)).then_inc(*empties(f"hl{n}"))
                dve.wait_ge(*full(f"hc{n}"))
                nc.vector.tensor_copy(raw[:, n % 2, LAT:T], bank(f"hc{n}", 0, CTX)).then_inc(*empties(f"hc{n}"))
                nc.vector.engine_nop().then_inc(raw_ready, 1)

            def norm_head(n):
                g = V_K if HEADS[n][0] == "k" else V_Q
                dve.wait_ge(*taken(f"hsl{n}"))
                dve.wait_ge(*taken(f"hsc{n}"))
                own(nc.vector.reciprocal(rrh[:, n % 2, :], rrh[:, n % 2, :]))
                nc.vector.scalar_tensor_tensor(out=raw[:, n % 2, 0:LAT], in0=raw[:, n % 2, 0:LAT],
                                               scalar=vec[:, g:g + 1], in1=rrh[:, n % 2, 0:LAT],
                                               op0=ALU.mult, op1=ALU.mult).then_inc(hnorm_ready, 1)
                nc.vector.scalar_tensor_tensor(out=head_dst(n)[1], in0=raw[:, n % 2, LAT:T],
                                               scalar=vec[:, g:g + 1], in1=rrh[:, n % 2, LAT:T],
                                               op0=ALU.mult, op1=ALU.mult)

            def finish_head(n):
                if n == 0:
                    dve.wait_ge(trig_loaded, 32)
                dst = head_dst(n)[0]
                dve.wait_ge(*full(f"rot{n}"))
                dve.wait_ge(hnorm_ready, n + 1)
                nc.vector.tensor_tensor(dst, raw[:, n % 2, 0:LAT], cos, ALU.mult)
                nc.vector.tensor_tensor(sqh[:, n % 2, 0:LAT], bank(f"rot{n}", 0, LAT), sin,
                                        ALU.mult).then_inc(*empties(f"rot{n}"))
                dve.wait_ge(*taken(f"rot{n}"))
                nc.vector.tensor_tensor(dst, dst, sqh[:, n % 2, 0:LAT], ALU.add).then_inc(head_ready, 1)

            for n in range(len(HEADS) + 2):
                if n == 8:
                    take_mod("ada0b", 0, G1, MC)
                    set_amp(1)
                if n >= 2:
                    finish_head(n - 2)
                if n < len(HEADS):
                    take_head(n)
                if 1 <= n <= len(HEADS):
                    norm_head(n - 1)

            dve.wait_ge(*full("cachek"))
            nc.vector.tensor_copy(kT[:, :, LAT:KEYS], bank("cachek", 0, NKV * HD)
                                  .rearrange("p (g t) -> p g t", g=NKV)).then_inc(*empties("cachek"))
            dve.wait_ge(*full("newk"))
            nc.vector.tensor_copy(new_k[:, :], bank("newk", 0, NKV * HD)).then_inc(*empties("newk"))

            def tile_max(n):
                w = KEYS if n % TT < LT else CTX
                dve.wait_ge(*full(f"S{n}"))
                own(nc.vector.tensor_reduce(stat[:, n % 4:n % 4 + 1], bank(f"S{n}", 0, w), AX.X, ALU.max))
                nc.vector.tensor_scalar(stat[:, 4 + n % 4:5 + n % 4], stat[:, n % 4:n % 4 + 1], -HD ** -0.5,
                                        None, ALU.mult).then_inc(nmax_ready, 1)

            def tile_probs(n):
                w = KEYS if n % TT < LT else CTX
                dve.wait_ge(*taken(f"S{n}"))
                own(nc.vector.reciprocal(stat[:, 12 + n % 4:13 + n % 4], stat[:, 8 + n % 4:9 + n % 4]))
                nc.vector.tensor_scalar(probs[:, n % 3, 0:w], probs[:, n % 3, 0:w],
                                        stat[:, 12 + n % 4:13 + n % 4], None, ALU.mult
                                        ).then_inc(probs_ready, 1)

            for n in range(NH * TT + 4):
                if n < NH * TT:
                    tile_max(n)
                if 1 <= n <= NH * TT:
                    tile_probs(n - 1)
                m = n - 4
                if m >= 0 and m % TT >= LT - 1:
                    lo, hi = (0, LAT) if m % TT == LT - 1 else (LAT, T)
                    dve.wait_ge(*full(f"O{m}"))
                    nc.vector.tensor_copy(oT[:, m // TT, lo:hi],
                                          bank(f"O{m}", 0, hi - lo)).then_inc(*empties(f"O{m}"))
            take_mod("ada1", 1, 0, MC)
            set_amp(2)
            set_amp(3)
            own(nc.vector.tensor_tensor(gate_pool[:, :, :], mod[1][:, G1:G1 + KD, :],
                                        vec[:, V_PS:V_PS + KD].unsqueeze(2).to_broadcast([P, KD, 2]), ALU.mult))

            def add_mixed(k, lat, ctx_, gate):
                dve.wait_ge(*full(lat))
                nc.vector.scalar_tensor_tensor(out=xT[:, k, 0:LAT], in0=bank(lat, 0, LAT), scalar=gate[:, k, 0:1],
                                               in1=xT[:, k, 0:LAT], op0=ALU.mult, op1=ALU.add
                                               ).then_inc(*empties(lat))
                dve.wait_ge(*full(ctx_))
                nc.vector.scalar_tensor_tensor(out=xT[:, k, LAT:T], in0=bank(ctx_, 0, CTX),
                                               scalar=gate[:, k, 1:2], in1=xT[:, k, LAT:T],
                                               op0=ALU.mult, op1=ALU.add).then_inc(*empties(ctx_))

            for k in range(KD):
                add_mixed(k, f"wol{k}", f"woc{k}", mod[0][:, G1:G1 + KD, :])

            def pool_windows():
                for lo, hi in ((0, Z_L), (Z_L + LAT, Z_C), (Z_C + CTX, ZW)):
                    nc.vector.memset(Z[:, :, lo:hi], 0.0)
                norm(2, lambda k: (Z[:, k, Z_L:Z_L + LAT], Z[:, k, Z_C:Z_C + CTX]))
                for g, w in enumerate(WINDOWS):
                    dve.wait_ge(h_ready, 2 * KD + 2 * g + 2)
                    if g > 0:
                        dve.wait_ge(pooled_ready, g)
                    z = Z[:, 2 * g:2 * g + 2, :]
                    src, lo, hi, reach = z, 1, ZW, 0
                    for s in range(g + 1):
                        dst = win[s % 2]
                        left, right = (1, 0) if s == 0 else (reach, reach)
                        own(nc.vector.tensor_tensor(dst[:, :, lo:hi], src[:, :, lo - left:hi - left],
                                                    src[:, :, lo + right:hi + right], ALU.add))
                        src, reach = dst, max(1, 2 * reach)
                        lo, hi = lo + reach, hi - reach
                    inv = T_INV + CTX * g
                    d = pooled[:, 2 * g:2 * g + 2, :]
                    half = CTX // 2
                    for at, n, tcol in ((Z_L, half, 0), (Z_L + LAT - half, half, half), (Z_C, CTX, 0)):
                        ins = nc.vector.tensor_tensor(
                            src[:, :, at:at + n], src[:, :, at:at + n],
                            tab[:, inv + tcol:inv + tcol + n].unsqueeze(1).to_broadcast([P, 2, n]), ALU.mult)
                    nc.vector.scalar_tensor_tensor(
                        out=d[:, :, half:LAT - half], in0=src[:, :, Z_L + half:Z_L + LAT - half], scalar=1.0 / w,
                        in1=z[:, :, Z_L + half:Z_L + LAT - half], op0=ALU.mult, op1=ALU.subtract)
                    own(ins)
                    for at, n, o in ((Z_L, half, 0), (Z_L + LAT - half, half, LAT - half), (Z_C, CTX, LAT)):
                        ins = nc.vector.tensor_tensor(d[:, :, o:o + n], src[:, :, at:at + n],
                                                      z[:, :, at:at + n], ALU.subtract)
                    ins.then_inc(pooled_ready, 1)

            def route(lay):
                logits = bank(f"rt{lay}", 0, TT * NE).rearrange("p (t e) -> p t e", e=NE)
                dve.wait_ge(*full(f"rt{lay}"))
                own(nc.vector.tensor_reduce(rmax[:, 0, :], logits, AX.X, ALU.max))
                nc.vector.tensor_tensor(aff[:, :, :], logits, rmax[:, 0, :].unsqueeze(2).to_broadcast([P, TT, NE]),
                                        ALU.subtract).then_inc(*empties(f"rt{lay}"))
                dve.wait_ge(aexp_ready, lay + 1)
                own(nc.vector.tensor_reduce(rmax[:, 1, :], slot[:, :, :], AX.X, ALU.add))
                own(nc.vector.reciprocal(rmax[:, 2, :], rmax[:, 1, :]))
                nc.vector.tensor_tensor(aff[:, :, :], slot[:, :, :],
                                        rmax[:, 2, :].unsqueeze(2).to_broadcast([P, TT, NE]),
                                        ALU.mult).then_inc(aff_ready, 1)
                dve.wait_ge(*full(f"afl{lay}"))
                nc.vector.tensor_copy(work[0:NE, 0:LAT], bank(f"afl{lay}", 0, LAT, NE)).then_inc(*empties(f"afl{lay}"))
                dve.wait_ge(*full(f"afc{lay}"))
                nc.vector.tensor_copy(work[0:NE, LAT:T], bank(f"afc{lay}", 0, CTX, NE)).then_inc(*empties(f"afc{lay}"))
                dve.wait_ge(*taken(f"afl{lay}"))
                dve.wait_ge(*taken(f"afc{lay}"))
                for lo, hi, cap in ((0, LAT, CAP_L), (LAT, T, CAP_C)):
                    for _ in range(cap // 8):
                        own(nc.vector.max(top8[0:NE, :], work[0:NE, lo:hi]))
                        own(nc.vector.match_replace(work[0:NE, lo:hi], top8[0:NE, :], work[0:NE, lo:hi], -1.0))
                own(nc.vector.tensor_scalar(mask[0:NE, :], work[0:NE, :], 0.0, None, ALU.is_lt))
                for lo, hi in ((0, LAT), (LAT, T)):
                    own(nc.vector.tensor_tensor_scan(cum[0:NE, lo:hi], mask[0:NE, lo:hi], mask[0:NE, lo:hi],
                                                     0.0, ALU.add, ALU.max))
                nc.vector.tensor_tensor(cum[0:NE, :], cum[0:NE, :], mask[0:NE, :], ALU.mult).then_inc(slots_ready, 1)
                dve.wait_ge(*full(f"sl{lay}"))
                nc.vector.tensor_copy(slot[:, :, :], bank(f"sl{lay}", 0, TT * NE)
                                      .rearrange("p (t e) -> p t e", e=NE)).then_inc(*empties(f"sl{lay}"))
                dve.wait_ge(*taken(f"sl{lay}"))

            def expert_pair(lay, i):
                gp = NP * lay + i
                L = f"L{lay}"
                es = bass.ds(2 * i, 2)
                iota = tab[:, T_IOTA:T_IOTA + CAP_L]
                nc.vector.tensor_tensor(
                    pick[:, :, :, :], slot[:, 0:LT, es].unsqueeze(3).to_broadcast([P, LT, 2, CAP_L]),
                    iota.unsqueeze(1).unsqueeze(1).to_broadcast([P, LT, 2, CAP_L]),
                    ALU.is_equal).then_inc(pick_ready, 1)
                nc.vector.tensor_tensor(
                    pick_c[:, :, :], slot[:, LT, es].unsqueeze(2).to_broadcast([P, 2, CAP_C]),
                    iota[:, 0:CAP_C].unsqueeze(1).to_broadcast([P, 2, CAP_C]),
                    ALU.is_equal).then_inc(pick_ready, 1)
                dve.wait_ge(pick_ready, 4 * gp + 2)
                nc.vector.tensor_tensor(
                    pick_g[:, :, :, :], pick[:, :, :, :],
                    aff[:, 0:LT, es].unsqueeze(3).to_broadcast([P, LT, 2, CAP_L]),
                    ALU.mult).then_inc(pick_ready, 1)
                nc.vector.tensor_tensor(
                    pick_gc[:, :, :], pick_c[:, :, :], aff[:, LT, es].unsqueeze(2).to_broadcast([P, 2, CAP_C]),
                    ALU.mult).then_inc(pick_ready, 1)
                for half in range(2):
                    name = L + f"XE{half}"
                    dve.wait_ge(*full(name, i))
                    nc.vector.tensor_copy(xe[:, 4 * half:4 * half + 4, :, 0:CAP_L], bank(name, 0, 4 * SEL_L)
                                          .rearrange("p (k e s) -> p k e s", k=4, e=2)).then_inc(*empties(name))
                dve.wait_ge(*full(L + "XEc", i))
                nc.vector.tensor_copy(xe[:, :, :, CAP_L:CAP], bank(L + "XEc", 0, KD * SEL_C)
                                      .rearrange("p (k e s) -> p k e s", k=KD, e=2)).then_inc(*empties(L + "XEc"))
                for e in range(2):
                    for m in range(2):
                        up = L + f"U{e}{m}"
                        dve.wait_ge(*full(up, i))
                        dve.wait_ge(*taken(L + f"G{e}{m}", i))
                        nc.vector.tensor_tensor(
                            hid[:, 4 * m:4 * m + 4, :], bank(up, 0, 4 * CAP).rearrange("p (f s) -> p f s", f=4),
                            sg[:, m, :, :], ALU.mult).then_inc(*empties(up))
                for half in range(2):
                    name = L + f"Y{half}"
                    dve.wait_ge(*full(name, i))
                    nc.vector.tensor_copy(ye[:, 512 * half:512 * (half + 1)], bank(name, 0, 512)).then_inc(*empties(name))
                for half in range(2):
                    name = L + f"Yc{half}"
                    dve.wait_ge(*full(name, i))
                    nc.vector.tensor_copy(ye_c[0:SEL_C, 512 * half:512 * (half + 1)],
                                          bank(name, 0, 512, SEL_C)).then_inc(*empties(name))
                for d in range(KD):
                    name = L + f"C{d}"
                    dve.wait_ge(*full(name, i))
                    nc.vector.scalar_tensor_tensor(
                        out=xT[:, d, 0:LAT], in0=bank(name, 0, LAT), scalar=mod[lay][:, G2 + d, 0:1],
                        in1=xT[:, d, 0:LAT], op0=ALU.mult, op1=ALU.add).then_inc(*empties(name))
                for half in range(2):
                    name = L + f"Cc{half}"
                    dve.wait_ge(*full(name, i))
                    for k in range(4):
                        d = 4 * half + k
                        ins = nc.vector.scalar_tensor_tensor(
                            out=xT[:, d, LAT:T], in0=bank(name, P * k, P * (k + 1)),
                            scalar=mod[lay][:, G2 + d, 1:2], in1=xT[:, d, LAT:T], op0=ALU.mult, op1=ALU.add)
                    ins.then_inc(*empties(name))

            for lay in range(2):
                if lay == 1:
                    pool_windows()
                    for k in range(KD):
                        add_mixed(k, f"pl{k}", f"pc{k}", gate_pool)
                norm(2 * lay + 1, lambda k: (h2T[:, k, 0:LAT], h2T[:, k, LAT:T]))
                route(lay)
                if lay == 0:
                    dve.wait_ge(new_v_stored, 16)
                with dve.Fori(0, NP) as i:
                    expert_pair(lay, i)
            for n in range(0, 2 * TT, 2):
                dve.wait_ge(*full(f"y{n}"))
                nc.vector.tensor_copy(y_rows[:, n // 2, 0:512], bank(f"y{n}", 0, 512)).then_inc(*empties(f"y{n}"))


_INS = ["x_prompt", "x_sample", "cache_k", "cache_v", "c", "c_ctx", "norm1", "norm2", "w_ada", "b_ada",
        "w_qkv", "q_norm", "k_norm", "w_o", "w_pool", "pool_scale", "w_router", "w_e_gate", "w_e_up", "w_e_down"]
_OUTS = {"y_prompt": (1, CTX, D), "y_sample": (1, LAT, D), "new_k": (1, 1, CTX, NKV, HD),
         "new_v": (1, 1, CTX, NKV, HD)}


def kernel(**inputs):
    import concourse.bacc as _bacc
    from concourse.bass_utils import run_bass_kernel_spmd as _run

    nc = _bacc.Bacc("TRN2", target_bir_lowering=False, num_devices=1)
    arrays, ins = {}, {}
    for name in _INS:
        arrays[f"in_{name}"] = np.ascontiguousarray(inputs[name])
    arrays["in_tables"] = shape_tables()
    for name, v in arrays.items():
        ins[name[3:]] = nc.dram_tensor(name, v.shape, mybir.dt.from_np(v.dtype), kind="ExternalInput").ap()
    outs = {name: nc.dram_tensor(f"out_{name}", shape, F32, kind="ExternalOutput").ap()
            for name, shape in _OUTS.items()}
    build(nc, ins, outs)
    r = _run(nc, [arrays], core_ids=[0])
    return tuple(r.results[0][f"out_{name}"] for name in _OUTS)
```

```python
from contextlib import ExitStack

import numpy as np

import concourse.bass as bass
from concourse import mybir

F32 = mybir.dt.float32
F32R = mybir.dt.float32r
ALU = mybir.AluOpType
ACT = mybir.ActivationFunctionType
AX = mybir.AxisListType

P = 128
D = 1024
KD = D // P
LAT, CTX = 512, 128
T = LAT + CTX
TT = T // P
LT = LAT // P
PAST = 128
GRID_W = 64
HD = 128
NH, NKV = D // HD, D // HD // 4
G = NH // NKV
KEYS = LAT + PAST
NE = 16
CAP_L, CAP_C = 2 * LAT // NE, 2 * CTX // NE
CAP = CAP_L + CAP_C
NP = NE // 2
SEL_L, SEL_C = 2 * CAP_L, 2 * CAP_C
NMOD = 6
MC = NMOD * KD
EPS = 1e-6
THETA = 10000.0
WINDOWS = (2, 4, 8, 16)
PADZ = 8
Z_L, Z_C = PADZ, PADZ + LAT + 2 * PADZ
ZW = Z_C + CTX + PADZ
UC = 512
KH = KD // 2
FRING = 12
RRING, SRING = 4, 4
ROWS = (CAP, P)
SH1, SC1, G1, SH2, SC2, G2 = (KD * m for m in range(NMOD))

V_C, V_CTX, V_N1, V_N2, V_PS, V_Q, V_K, V_ROWS = 0, 8, 16, 32, 48, 56, 57, 58
T_ID, T_SWAP, T_IOTA, T_INV, T_COS, T_SIN, T_COLS = 0, 128, 256, 320, 832, 1344, 1856


def shape_tables():
    f = np.float32
    tab = np.zeros((P, T_COLS), f)
    tab[:, T_ID:T_ID + P] = np.eye(P, dtype=f)
    p = np.arange(P)
    tab[p ^ 32, T_SWAP + p] = 1.0
    tab[:, T_IOTA:T_IOTA + CAP_L] = np.arange(1, CAP_L + 1, dtype=f)
    t = np.arange(CTX)
    for g, w in enumerate(WINDOWS):
        n = np.clip(t + w - w // 2, 0, CTX) - np.clip(t - w // 2, 0, CTX)
        tab[:, T_INV + CTX * g:T_INV + CTX * (g + 1)] = f(1) / n.astype(f)
    n = HD // 4
    inv_freq = np.power(f(THETA), -np.arange(n, dtype=f) / f(n)).astype(f)
    tok = np.arange(LAT)
    pos = np.stack([tok // GRID_W, tok % GRID_W]).astype(f)
    ang = pos[p // (2 * n)] * inv_freq[p % n][:, None]
    sign = np.where(p % (2 * n) < n, f(-1), f(1))[:, None]
    tab[:, T_COS:T_COS + LAT] = np.cos(ang)
    tab[:, T_SIN:T_SIN + LAT] = np.sin(ang) * sign
    return tab


def weight_order():
    u = [("ada0", n) for n in range(6)] + [("qkv", 2), ("qkv", 0)]
    u += [("ada0", n) for n in range(6, 10)] + [("qkv", 1)]
    u += [("ada0", 10), ("ada0", 11), ("ada1", 0), ("ada1", 1)]
    u += [("ada1", n) for n in range(2, 12)] + [("wo", 0), ("wo", 1)]
    return u


class PsumUses:

    def __init__(self):
        self.opened, self.filled = [0] * 8, [0] * 8
        self.at = {}

    def take(self, name, bank, unit=None):
        self.at[name] = (bank, self.opened[bank], 0, self.filled[bank], 0, unit, 0)
        self.opened[bank] += 1
        self.filled[bank] += unit is None

    def loop(self, prefix, uses, trips, base):
        opens = [sum(b == bank for _, b, _ in uses) for bank in range(8)]
        fills = [sum(b == bank and u is None for _, b, u in uses) for bank in range(8)]
        o, f = list(self.opened), list(self.filled)
        for name, b, u in uses:
            unit = None if u is None else ("split", base + u)
            self.at[prefix + name] = (b, o[b], opens[b], f[b], fills[b], unit, UNITS // SRING)
            o[b] += 1
            f[b] += u is None
        self.opened = [c + trips * n for c, n in zip(self.opened, opens)]
        self.filled = [c + trips * n for c, n in zip(self.filled, fills)]


HEADS = [("k", 0), ("k", 1)] + [("q", h) for h in range(NH)]
ADA_AFTER_HEAD = {2: (0, 6), 3: (0, 7), 4: (0, 8), 5: (0, 9), 6: (0, 10), 7: (0, 11), 8: (1, 0), 9: (1, 1)}
EXPERT_UNITS = ([(w, c, r) for c in range(2) for w in "gu" for r in range(2)]
                + [("d", c, r) for r in range(2) for c in range(2)])
UNITS = 2 * len(EXPERT_UNITS)
GATHER_USES = [("XE0", 0, None), ("XE1", 1, None), ("XEc", 2, None)]


SPLITS = UNITS * NP
POOL_UNIT = SPLITS


def pair_uses(gather):
    uses = []
    for e in range(2):
        n = UNITS // 2 * e
        uses += [(f"G{e}0", 0, n + 1), (f"U{e}0", 1, n + 3)]
        if e == 0:
            uses += [("PT", 6, None), ("PTc", 7, None)]
        uses += [(f"G{e}1", 2, n + 5), (f"T{e}0", 4, None), (f"U{e}1", 3, n + 7)]
        uses += [(f"D{e}0", 5, n + 10), (f"T{e}1", 7, None), (f"D{e}1", 6, n + 11)]
    uses += GATHER_USES if gather else []
    uses += [(f"C{d}", b, None) for d, b in enumerate((4, 7, 3, 0, 1, 2, 4, 7))]
    return uses + [("Cc0", 5, None), ("Cc1", 6, None)]


def plan_psum(unit_of, base):
    u = PsumUses()

    def last_of(kind, n):
        return "front", unit_of[(kind, n)] + 1

    u.take("vec", 7)
    u.take("bada", 6)
    for n in range(2 * TT):
        u.take(f"x{n}", n % 6)

    def norm(i):
        u.take(f"ssl{i}", 0)
        u.take(f"ssc{i}", 1)

    norm(0)
    u.take("ada0a", 7, last_of("ada0", 3))
    u.take("ada0b", 7, last_of("ada0", 11))
    for n in range(len(HEADS) + 2):
        if n < len(HEADS):
            u.take(f"hl{n}", 2 * (n % 2))
            last = {5: ("qkv", 0), 9: ("qkv", 1)}.get(n)
            u.take(f"hc{n}", 2 * (n % 2) + 1, last_of(*last) if last else None)
        if n == 1:
            for m, b in enumerate((6, 0, 6)):
                u.take(f"v{m}", b, last_of("qkv", 2) if m == 2 else None)
        if 1 <= n <= len(HEADS):
            u.take(f"hsl{n - 1}", 4)
            u.take(f"hsc{n - 1}", 5)
        if n >= 2:
            u.take(f"rot{n - 2}", 6)
        if n == 8:
            u.take("ada1", 7, last_of("ada1", 11))
    u.take("cachek", 5)
    u.take("newk", 4)
    for n in range(NH * TT + 3):
        if n < NH * TT:
            u.take(f"S{n}", 2 * (n % 2))
        if 2 <= n < NH * TT + 2:
            u.take(f"T{n - 2}", 4)
        if n >= 3 and (n - 3) % TT >= TT - 2:
            u.take(f"O{n - 3}", 6)
    for d in range(KD):
        u.take(f"wol{d}", 2 * (d % 2))
        u.take(f"woc{d}", 2 * (d % 2) + 1, last_of("wo", d // 4) if d % 4 == 3 else None)
    for lay in range(2):
        if lay == 1:
            norm(2)
            for d in range(KD):
                u.take(f"pl{d}", 2 * (d % 2))
                u.take(f"pc{d}", 2 * (d % 2) + 1, ("raw", POOL_UNIT) if d == KD - 1 else None)
        norm(2 * lay + 1)
        u.take(f"rt{lay}", 2)
        for n in range(2 * TT):
            u.take(f"ht{lay}_{n}", 3 + n % 3)
        u.take(f"afl{lay}", 6)
        u.take(f"afc{lay}", 7)
        u.take(f"sl{lay}", 2)
        for name, b, _ in GATHER_USES:
            u.take(f"L{lay}g{name}", b)
        u.loop(f"L{lay}", pair_uses(True), NP - 1, SPLITS * lay)
        for name, b, n in pair_uses(False):
            u.take(f"L{lay}z{name}", b, None if n is None else ("split", SPLITS * (lay + 1) - UNITS + n))
    for n in range(2 * TT):
        u.take(f"y{n}", n % 8)
    return u.at


def build(nc, a, out):
    front = weight_order()
    unit_of = {u: 2 * n for n, u in enumerate(front)}
    base = {0: 0, 1: POOL_UNIT + 1}
    use = plan_psum(unit_of, base)

    with ExitStack() as ctx:
        def sb(name, *shape):
            return ctx.enter_context(nc.sbuf_tensor(name, [P, *shape], F32))

        def sem(name):
            return ctx.enter_context(nc.semaphore(name))

        xT = sb("xT", KD, T)
        bufH = sb("bufH", KD * ZW)
        tab = sb("tab", T_COS)
        vec_rows = sb("vec_rows", P)
        bada_rows = sb("bada_rows", P)
        vec = sb("vec", V_ROWS)
        bada = sb("bada", 2 * MC)
        cond = sb("cond", KD, 2)
        mod = [sb(f"mod{i}", MC, 2) for i in range(2)]
        amp = [sb(f"amp{i}", KD, 2) for i in range(4)]
        gate_pool = sb("gate_pool", KD, 2)
        wr = sb("wr", 2, KD, NE)
        ones = sb("ones", P)
        eps = sb("eps", 1)
        new_k = sb("new_k", NKV * HD)
        stat = sb("stat", 16)
        rmax = sb("rmax", 3, TT)
        aff = sb("aff", TT, NE)
        slot = sb("slot", TT, NE)
        top8 = sb("top8", 8)

        free = [-(-nc.sbuf_base // 64) * 64]

        def place(name, at, *shape, dtype=F32):
            return nc.alloc_sbuf_tensor_at(name, [P, *shape], dtype, offset=at), at + 4 * int(np.prod(shape))

        slots_at = free[0]
        unit_bytes = 4 * KH * UC
        fring = [place(f"front{n}", slots_at + unit_bytes * n, KH, UC)[0] for n in range(FRING)]
        raw_w = [place(f"raw_w{n}", slots_at + unit_bytes * n, KH, UC)[0] for n in range(RRING)]
        split_w = [place(f"split_w{n}", slots_at + unit_bytes * (RRING + 2 * n), 2, KH, UC, dtype=F32R)[0]
                   for n in range(SRING)]
        shared_at = slots_at + unit_bytes * FRING
        bufQ, at = place("bufQ", shared_at, KD * T)
        bufS, at = place("bufS", at, 8704)
        xe, at = place("xe", shared_at, 2, 2 * KD * P + P, dtype=F32R)
        hT, at = place("hT", at, 2, KD, P, dtype=F32R)
        ye, at = place("ye", at, 2, D, dtype=F32R)
        ye_c, at = place("ye_c", at, 2, D, dtype=F32R)
        put, at = place("put", at, LAT, dtype=F32R)
        put_c, at = place("put_c", at, CTX, dtype=F32R)
        hid, at = place("hid", at, 2, UC)
        pick, at = place("pick", at, LT, 2, CAP_L)
        pick_c, at = place("pick_c", at, 2, CAP_C)
        pick_w, at = place("pick_w", at, 2, CAP_L)
        gates, at = place("gates", at, 4)

        ident, swap = tab[:, T_ID:T_ID + P], tab[:, T_SWAP:T_SWAP + P]

        def view(buf, at, *shape):
            n = int(np.prod(shape))
            v = buf[:, at:at + n]
            names = "abcd"[:len(shape)]
            if len(shape) == 1:
                return v
            return v.rearrange(f"p ({' '.join(names)}) -> p {' '.join(names)}",
                               **{k: s for k, s in zip(names, shape)})

        x_rows = view(bufH, 0, TT, D)
        hA = view(bufH, 0, KD, T)
        oT = hA
        h_rows = x_rows
        y_rows = x_rows
        Z = view(bufH, 0, KD, ZW)
        qT = view(bufQ, 0, NH, T)
        h2T = view(bufQ, 0, KD, T)
        pooled = view(bufQ, 0, KD, T)
        V = view(bufS, 0, TT + 1, NKV * HD)
        kT = view(bufS, 1536, NKV, KEYS)
        kTc = view(bufS, 2816, NKV, CTX)
        cos, sin = view(bufS, 3072, LAT), view(bufS, 3584, LAT)
        raw = view(bufS, 4096, 2, T)
        sqh = view(bufS, 5376, 2, T)
        rrh = view(bufS, 6656, 2, T)
        cache_rows = view(bufS, 7936, NKV * HD)
        probs = view(bufS, 4096, 3, KEYS)
        pT = view(bufS, 6016, TT, LAT)
        pTc = view(bufS, 8576, CTX)
        sq = view(bufS, 4096, 2, T)
        rstd = view(bufS, 5376, T)
        win = [view(bufS, n * 2 * ZW, 2, ZW) for n in range(2)]
        work = view(bufS, 6016, T)
        mask = view(bufS, 6656, T)
        cum = view(bufS, 7296, T)
        zeros = view(bufS, 7936, T)
        psum = ctx.enter_context(nc.psum_tensor("psum", [P, 8 * 512], F32))

        def bank(name, lo, hi, rows=P):
            b = use[name][0]
            return psum[0:rows, 512 * b + lo:512 * b + hi]

        def xe_lat(part, half):
            v = xe[:, part, 0:2 * (KD * P + CAP_L)].rearrange("p (e x) -> p e x", e=2)
            return v[:, :, 4 * P * half:4 * P * (half + 1)].rearrange("p e (k c) -> p e k c", c=P)[:, :, :, 0:CAP_L]

        def xe_ctx(part):
            full_rows = xe[:, part, :]
            return [full_rows[:, CAP_L:CAP_L + KD * P].rearrange("p (k c) -> p k c", c=P)[:, :, 0:CAP_C],
                    full_rows[:, KD * P:2 * KD * P].rearrange("p (k c) -> p k c", c=P)[:, :, 0:CAP_C]]

        def out_rows(e):
            if e == 0:
                return ((0, CAP_L, ye, 0), (CAP_L, CAP, ye_c, 2))
            return ((CAP_L, P, ye, 1), (0, CAP_C, ye_c, 3))

        x_loaded = [sem(f"x_loaded{t}") for t in range(TT)]
        ident_loaded = sem("ident_loaded")
        tab_loaded = sem("tab_loaded")
        trig_loaded = sem("trig_loaded")
        vec_loaded = sem("vec_loaded")
        bada_loaded = sem("bada_loaded")
        wr_loaded = sem("wr_loaded")
        cache_loaded = sem("cache_loaded")
        front_full = [sem(f"front_full{n}") for n in range(FRING)]
        front_used = [sem(f"front_used{n}") for n in range(FRING)]
        raw_full = [sem(f"raw_full{n}") for n in range(RRING)]
        raw_used = [sem(f"raw_used{n}") for n in range(RRING)]
        split_used = [sem(f"split_used{n}") for n in range(SRING)]
        rounded = sem("rounded")
        xeh_ready = sem("xeh_ready")
        zeros_set = sem("zeros_set")
        hTh_ready = sem("hTh_ready")
        yeh_ready = sem("yeh_ready")
        bank_full = [sem(f"bank_full{b}") for b in range(8)]
        bank_empty = [sem(f"bank_empty{b}") for b in range(8)]
        dve_step = sem("dve_step")
        consts_set = sem("consts_set")
        cond_ready = sem("cond_ready")
        amp_ready = sem("amp_ready")
        nsq_ready = sem("nsq_ready")
        nsq_used = sem("nsq_used")
        nscaled = sem("nscaled")
        h_ready = sem("h_ready")
        raw_ready = sem("raw_ready")
        hsq_ready = sem("hsq_ready")
        hnorm_ready = sem("hnorm_ready")
        head_ready = sem("head_ready")
        nmax_ready = sem("nmax_ready")
        probs_ready = sem("probs_ready")
        pooled_ready = sem("pooled_ready")
        aexp_ready = sem("aexp_ready")
        aff_ready = sem("aff_ready")
        slots_ready = sem("slots_ready")
        pick_ready = sem("pick_ready")
        new_v_stored = sem("new_v_stored")
        new_k_stored = sem("new_k_stored")
        stored = sem("stored")

        def full(name, i=0):
            _, _, _, n, per, unit, per_unit = use[name]
            if unit is None:
                return bank_full[use[name][0]], n + 1 + (per * i if per else 0)
            kind, u = unit
            sems = {"front": front_used, "raw": raw_used, "split": split_used}[kind]
            return sems[u % len(sems)], u // len(sems) + 1 + (per_unit * i if per_unit else 0)

        def empty(name, i=0):
            b, n, per = use[name][:3]
            return bank_empty[b], n + (per * i if per else 0)

        def fills(name):
            return full(name)[0], 1

        def empties(name):
            return bank_empty[use[name][0]], 1

        def taken(name, i=0):
            s, v = empty(name, i)
            return s, v + 1

        def wait_empty(eng, name, i=0):
            s, v = empty(name, i)
            if not isinstance(v, int) or v > 0:
                eng.wait_ge(s, v)

        unit_cols = {
            "ada0": lambda n: a["w_ada"][0, :, UC * n:UC * (n + 1)],
            "ada1": lambda n: a["w_ada"][1, :, UC * n:UC * (n + 1)],
            "qkv": lambda n: a["w_qkv"][0, :, UC * n:UC * (n + 1)],
            "wo": lambda n: a["w_o"][0, :, UC * n:UC * (n + 1)],
        }

        block = ctx.enter_context(nc.Block())

        @block.sync
        def _(sp):
            for t in range(TT):
                src = a["x_sample"][0, P * t:P * (t + 1), :] if t < LT else a["x_prompt"][0, :, :]
                sp.dma_start(x_rows[:, t, :], src).then_inc(x_loaded[t], 16)
            for n, (kind, m) in enumerate(front):
                for r in range(2):
                    u = 2 * n + r
                    if u >= FRING:
                        sp.wait_ge(front_used[u % FRING], u // FRING)
                    sp.dma_start(fring[u % FRING][:, :, :],
                                 unit_cols[kind](m)[P * KH * r:P * KH * (r + 1), :]
                                 .rearrange("(k p) n -> p k n", p=P)).then_inc(front_full[u % FRING], 16)

            def expert_units(lay, e0, first, i=0):
                for e in range(2):
                    for m, (w, c, r) in enumerate(EXPERT_UNITS):
                        u = base[lay] + UNITS // 2 * e + m + first
                        src = {"g": a["w_e_gate"], "u": a["w_e_up"], "d": a["w_e_down"]}[w]
                        if isinstance(i, int) and u < RRING:
                            last = (2 * len(front) - 1 - u) // FRING * FRING + u
                            sp.wait_ge(front_used[u], last // FRING + 1)
                        else:
                            sp.wait_ge(raw_used[u % RRING], u // RRING + (0 if isinstance(i, int) else UNITS // RRING * i))
                        sp.dma_start(raw_w[u % RRING][:, :, :],
                                     src[lay, bass.ds(e0 + e, 1), P * KH * r:P * KH * (r + 1), UC * c:UC * (c + 1)]
                                     .rearrange("e (k p) n -> p (e k) n", p=P)
                                     ).then_inc(raw_full[u % RRING], 16)

            for lay in range(2):
                expert_units(lay, 0, 0)
                with sp.Fori(0, NP - 1) as i:
                    expert_units(lay, 2 * i + 2, UNITS, i)
                if lay == 0:
                    sp.wait_ge(raw_used[POOL_UNIT % RRING], POOL_UNIT // RRING)
                    sp.dma_start(raw_w[POOL_UNIT % RRING][:, :, :].rearrange("p k (h n) -> p (k h) n", h=2),
                                 a["w_pool"][0].rearrange("g (c p) n -> p (g c) n", p=P)
                                 ).then_inc(raw_full[POOL_UNIT % RRING], 16)
            for t in range(TT):
                sp.wait_ge(*taken(f"y{2 * t}"))
                sp.wait_ge(*taken(f"y{2 * t + 1}"))
                dst = out["y_sample"][0, P * t:P * (t + 1), :] if t < LT else out["y_prompt"][0, :, :]
                sp.dma_start(dst, y_rows[:, t, :]).then_inc(stored, 16)
            sp.wait_ge(stored, 16 * TT)

        @block.gpsimd
        def _(pool):
            pool.wait_ge(*taken("v2"))
            pool.dma_start(out["new_v"][0, 0].rearrange("t h d -> t (h d)"),
                           V[:, TT, :]).then_inc(new_v_stored, 16)
            pool.wait_ge(*taken("newk"))
            pool.dma_start(out["new_k"][0, 0].rearrange("t h d -> t (h d)"),
                           new_k[:, :]).then_inc(new_k_stored, 16)
            def low_unit(lay, m, i=0, looped=False):
                s, r = SPLITS * lay + m, base[lay] + m
                pool.wait_ge(rounded, s + 1 + (UNITS * i if looped else 0))
                w = split_w[s % SRING]
                nc.gpsimd.tensor_tensor(w[:, 1, :, :], raw_w[r % RRING][:, :, :], w[:, 0, :, :].bitcast(F32),
                                        ALU.subtract).then_inc(raw_used[r % RRING], 1)

            for lay in range(2):
                with pool.Fori(0, NP) as i:
                    for m in range(3, UNITS, 4):
                        low_unit(lay, m, i, True)
            pool.wait_ge(new_v_stored, 16)
            pool.wait_ge(new_k_stored, 16)

        @block.tensor
        def _(pe):
            def front_unit(kind, n):
                u = unit_of[(kind, n)]
                for r in range(2):
                    pe.wait_ge(front_full[(u + r) % FRING], 16 * ((u + r) // FRING + 1))
                return lambda k: fring[(u + k // KH) % FRING][:, k % KH, :]

            def first_half_used(kind, n):
                return front_used[unit_of[(kind, n)] % FRING], 1

            pe.wait_ge(ident_loaded, 16)
            pe.wait_ge(vec_loaded, 16 * 7)
            pe.transpose(bank("vec", 0, V_ROWS), vec_rows[0:V_ROWS, :],
                         ident[0:V_ROWS, 0:V_ROWS]).then_inc(*fills("vec"))
            pe.wait_ge(bada_loaded, 16)
            pe.transpose(bank("bada", 0, 2 * MC), bada_rows[0:2 * MC, :],
                         ident[0:2 * MC, 0:2 * MC]).then_inc(*fills("bada"))
            for t in range(TT):
                pe.wait_ge(x_loaded[t], 16)
                for half in range(2):
                    name = f"x{2 * t + half}"
                    wait_empty(pe, name)
                    for k in range(4):
                        kk = 4 * half + k
                        mm = pe.transpose(bank(name, P * k, P * (k + 1)),
                                          x_rows[:, t, P * kk:P * (kk + 1)], ident)
                    mm.then_inc(*fills(name))

            def norm_stats(i):
                wait_empty(pe, f"ssl{i}")
                wait_empty(pe, f"ssc{i}")
                for k in range(KD):
                    pe.wait_ge(nsq_ready, KD * i + k + 1)
                    ml = pe.matmul(bank(f"ssl{i}", 0, LAT), ones[:, :], sq[:, k % 2, 0:LAT],
                                   start=(k == 0), stop=(k == KD - 1))
                    mc = pe.matmul(bank(f"ssc{i}", 0, CTX), ones[:, :], sq[:, k % 2, LAT:T],
                                   start=(k == 0), stop=(k == KD - 1))
                    if k == KD - 1:
                        ml.then_inc(*fills(f"ssl{i}"))
                        mc.then_inc(*fills(f"ssc{i}"))
                    else:
                        mc.then_inc(nsq_used, 1)

            def ada_unit(lay, n):
                kind = f"ada{lay}"
                w = front_unit(kind, n)
                name = "ada1" if lay else ("ada0a" if n < 4 else "ada0b")
                if n == 0 or (lay == 0 and n == 4):
                    wait_empty(pe, name)
                if lay == 0 and n == 0:
                    pe.wait_ge(cond_ready, 1)
                for c in range(UC // P):
                    at = 2 * (4 * n + c)
                    for k in range(KD):
                        mm = pe.matmul(bank(name, at, at + 2), w(k)[:, P * c:P * (c + 1)],
                                       cond[:, k, :], start=(k == 0), stop=(k == KD - 1))
                        if c == UC // P - 1 and k == KH - 1:
                            mm.then_inc(*first_half_used(kind, n))
                mm.then_inc(front_used[(unit_of[(kind, n)] + 1) % FRING], 1)

            pe.wait_ge(consts_set, 2)
            norm_stats(0)
            for n in range(6):
                ada_unit(0, n)

            def project(n):
                kind, h = HEADS[n]
                m = 2 if kind == "k" else h // 4
                c = h if kind == "k" else h % 4
                w = front_unit("qkv", m)
                wait_empty(pe, f"hl{n}")
                wait_empty(pe, f"hc{n}")
                for k in range(KD):
                    if n == 0:
                        pe.wait_ge(h_ready, k + 1)
                    ml = pe.matmul(bank(f"hl{n}", 0, LAT), w(k)[:, P * c:P * (c + 1)],
                                   hA[:, k, 0:LAT], start=(k == 0), stop=(k == KD - 1))
                    mc = pe.matmul(bank(f"hc{n}", 0, CTX), w(k)[:, P * c:P * (c + 1)],
                                   hA[:, k, LAT:T], start=(k == 0), stop=(k == KD - 1))
                    if kind == "q" and c == 3 and k == KH - 1:
                        mc.then_inc(*first_half_used("qkv", m))
                ml.then_inc(*fills(f"hl{n}"))
                mc.then_inc(*fills(f"hc{n}"))

            def values():
                w = front_unit("qkv", 2)
                for t in range(TT):
                    name = f"v{t // 2}"
                    if t % 2 == 0:
                        wait_empty(pe, name)
                    o = NKV * HD * (t % 2)
                    for k in range(KD):
                        mm = pe.matmul(bank(name, o, o + NKV * HD), hA[:, k, P * t:P * (t + 1)],
                                       w(k)[:, NKV * HD:2 * NKV * HD], start=(k == 0), stop=(k == KD - 1))
                        if t == TT - 1 and k == KH - 1:
                            mm.then_inc(*first_half_used("qkv", 2))
                    if t % 2 == 1 or t == TT - 1:
                        mm.then_inc(*fills(name))

            def head_stats(n):
                wait_empty(pe, f"hsl{n}")
                wait_empty(pe, f"hsc{n}")
                pe.wait_ge(hsq_ready, n + 1)
                pe.matmul(bank(f"hsl{n}", 0, LAT), ones[:, :], sqh[:, n % 2, 0:LAT],
                          start=True, stop=True).then_inc(*fills(f"hsl{n}"))
                pe.matmul(bank(f"hsc{n}", 0, CTX), ones[:, :], sqh[:, n % 2, LAT:T],
                          start=True, stop=True).then_inc(*fills(f"hsc{n}"))

            def rotate(n):
                wait_empty(pe, f"rot{n}")
                pe.wait_ge(hnorm_ready, n + 1)
                if n == 0:
                    pe.wait_ge(tab_loaded, 16)
                pe.matmul(bank(f"rot{n}", 0, LAT), swap, raw[:, n % 2, 0:LAT],
                          start=True, stop=True).then_inc(*fills(f"rot{n}"))

            for n in range(len(HEADS) + 2):
                if n < len(HEADS):
                    project(n)
                if n == 1:
                    values()
                if 1 <= n <= len(HEADS):
                    head_stats(n - 1)
                if n >= 2:
                    rotate(n - 2)
                if n in ADA_AFTER_HEAD:
                    ada_unit(*ADA_AFTER_HEAD[n])

            pe.wait_ge(cache_loaded, 32)
            wait_empty(pe, "cachek")
            for g in range(NKV):
                mm = pe.transpose(bank("cachek", P * g, P * (g + 1)),
                                  cache_rows[:, HD * g:HD * (g + 1)], ident)
            mm.then_inc(*fills("cachek"))
            wait_empty(pe, "newk")
            pe.wait_ge(head_ready, NKV)
            for g in range(NKV):
                mm = pe.transpose(bank("newk", P * g, P * (g + 1)), kTc[:, g, :], ident)
            mm.then_inc(*fills("newk"))

            def scores(n):
                h, t = n // TT, n % TT
                g = h // G
                wait_empty(pe, f"S{n}")
                if t == 0:
                    pe.wait_ge(head_ready, NKV + h + 1)
                q = qT[:, h, P * t:P * (t + 1)]
                if t < LT:
                    if n == 0:
                        pe.wait_ge(*taken("cachek"))
                        pe.wait_ge(*taken("v2"))
                    pe.matmul(bank(f"S{n}", 0, LAT), q, kT[:, g, 0:LAT], start=True, stop=True)
                    mm = pe.matmul(bank(f"S{n}", LAT, KEYS), q, kT[:, g, LAT:KEYS], start=True, stop=True)
                else:
                    mm = pe.matmul(bank(f"S{n}", 0, CTX), q, kTc[:, g, :], start=True, stop=True)
                mm.then_inc(*fills(f"S{n}"))

            def probs_turn(n):
                wait_empty(pe, f"T{n}")
                pe.wait_ge(probs_ready, n + 1)
                for c in range(TT if n % TT < LT else 1):
                    mm = pe.transpose(bank(f"T{n}", P * c, P * (c + 1)),
                                      probs[:, n % 3, P * c:P * (c + 1)], ident)
                mm.then_inc(*fills(f"T{n}"))

            def weigh(n):
                h, t = n // TT, n % TT
                g = h // G
                wait_empty(pe, f"O{n}")
                pe.wait_ge(*taken(f"T{n}"))
                if t == LT - 1:
                    for c in range(TT):
                        mm = pe.matmul(bank(f"O{n}", 0, LAT), V[:, c, HD * g:HD * (g + 1)],
                                       pT[:, c, :], start=(c == 0), stop=(c == TT - 1))
                else:
                    mm = pe.matmul(bank(f"O{n}", 0, CTX), V[:, TT, HD * g:HD * (g + 1)], pTc[:, :],
                                   start=True, stop=True)
                mm.then_inc(*fills(f"O{n}"))

            for n in range(NH * TT + 3):
                if n < NH * TT:
                    scores(n)
                if 2 <= n < NH * TT + 2:
                    probs_turn(n - 2)
                if n >= 3 and (n - 3) % TT >= TT - 2:
                    weigh(n - 3)
                if n % 4 == 1 and n // 4 < 10:
                    ada_unit(1, 2 + n // 4)

            pe.wait_ge(*taken(f"O{NH * TT - 1}"))
            for d in range(KD):
                w = front_unit("wo", d // 4)
                c = d % 4
                wait_empty(pe, f"wol{d}")
                wait_empty(pe, f"woc{d}")
                for h in range(NH):
                    ml = pe.matmul(bank(f"wol{d}", 0, LAT), w(h)[:, P * c:P * (c + 1)],
                                   oT[:, h, 0:LAT], start=(h == 0), stop=(h == NH - 1))
                    mc = pe.matmul(bank(f"woc{d}", 0, CTX), w(h)[:, P * c:P * (c + 1)],
                                   oT[:, h, LAT:T], start=(h == 0), stop=(h == NH - 1))
                    if c == 3 and h == KH - 1:
                        mc.then_inc(*first_half_used("wo", d // 4))
                ml.then_inc(*fills(f"wol{d}"))
                mc.then_inc(*fills(f"woc{d}"))

            def pool_products():
                norm_stats(2)
                pe.wait_ge(raw_full[POOL_UNIT % RRING], 16 * (POOL_UNIT // RRING + 1))
                w = raw_w[POOL_UNIT % RRING][:, :, :].rearrange("p k (h n) -> p (k h) n", h=2)
                for k in range(KD):
                    g = k // 2
                    wait_empty(pe, f"pl{k}")
                    wait_empty(pe, f"pc{k}")
                    pe.wait_ge(pooled_ready, g + 1)
                    for c in range(2):
                        wc = w[:, 2 * g + c, P * (k % 2):P * (k % 2 + 1)]
                        ml = pe.matmul(bank(f"pl{k}", 0, LAT), wc, pooled[:, 2 * g + c, 0:LAT],
                                       start=(c == 0), stop=(c == 1))
                        mc = pe.matmul(bank(f"pc{k}", 0, CTX), wc, pooled[:, 2 * g + c, LAT:T],
                                       start=(c == 0), stop=(c == 1))
                    ml.then_inc(*fills(f"pl{k}"))
                    mc.then_inc(*fills(f"pc{k}"))

            def route(lay):
                norm_stats(2 * lay + 1)
                if lay == 0:
                    pe.wait_ge(wr_loaded, 32)
                wait_empty(pe, f"rt{lay}")
                pe.wait_ge(h_ready, KD * (2 * lay + 2))
                for t in range(TT):
                    for k in range(KD):
                        mm = pe.matmul(bank(f"rt{lay}", NE * t, NE * (t + 1)), h2T[:, k, P * t:P * (t + 1)],
                                       wr[:, lay, k, :], start=(k == 0), stop=(k == KD - 1))
                mm.then_inc(*fills(f"rt{lay}"))
                def turn_h(n):
                    t, half = n // 2, n % 2
                    name = f"ht{lay}_{n}"
                    wait_empty(pe, name)
                    for k in range(4):
                        mm = pe.transpose(bank(name, P * k, P * (k + 1)),
                                          h2T[:, 4 * half + k, P * t:P * (t + 1)], ident)
                    mm.then_inc(*fills(name))

                for n in range(3):
                    turn_h(n)
                wait_empty(pe, f"afl{lay}")
                wait_empty(pe, f"afc{lay}")
                pe.wait_ge(aff_ready, lay + 1)
                for t in range(LT):
                    mm = pe.transpose(bank(f"afl{lay}", P * t, P * (t + 1), NE), aff[:, t, :], ident)
                mm.then_inc(*fills(f"afl{lay}"))
                pe.transpose(bank(f"afc{lay}", 0, P, NE), aff[:, LT, :], ident).then_inc(*fills(f"afc{lay}"))
                for n in range(3, 2 * TT):
                    turn_h(n)
                wait_empty(pe, f"sl{lay}")
                pe.wait_ge(slots_ready, lay + 1)
                for t in range(TT):
                    mm = pe.transpose(bank(f"sl{lay}", NE * t, NE * (t + 1)),
                                      cum[0:NE, P * t:P * (t + 1)], ident[0:NE, 0:NE])
                mm.then_inc(*fills(f"sl{lay}"))
                pe.wait_ge(*taken(f"ht{lay}_{2 * TT - 1}"))

            def gather(L, n_pick, i=0):
                pe.wait_ge(pick_ready, n_pick)
                for half in range(2):
                    name = L + f"XE{half}"
                    wait_empty(pe, name, i)
                    for k in range(4):
                        kk = 4 * half + k
                        for c in range(LT):
                            mm = pe.matmul(bank(name, P * k, P * (k + 1)),
                                           h_rows[:, c, P * kk:P * (kk + 1)],
                                           pick[:, c, :, :].rearrange("p e s -> p (e s)"),
                                           start=(c == 0), stop=(c == LT - 1))
                    mm.then_inc(*fills(name))
                wait_empty(pe, L + "XEc", i)
                for k in range(KD):
                    mm = pe.matmul(bank(L + "XEc", SEL_C * k, SEL_C * (k + 1)),
                                   h_rows[:, LT, P * k:P * (k + 1)],
                                   pick_c[:, :, :].rearrange("p e s -> p (e s)"), start=True, stop=True)
                mm.then_inc(*fills(L + "XEc"))

            def expert_pair(lay, L, pair, i, last):
                per_s, per_r = ((0, 0) if last else (UNITS // SRING * i, UNITS // RRING * i))
                gp = NP * lay + pair
                first_s = SPLITS * lay + (SPLITS - UNITS if last else 0)
                first_r = base[lay] + (SPLITS - UNITS if last else 0)

                def split_unit(m):
                    r = first_r + m
                    pe.wait_ge(raw_used[r % RRING], r // RRING + 1 + per_r)
                    return split_w[(first_s + m) % SRING]

                def three_passes(name, e, m, high, low, half, closes):
                    w = split_unit(m)
                    for k in range(KH):
                        kk = KH * half + k
                        for j, (x, part) in enumerate(((high, 0), (high, 1), (low, 0))):
                            mm = pe.matmul(bank(name, 0, UC, ROWS[e]), x(kk), w[:, part, k, :],
                                           start=(half == 0 and k == 0 and j == 0),
                                           stop=(half == 1 and k == KH - 1 and j == 2))
                    if closes:
                        mm.then_inc(*fills(name))
                    else:
                        mm.then_inc(split_used[(first_s + m) % SRING], 1)

                def turn_hidden(e, half):
                    name = L + f"T{e}{half}"
                    wait_empty(pe, name, i)
                    pe.wait_ge(*taken(L + f"U{e}{half}", i))
                    for k in range(4):
                        mm = pe.transpose(bank(name, ROWS[e] * k, ROWS[e] * (k + 1)),
                                          hid[0:ROWS[e], half, P * k:P * (k + 1)], ident[0:ROWS[e], 0:ROWS[e]])
                    mm.then_inc(*fills(name))

                for e in range(2):
                    n0 = UNITS // 2 * e

                    def tokens(part):
                        return lambda k: xe[:, part, KD * P * e + P * k:KD * P * e + P * k + ROWS[e]]

                    def hidden(part):
                        return lambda k: hT[:, part, k, 0:ROWS[e]]

                    def gate_up(m, kind, c):
                        name = L + f"{kind}{e}{c}"
                        wait_empty(pe, name, i)
                        for r in range(2):
                            three_passes(name, e, n0 + m + r, tokens(0), tokens(1), r, r == 1)

                    gate_up(0, "G", 0)
                    gate_up(2, "U", 0)
                    if e == 0:
                        wait_empty(pe, L + "PT", i)
                        wait_empty(pe, L + "PTc", i)
                        for c in range(LT):
                            mm = pe.transpose(bank(L + "PT", P * c, P * (c + 1)),
                                              pick[:, c, :, :].rearrange("p e s -> p (e s)"), ident)
                        mm.then_inc(*fills(L + "PT"))
                        wide = pick_w[:, :, :].rearrange("p e s -> p (e s)")
                        es = bass.ds(2 * pair, 2)
                        pe.transpose(bank(L + "PTc", 0, CTX), wide, ident)
                        for c in range(LT):
                            pe.matmul(bank(L + "PTc", CTX, CTX + 2), pick[:, c, :, :].rearrange("p e s -> p (e s)"),
                                      aff[:, c, es], start=(c == 0), stop=(c == LT - 1))
                        pe.matmul(bank(L + "PTc", CTX + 2, CTX + 4), wide, aff[:, LT, es],
                                  start=True, stop=True).then_inc(*fills(L + "PTc"))
                    gate_up(4, "G", 1)
                    turn_hidden(e, 0)
                    gate_up(6, "U", 1)
                    for c in range(2):
                        wait_empty(pe, L + f"D{e}{c}", i)
                        if c == 0:
                            pe.wait_ge(*taken(L + f"T{e}0", i))
                        three_passes(L + f"D{e}{c}", e, n0 + 8 + c, hidden(0), hidden(1), 0, False)
                        if c == 0:
                            turn_hidden(e, 1)
                    if e == 1 and not last:
                        gather(L, 3 * gp + 6, i)
                    pe.wait_ge(*taken(L + f"T{e}1", i))
                    for c in range(2):
                        three_passes(L + f"D{e}{c}", e, n0 + 10 + c, hidden(0), hidden(1), 1, True)

                pe.wait_ge(*taken(L + "PTc", i))
                for d in range(KD):
                    name = L + f"C{d}"
                    wait_empty(pe, name, i)
                    if d % 4 == 0:
                        pe.wait_ge(*taken(L + f"D1{d // 4}", i))
                    pe.matmul(bank(name, 0, LAT), ye[:, 0, P * d:P * (d + 1)], put[:, :], start=True, stop=False)
                    pe.matmul(bank(name, 0, LAT), ye[:, 1, P * d:P * (d + 1)], put[:, :],
                              start=False, stop=True).then_inc(*fills(name))
                for half in range(2):
                    name = L + f"Cc{half}"
                    wait_empty(pe, name, i)
                    for k in range(4):
                        d = 4 * half + k
                        pe.matmul(bank(name, P * k, P * (k + 1)), ye_c[0:CAP, 0, P * d:P * (d + 1)],
                                  put_c[0:CAP, :], start=True, stop=False)
                        mm = pe.matmul(bank(name, P * k, P * (k + 1)), ye_c[0:CAP, 1, P * d:P * (d + 1)],
                                       put_c[0:CAP, :], start=False, stop=True)
                    mm.then_inc(*fills(name))

            for lay in range(2):
                if lay == 1:
                    pool_products()
                route(lay)
                gather(f"L{lay}g", 3 * NP * lay + 3)
                with pe.Fori(0, NP - 1) as i:
                    expert_pair(lay, f"L{lay}", i, i, False)
                expert_pair(lay, f"L{lay}z", NP - 1, 0, True)

            pe.wait_ge(*taken("L1zCc1"))
            for n in range(2 * TT):
                t, half = n // 2, n % 2
                name = f"y{n}"
                wait_empty(pe, name)
                for k in range(4):
                    mm = pe.transpose(bank(name, P * k, P * (k + 1)),
                                      xT[:, 4 * half + k, P * t:P * (t + 1)], ident)
                mm.then_inc(*fills(name))

        @block.scalar
        def _(act):
            act.dma_start(ident, a["tables"][:, T_ID:T_ID + P]).then_inc(ident_loaded, 16)
            rows = [(V_C, V_CTX, a["c"].rearrange("a (k p) -> (a k) p", p=P)),
                    (V_CTX, V_N1, a["c_ctx"].rearrange("(k p) -> k p", p=P)),
                    (V_N1, V_N2, a["norm1"].rearrange("a (k p) -> (a k) p", p=P)),
                    (V_N2, V_PS, a["norm2"].rearrange("a (k p) -> (a k) p", p=P)),
                    (V_PS, V_Q, a["pool_scale"].rearrange("a (k p) -> (a k) p", p=P)),
                    (V_Q, V_K, a["q_norm"]), (V_K, V_ROWS, a["k_norm"])]
            for lo, hi, src in rows:
                act.dma_start(vec_rows[lo:hi, :], src).then_inc(vec_loaded, 16)
            act.dma_start(bada_rows[0:2 * MC, :],
                          a["b_ada"].rearrange("l (m p) -> (l m) p", p=P)).then_inc(bada_loaded, 16)
            act.dma_start(tab[:, T_SWAP:T_COS], a["tables"][:, T_SWAP:T_COS]).then_inc(tab_loaded, 16)
            act.dma_start(cos, a["tables"][:, T_COS:T_SIN]).then_inc(trig_loaded, 16)
            act.dma_start(sin, a["tables"][:, T_SIN:T_COLS]).then_inc(trig_loaded, 16)
            act.dma_start(cache_rows, a["cache_k"][0, 0].rearrange("t h d -> t (h d)")).then_inc(cache_loaded, 16)
            act.dma_start(V[:, LT, :], a["cache_v"][0, 0].rearrange("t h d -> t (h d)")).then_inc(cache_loaded, 16)
            for lay in range(2):
                act.dma_start(wr[:, lay, :, :],
                              a["w_router"][lay].rearrange("(k p) e -> p k e", p=P)).then_inc(wr_loaded, 16)

            act.wait_ge(*taken("vec"))
            nc.scalar.activation(cond[:, :, :].rearrange("p k t -> p t k"),
                                 vec[:, V_C:V_N1].rearrange("p (t k) -> p t k", t=2),
                                 ACT.Silu).then_inc(cond_ready, 1)
            for n in range(1, 2 * TT, 2):
                act.wait_ge(*full(f"x{n}"))
                nc.scalar.copy(xT[:, 4:8, P * (n // 2):P * (n // 2 + 1)],
                               bank(f"x{n}", 0, 512).rearrange("p (k t) -> p k t", k=4)
                               ).then_inc(*empties(f"x{n}"))

            def norm(i, dst):
                lay, second = i // 2, i % 2
                for k in range(KD):
                    if k >= 2:
                        act.wait_ge(nsq_used, (KD - 1) * i + k - 1)
                    if i == 0 and k == 0:
                        act.wait_ge(*taken("x8"))
                        act.wait_ge(*taken("x9"))
                    if i == 1:
                        act.wait_ge(*taken(f"woc{k}"))
                    if i == 2 and k == 0:
                        act.wait_ge(*taken("L0zCc1"))
                    if i == 3:
                        act.wait_ge(*taken(f"pc{k}"))
                    nc.scalar.activation(sq[:, k % 2, :], xT[:, k, :], ACT.Square).then_inc(nsq_ready, 1)
                act.wait_ge(*full(f"ssl{i}"))
                if i == 0:
                    act.wait_ge(consts_set, 2)
                nc.scalar.activation(rstd[:, 0:LAT], bank(f"ssl{i}", 0, LAT), ACT.Sqrt,
                                     bias=eps[:, :], scale=1.0 / D).then_inc(*empties(f"ssl{i}"))
                act.wait_ge(*full(f"ssc{i}"))
                nc.scalar.activation(rstd[:, LAT:T], bank(f"ssc{i}", 0, CTX), ACT.Sqrt,
                                     bias=eps[:, :], scale=1.0 / D).then_inc(*empties(f"ssc{i}"))
                sh = SH2 if second else SH1
                for k in range(KD):
                    act.wait_ge(nscaled, KD * i + k + 1)
                    lat, ctx_ = dst(k)
                    nc.scalar.activation(lat, lat, ACT.Identity, bias=mod[lay][:, sh + k, 0:1])
                    nc.scalar.activation(ctx_, ctx_, ACT.Identity,
                                         bias=mod[lay][:, sh + k, 1:2]).then_inc(h_ready, 1)

            norm(0, lambda k: (hA[:, k, 0:LAT], hA[:, k, LAT:T]))

            for n in range(len(HEADS) + 2):
                if n == 1:
                    for m in range(3):
                        name = f"v{m}"
                        act.wait_ge(*full(name))
                        if m < 2:
                            nc.scalar.copy(V[:, 2 * m:2 * m + 2, :],
                                           bank(name, 0, 512).rearrange("p (t c) -> p t c", t=2)
                                           ).then_inc(*empties(name))
                        else:
                            nc.scalar.copy(V[:, TT, :], bank(name, 0, NKV * HD)).then_inc(*empties(name))
                if 1 <= n <= len(HEADS):
                    m = n - 1
                    act.wait_ge(*full(f"hsl{m}"))
                    nc.scalar.activation(rrh[:, m % 2, 0:LAT], bank(f"hsl{m}", 0, LAT), ACT.Sqrt,
                                         bias=eps[:, :], scale=1.0 / HD).then_inc(*empties(f"hsl{m}"))
                    act.wait_ge(*full(f"hsc{m}"))
                    nc.scalar.activation(rrh[:, m % 2, LAT:T], bank(f"hsc{m}", 0, CTX), ACT.Sqrt,
                                         bias=eps[:, :], scale=1.0 / HD).then_inc(*empties(f"hsc{m}"))
                if n < len(HEADS):
                    act.wait_ge(raw_ready, n + 1)
                    nc.scalar.activation(sqh[:, n % 2, :], raw[:, n % 2, :], ACT.Square).then_inc(hsq_ready, 1)

            def expo(n):
                w = KEYS if n % TT < LT else CTX
                act.wait_ge(nmax_ready, n + 1)
                nc.scalar.activation(probs[:, n % 3, 0:w], bank(f"S{n}", 0, w), ACT.Exp,
                                     bias=stat[:, 4 + n % 4:5 + n % 4], scale=HD ** -0.5,
                                     accum_out=stat[:, 8 + n % 4:9 + n % 4]).then_inc(*empties(f"S{n}"))

            def keep_turned(n):
                act.wait_ge(*full(f"T{n}"))
                t = n % TT
                if t < LT:
                    nc.scalar.copy(pT[:, :, P * t:P * (t + 1)],
                                   bank(f"T{n}", 0, KEYS).rearrange("p (c q) -> p c q", q=P)
                                   ).then_inc(*empties(f"T{n}"))
                else:
                    nc.scalar.copy(pTc[:, :], bank(f"T{n}", 0, CTX)).then_inc(*empties(f"T{n}"))

            for n in range(NH * TT + 2):
                if n < NH * TT:
                    expo(n)
                if n >= 2:
                    keep_turned(n - 2)

            def round_unit(lay, m, i=0, looped=False):
                s, r = SPLITS * lay + m, base[lay] + m
                act.wait_ge(raw_full[r % RRING], 16 * (r // RRING + 1) + (16 * (UNITS // RRING) * i if looped else 0))
                if looped or s >= SRING:
                    act.wait_ge(split_used[s % SRING], s // SRING + (UNITS // SRING * i if looped else 0))
                nc.scalar.copy(split_w[s % SRING][:, 0, :, :], raw_w[r % RRING][:, :, :]).then_inc(rounded, 1)

            def keep_tokens(L, i=0):
                act.wait_ge(*full(L + "XEc", i))
                for e, dst in enumerate(xe_ctx(0)):
                    ins = nc.scalar.copy(dst, bank(L + "XEc", 0, KD * SEL_C)
                                         .rearrange("p (k e s) -> p k e s", e=2, k=KD)[:, :, e, :])
                ins.then_inc(xeh_ready, 1)
                for half in (1, 0):
                    nc.scalar.copy(xe_lat(0, half), bank(L + f"XE{half}", 0, 512)
                                   .rearrange("p (k e s) -> p e k s", e=2, k=4)).then_inc(xeh_ready, 1)

            def after_unit(lay, L, pair, m, i, last):
                e, j = m // (UNITS // 2), m % (UNITS // 2)
                if j in (1, 5):
                    name = L + f"G{e}{j // 5}"
                    act.wait_ge(*full(name, i))
                    nc.scalar.activation(hid[0:ROWS[e], j // 5, :], bank(name, 0, UC, ROWS[e]),
                                         ACT.Silu).then_inc(*empties(name))
                if m == 3:
                    act.wait_ge(*full(L + "PT", i))
                    nc.scalar.copy(put[:, :], bank(L + "PT", 0, LAT)).then_inc(*empties(L + "PT"))
                    act.wait_ge(*full(L + "PTc", i))
                    nc.scalar.copy(gates[:, :], bank(L + "PTc", CTX, CTX + 4))
                    nc.scalar.copy(put_c[:, :], bank(L + "PTc", 0, CTX)).then_inc(*empties(L + "PTc"))
                if j in (5, 8):
                    half = int(j == 8)
                    name = L + f"T{e}{half}"
                    act.wait_ge(*full(name, i))
                    nc.scalar.copy(hT[:, 0, 4 * half:4 * half + 4, 0:ROWS[e]], bank(name, 0, 4 * ROWS[e])
                                   .rearrange("p (k s) -> p k s", k=4)).then_inc(hTh_ready, 1)
                if m == 21 and not last:
                    keep_tokens(L, i)
                if j in (10, 11):
                    c = j - 10
                    name = L + f"D{e}{c}"
                    act.wait_ge(*full(name, i))
                    if j == 10 and e == 0:
                        act.wait_ge(*taken(L + "PTc", i))
                    for lo, hi, dst, g in out_rows(e):
                        ins = nc.scalar.activation(dst[lo:hi, 0, UC * c:UC * (c + 1)],
                                                   psum[lo:hi, 512 * use[name][0]:512 * use[name][0] + UC],
                                                   ACT.Copy, scale=gates[lo:hi, g:g + 1])
                    ins.then_inc(yeh_ready, 1)

            def experts(lay):
                for m in range(SRING):
                    round_unit(lay, m)
                keep_tokens(f"L{lay}g")
                with act.Fori(0, NP - 1) as i:
                    for m in range(UNITS):
                        after_unit(lay, f"L{lay}", i, m, i, False)
                        round_unit(lay, m + SRING, i, True)
                for m in range(UNITS):
                    after_unit(lay, f"L{lay}z", NP - 1, m, 0, True)
                    if m + SRING < UNITS:
                        round_unit(lay, SPLITS - UNITS + m + SRING)

            for lay in range(2):
                if lay == 1:
                    norm(2, lambda k: (Z[:, k, Z_L:Z_L + LAT], Z[:, k, Z_C:Z_C + CTX]))
                norm(2 * lay + 1, lambda k: (h2T[:, k, 0:LAT], h2T[:, k, LAT:T]))
                act.wait_ge(*taken(f"rt{lay}"))
                nc.scalar.activation(slot[:, :, :], aff[:, :, :], ACT.Exp).then_inc(aexp_ready, 1)
                for n in range(2 * TT):
                    name = f"ht{lay}_{n}"
                    act.wait_ge(*full(name))
                    nc.scalar.copy(h_rows[:, n // 2, 512 * (n % 2):512 * (n % 2 + 1)],
                                   bank(name, 0, 512)).then_inc(*empties(name))
                if lay == 0:
                    act.wait_ge(new_v_stored, 16)
                act.wait_ge(zeros_set, lay + 1)
                experts(lay)
            for n in range(1, 2 * TT, 2):
                act.wait_ge(*full(f"y{n}"))
                nc.scalar.copy(y_rows[:, n // 2, 512:1024], bank(f"y{n}", 0, 512)).then_inc(*empties(f"y{n}"))

        @block.vector
        def _(dve):
            dve_steps = [0]

            def own(ins):
                dve_steps[0] += 1
                ins.then_inc(dve_step, 1)
                dve.wait_ge(dve_step, dve_steps[0])

            nc.vector.memset(ones[:, :], 1.0).then_inc(consts_set, 1)
            nc.vector.memset(eps[:, :], EPS).then_inc(consts_set, 1)
            dve.wait_ge(*full("vec"))
            nc.vector.tensor_copy(vec[:, :], bank("vec", 0, V_ROWS)).then_inc(*empties("vec"))
            dve.wait_ge(*full("bada"))
            nc.vector.tensor_copy(bada[:, :], bank("bada", 0, 2 * MC)).then_inc(*empties("bada"))
            for n in range(0, 2 * TT, 2):
                dve.wait_ge(*full(f"x{n}"))
                nc.vector.tensor_copy(xT[:, 0:4, P * (n // 2):P * (n // 2 + 1)],
                                      bank(f"x{n}", 0, 512).rearrange("p (k t) -> p k t", k=4)
                                      ).then_inc(*empties(f"x{n}"))

            def take_mod(name, lay, c0, c1):
                dve.wait_ge(*full(name))
                if name == "ada0a":
                    dve.wait_ge(*taken("bada"))
                nc.vector.tensor_tensor(
                    mod[lay][:, c0:c1, :], bank(name, 2 * c0, 2 * c1).rearrange("p (c t) -> p c t", t=2),
                    bada[:, MC * lay + c0:MC * lay + c1].unsqueeze(2).to_broadcast([P, c1 - c0, 2]),
                    ALU.add).then_inc(*empties(name))
                dve.wait_ge(*taken(name))

            def set_amp(i):
                lay, second = i // 2, i % 2
                sc = SC2 if second else SC1
                g = (V_N2 if second else V_N1) + KD * lay
                own(nc.vector.scalar_tensor_tensor(
                    out=amp[i][:, :, :], in0=mod[lay][:, sc:sc + KD, :], scalar=1.0,
                    in1=vec[:, g:g + KD].unsqueeze(2).to_broadcast([P, KD, 2]), op0=ALU.add, op1=ALU.mult))

            def norm(i, dst):
                dve.wait_ge(*taken(f"ssl{i}"))
                dve.wait_ge(*taken(f"ssc{i}"))
                own(nc.vector.reciprocal(rstd[:, :], rstd[:, :]))
                for k in range(KD):
                    lat, ctx_ = dst(k)
                    nc.vector.scalar_tensor_tensor(out=lat, in0=xT[:, k, 0:LAT], scalar=amp[i][:, k, 0:1],
                                                   in1=rstd[:, 0:LAT], op0=ALU.mult, op1=ALU.mult)
                    nc.vector.scalar_tensor_tensor(out=ctx_, in0=xT[:, k, LAT:T], scalar=amp[i][:, k, 1:2],
                                                   in1=rstd[:, LAT:T], op0=ALU.mult, op1=ALU.mult
                                                   ).then_inc(nscaled, 1)

            take_mod("ada0a", 0, 0, G1)
            set_amp(0)
            dve.wait_ge(*taken("x9"))
            norm(0, lambda k: (hA[:, k, 0:LAT], hA[:, k, LAT:T]))

            def head_dst(n):
                kind, h = HEADS[n]
                return (kT[:, h, 0:LAT], kTc[:, h, :]) if kind == "k" else (qT[:, h, 0:LAT], qT[:, h, LAT:T])

            def take_head(n):
                dve.wait_ge(*full(f"hl{n}"))
                nc.vector.tensor_copy(raw[:, n % 2, 0:LAT], bank(f"hl{n}", 0, LAT)).then_inc(*empties(f"hl{n}"))
                dve.wait_ge(*full(f"hc{n}"))
                nc.vector.tensor_copy(raw[:, n % 2, LAT:T], bank(f"hc{n}", 0, CTX)).then_inc(*empties(f"hc{n}"))
                nc.vector.engine_nop().then_inc(raw_ready, 1)

            def norm_head(n):
                g = V_K if HEADS[n][0] == "k" else V_Q
                dve.wait_ge(*taken(f"hsl{n}"))
                dve.wait_ge(*taken(f"hsc{n}"))
                own(nc.vector.reciprocal(rrh[:, n % 2, :], rrh[:, n % 2, :]))
                nc.vector.scalar_tensor_tensor(out=raw[:, n % 2, 0:LAT], in0=raw[:, n % 2, 0:LAT],
                                               scalar=vec[:, g:g + 1], in1=rrh[:, n % 2, 0:LAT],
                                               op0=ALU.mult, op1=ALU.mult).then_inc(hnorm_ready, 1)
                nc.vector.scalar_tensor_tensor(out=head_dst(n)[1], in0=raw[:, n % 2, LAT:T],
                                               scalar=vec[:, g:g + 1], in1=rrh[:, n % 2, LAT:T],
                                               op0=ALU.mult, op1=ALU.mult)

            def finish_head(n):
                if n == 0:
                    dve.wait_ge(trig_loaded, 32)
                dst = head_dst(n)[0]
                dve.wait_ge(*full(f"rot{n}"))
                dve.wait_ge(hnorm_ready, n + 1)
                nc.vector.tensor_tensor(dst, raw[:, n % 2, 0:LAT], cos, ALU.mult)
                nc.vector.tensor_tensor(sqh[:, n % 2, 0:LAT], bank(f"rot{n}", 0, LAT), sin,
                                        ALU.mult).then_inc(*empties(f"rot{n}"))
                dve.wait_ge(*taken(f"rot{n}"))
                nc.vector.tensor_tensor(dst, dst, sqh[:, n % 2, 0:LAT], ALU.add).then_inc(head_ready, 1)

            for n in range(len(HEADS) + 2):
                if n == 8:
                    take_mod("ada0b", 0, G1, MC)
                    set_amp(1)
                if n >= 2:
                    finish_head(n - 2)
                if n < len(HEADS):
                    take_head(n)
                if 1 <= n <= len(HEADS):
                    norm_head(n - 1)

            dve.wait_ge(*full("cachek"))
            nc.vector.tensor_copy(kT[:, :, LAT:KEYS], bank("cachek", 0, NKV * HD)
                                  .rearrange("p (g t) -> p g t", g=NKV)).then_inc(*empties("cachek"))
            dve.wait_ge(*full("newk"))
            nc.vector.tensor_copy(new_k[:, :], bank("newk", 0, NKV * HD)).then_inc(*empties("newk"))

            def tile_max(n):
                w = KEYS if n % TT < LT else CTX
                dve.wait_ge(*full(f"S{n}"))
                own(nc.vector.tensor_reduce(stat[:, n % 4:n % 4 + 1], bank(f"S{n}", 0, w), AX.X, ALU.max))
                nc.vector.tensor_scalar(stat[:, 4 + n % 4:5 + n % 4], stat[:, n % 4:n % 4 + 1], -HD ** -0.5,
                                        None, ALU.mult).then_inc(nmax_ready, 1)

            def tile_probs(n):
                w = KEYS if n % TT < LT else CTX
                dve.wait_ge(*taken(f"S{n}"))
                own(nc.vector.reciprocal(stat[:, 12 + n % 4:13 + n % 4], stat[:, 8 + n % 4:9 + n % 4]))
                nc.vector.tensor_scalar(probs[:, n % 3, 0:w], probs[:, n % 3, 0:w],
                                        stat[:, 12 + n % 4:13 + n % 4], None, ALU.mult
                                        ).then_inc(probs_ready, 1)

            for n in range(NH * TT + 4):
                if n < NH * TT:
                    tile_max(n)
                if 1 <= n <= NH * TT:
                    tile_probs(n - 1)
                m = n - 4
                if m >= 0 and m % TT >= LT - 1:
                    lo, hi = (0, LAT) if m % TT == LT - 1 else (LAT, T)
                    dve.wait_ge(*full(f"O{m}"))
                    nc.vector.tensor_copy(oT[:, m // TT, lo:hi],
                                          bank(f"O{m}", 0, hi - lo)).then_inc(*empties(f"O{m}"))
            take_mod("ada1", 1, 0, MC)
            set_amp(2)
            set_amp(3)
            own(nc.vector.tensor_tensor(gate_pool[:, :, :], mod[1][:, G1:G1 + KD, :],
                                        vec[:, V_PS:V_PS + KD].unsqueeze(2).to_broadcast([P, KD, 2]), ALU.mult))

            def add_mixed(k, lat, ctx_, gate):
                dve.wait_ge(*full(lat))
                nc.vector.scalar_tensor_tensor(out=xT[:, k, 0:LAT], in0=bank(lat, 0, LAT), scalar=gate[:, k, 0:1],
                                               in1=xT[:, k, 0:LAT], op0=ALU.mult, op1=ALU.add
                                               ).then_inc(*empties(lat))
                dve.wait_ge(*full(ctx_))
                nc.vector.scalar_tensor_tensor(out=xT[:, k, LAT:T], in0=bank(ctx_, 0, CTX),
                                               scalar=gate[:, k, 1:2], in1=xT[:, k, LAT:T],
                                               op0=ALU.mult, op1=ALU.add).then_inc(*empties(ctx_))

            for k in range(KD):
                add_mixed(k, f"wol{k}", f"woc{k}", mod[0][:, G1:G1 + KD, :])

            def pool_windows():
                for lo, hi in ((0, Z_L), (Z_L + LAT, Z_C), (Z_C + CTX, ZW)):
                    nc.vector.memset(Z[:, :, lo:hi], 0.0)
                norm(2, lambda k: (Z[:, k, Z_L:Z_L + LAT], Z[:, k, Z_C:Z_C + CTX]))
                for g, w in enumerate(WINDOWS):
                    dve.wait_ge(h_ready, 2 * KD + 2 * g + 2)
                    if g > 0:
                        dve.wait_ge(pooled_ready, g)
                    z = Z[:, 2 * g:2 * g + 2, :]
                    src, lo, hi, reach = z, 1, ZW, 0
                    for s in range(g + 1):
                        dst = win[s % 2]
                        left, right = (1, 0) if s == 0 else (reach, reach)
                        own(nc.vector.tensor_tensor(dst[:, :, lo:hi], src[:, :, lo - left:hi - left],
                                                    src[:, :, lo + right:hi + right], ALU.add))
                        src, reach = dst, max(1, 2 * reach)
                        lo, hi = lo + reach, hi - reach
                    inv = T_INV + CTX * g
                    d = pooled[:, 2 * g:2 * g + 2, :]
                    half = CTX // 2
                    for at, n, tcol in ((Z_L, half, 0), (Z_L + LAT - half, half, half), (Z_C, CTX, 0)):
                        ins = nc.vector.tensor_tensor(
                            src[:, :, at:at + n], src[:, :, at:at + n],
                            tab[:, inv + tcol:inv + tcol + n].unsqueeze(1).to_broadcast([P, 2, n]), ALU.mult)
                    nc.vector.scalar_tensor_tensor(
                        out=d[:, :, half:LAT - half], in0=src[:, :, Z_L + half:Z_L + LAT - half], scalar=1.0 / w,
                        in1=z[:, :, Z_L + half:Z_L + LAT - half], op0=ALU.mult, op1=ALU.subtract)
                    own(ins)
                    for at, n, o in ((Z_L, half, 0), (Z_L + LAT - half, half, LAT - half), (Z_C, CTX, LAT)):
                        ins = nc.vector.tensor_tensor(d[:, :, o:o + n], src[:, :, at:at + n],
                                                      z[:, :, at:at + n], ALU.subtract)
                    ins.then_inc(pooled_ready, 1)

            def route(lay):
                logits = bank(f"rt{lay}", 0, TT * NE).rearrange("p (t e) -> p t e", e=NE)
                dve.wait_ge(*full(f"rt{lay}"))
                own(nc.vector.tensor_reduce(rmax[:, 0, :], logits, AX.X, ALU.max))
                nc.vector.tensor_tensor(aff[:, :, :], logits, rmax[:, 0, :].unsqueeze(2).to_broadcast([P, TT, NE]),
                                        ALU.subtract).then_inc(*empties(f"rt{lay}"))
                dve.wait_ge(aexp_ready, lay + 1)
                own(nc.vector.tensor_reduce(rmax[:, 1, :], slot[:, :, :], AX.X, ALU.add))
                own(nc.vector.reciprocal(rmax[:, 2, :], rmax[:, 1, :]))
                nc.vector.tensor_tensor(aff[:, :, :], slot[:, :, :],
                                        rmax[:, 2, :].unsqueeze(2).to_broadcast([P, TT, NE]),
                                        ALU.mult).then_inc(aff_ready, 1)
                dve.wait_ge(*full(f"afl{lay}"))
                nc.vector.tensor_copy(work[0:NE, 0:LAT], bank(f"afl{lay}", 0, LAT, NE)).then_inc(*empties(f"afl{lay}"))
                dve.wait_ge(*full(f"afc{lay}"))
                nc.vector.tensor_copy(work[0:NE, LAT:T], bank(f"afc{lay}", 0, CTX, NE)).then_inc(*empties(f"afc{lay}"))
                dve.wait_ge(*taken(f"afl{lay}"))
                dve.wait_ge(*taken(f"afc{lay}"))
                for lo, hi, cap in ((0, LAT, CAP_L), (LAT, T, CAP_C)):
                    for _ in range(cap // 8):
                        own(nc.vector.max(top8[0:NE, :], work[0:NE, lo:hi]))
                        own(nc.vector.match_replace(work[0:NE, lo:hi], top8[0:NE, :], work[0:NE, lo:hi], -1.0))
                own(nc.vector.tensor_scalar(mask[0:NE, :], work[0:NE, :], 0.0, None, ALU.is_lt))
                for lo, hi in ((0, LAT), (LAT, T)):
                    own(nc.vector.tensor_tensor_scan(cum[0:NE, lo:hi], mask[0:NE, lo:hi], mask[0:NE, lo:hi],
                                                     0.0, ALU.add, ALU.max))
                nc.vector.tensor_tensor(cum[0:NE, :], cum[0:NE, :], mask[0:NE, :], ALU.mult).then_inc(slots_ready, 1)
                dve.wait_ge(*full(f"sl{lay}"))
                nc.vector.tensor_copy(slot[:, :, :], bank(f"sl{lay}", 0, TT * NE)
                                      .rearrange("p (t e) -> p t e", e=NE)).then_inc(*empties(f"sl{lay}"))
                dve.wait_ge(*taken(f"sl{lay}"))

            def set_picks(pair):
                es = bass.ds(2 * pair, 2)
                iota = tab[:, T_IOTA:T_IOTA + CAP_L]
                nc.vector.tensor_tensor(
                    pick[:, :, :, :], slot[:, 0:LT, es].unsqueeze(3).to_broadcast([P, LT, 2, CAP_L]),
                    iota.unsqueeze(1).unsqueeze(1).to_broadcast([P, LT, 2, CAP_L]),
                    ALU.is_equal).then_inc(pick_ready, 1)
                nc.vector.tensor_tensor(
                    pick_c[:, :, :], slot[:, LT, es].unsqueeze(2).to_broadcast([P, 2, CAP_C]),
                    iota[:, 0:CAP_C].unsqueeze(1).to_broadcast([P, 2, CAP_C]),
                    ALU.is_equal).then_inc(pick_ready, 1)
                for e in range(2):
                    ins = nc.vector.tensor_tensor(
                        pick_w[:, 1 - e, 0:CAP_C], slot[:, LT, bass.ds(2 * pair + e, 1)].to_broadcast([P, CAP_C]),
                        iota[:, 0:CAP_C], ALU.is_equal)
                ins.then_inc(pick_ready, 1)

            def low_unit(lay, m, i=0, looped=False):
                s, r = SPLITS * lay + m, base[lay] + m
                if m % 4 == 3:
                    return
                dve.wait_ge(rounded, s + 1 + (UNITS * i if looped else 0))
                w = split_w[s % SRING]
                nc.vector.tensor_tensor(w[:, 1, :, :], raw_w[r % RRING][:, :, :], w[:, 0, :, :].bitcast(F32),
                                        ALU.subtract).then_inc(raw_used[r % RRING], 1)

            def keep_tokens(L, n, i=0):
                dve.wait_ge(xeh_ready, n + 1)
                for e, (dst, high) in enumerate(zip(xe_ctx(1), xe_ctx(0))):
                    ins = nc.vector.tensor_tensor(dst, bank(L + "XEc", 0, KD * SEL_C)
                                                  .rearrange("p (k e s) -> p k e s", e=2, k=KD)[:, :, e, :],
                                                  high.bitcast(F32), ALU.subtract)
                ins.then_inc(*empties(L + "XEc"))
                for j, half in enumerate((1, 0)):
                    dve.wait_ge(xeh_ready, n + 2 + j)
                    name = L + f"XE{half}"
                    nc.vector.tensor_tensor(xe_lat(1, half), bank(name, 0, 512)
                                            .rearrange("p (k e s) -> p e k s", e=2, k=4),
                                            xe_lat(0, half).bitcast(F32), ALU.subtract).then_inc(*empties(name))

            def after_unit(lay, L, pair, m, i, last):
                e, j = m // (UNITS // 2), m % (UNITS // 2)
                gp = NP * lay + pair
                if j in (3, 7):
                    half = j // 7
                    name = L + f"U{e}{half}"
                    dve.wait_ge(*full(name, i))
                    dve.wait_ge(*taken(L + f"G{e}{half}", i))
                    h = hid[0:ROWS[e], half, :]
                    nc.vector.tensor_tensor(h, bank(name, 0, UC, ROWS[e]), h, ALU.mult).then_inc(*empties(name))
                if j in (5, 8):
                    half = int(j == 8)
                    name = L + f"T{e}{half}"
                    dve.wait_ge(hTh_ready, 4 * gp + 2 * e + half + 1)
                    nc.vector.tensor_tensor(hT[:, 1, 4 * half:4 * half + 4, 0:ROWS[e]],
                                            bank(name, 0, 4 * ROWS[e]).rearrange("p (k s) -> p k s", k=4),
                                            hT[:, 0, 4 * half:4 * half + 4, 0:ROWS[e]].bitcast(F32),
                                            ALU.subtract).then_inc(*empties(name))
                if m == 9 and not last:
                    dve.wait_ge(*full(L + "PTc", i))
                    set_picks(pair + 1)
                if m == 21 and not last:
                    keep_tokens(L, 3 * gp + 3, i)
                if j in (10, 11):
                    c = j - 10
                    name = L + f"D{e}{c}"
                    dve.wait_ge(yeh_ready, 4 * gp + 2 * e + c + 1)
                    for lo, hi, dst, g in out_rows(e):
                        ins = nc.vector.scalar_tensor_tensor(
                            out=dst[lo:hi, 1, UC * c:UC * (c + 1)],
                            in0=psum[lo:hi, 512 * use[name][0]:512 * use[name][0] + UC],
                            scalar=gates[lo:hi, g:g + 1], in1=dst[lo:hi, 0, UC * c:UC * (c + 1)].bitcast(F32),
                            op0=ALU.mult, op1=ALU.subtract)
                    ins.then_inc(*empties(name))

            def add_outputs(lay, L, i=0):
                for d in range(KD):
                    name = L + f"C{d}"
                    dve.wait_ge(*full(name, i))
                    nc.vector.scalar_tensor_tensor(
                        out=xT[:, d, 0:LAT], in0=bank(name, 0, LAT), scalar=mod[lay][:, G2 + d, 0:1],
                        in1=xT[:, d, 0:LAT], op0=ALU.mult, op1=ALU.add).then_inc(*empties(name))
                for half in range(2):
                    name = L + f"Cc{half}"
                    dve.wait_ge(*full(name, i))
                    for k in range(4):
                        d = 4 * half + k
                        ins = nc.vector.scalar_tensor_tensor(
                            out=xT[:, d, LAT:T], in0=bank(name, P * k, P * (k + 1)),
                            scalar=mod[lay][:, G2 + d, 1:2], in1=xT[:, d, LAT:T], op0=ALU.mult, op1=ALU.add)
                    ins.then_inc(*empties(name))

            def experts(lay):
                nc.vector.memset(pick_w[:, :, :], 0.0)
                nc.vector.memset(xe[:, :, :].bitcast(F32), 0.0)
                own(nc.vector.memset(ye_c[:, :, :].bitcast(F32), 0.0))
                nc.vector.engine_nop().then_inc(zeros_set, 1)
                set_picks(0)
                for m in range(SRING):
                    low_unit(lay, m)
                keep_tokens(f"L{lay}g", 3 * NP * lay)
                with dve.Fori(0, NP - 1) as i:
                    for m in range(UNITS):
                        after_unit(lay, f"L{lay}", i, m, i, False)
                        if m < UNITS - 1:
                            low_unit(lay, m + SRING, i, True)
                    add_outputs(lay, f"L{lay}", i)
                    low_unit(lay, UNITS - 1 + SRING, i, True)
                for m in range(UNITS):
                    after_unit(lay, f"L{lay}z", NP - 1, m, 0, True)
                    if m + SRING < UNITS:
                        low_unit(lay, SPLITS - UNITS + m + SRING)
                add_outputs(lay, f"L{lay}z")

            for lay in range(2):
                if lay == 1:
                    pool_windows()
                    for k in range(KD):
                        add_mixed(k, f"pl{k}", f"pc{k}", gate_pool)
                norm(2 * lay + 1, lambda k: (h2T[:, k, 0:LAT], h2T[:, k, LAT:T]))
                route(lay)
                if lay == 0:
                    dve.wait_ge(new_v_stored, 16)
                experts(lay)
            for n in range(0, 2 * TT, 2):
                dve.wait_ge(*full(f"y{n}"))
                nc.vector.tensor_copy(y_rows[:, n // 2, 0:512], bank(f"y{n}", 0, 512)).then_inc(*empties(f"y{n}"))


_INS = ["x_prompt", "x_sample", "cache_k", "cache_v", "c", "c_ctx", "norm1", "norm2", "w_ada", "b_ada",
        "w_qkv", "q_norm", "k_norm", "w_o", "w_pool", "pool_scale", "w_router", "w_e_gate", "w_e_up", "w_e_down"]
_OUTS = {"y_prompt": (1, CTX, D), "y_sample": (1, LAT, D), "new_k": (1, 1, CTX, NKV, HD),
         "new_v": (1, 1, CTX, NKV, HD)}


def kernel(**inputs):
    import concourse.bacc as _bacc
    from concourse.bass_utils import run_bass_kernel_spmd as _run

    nc = _bacc.Bacc("TRN2", target_bir_lowering=False, num_devices=1)
    arrays, ins = {}, {}
    for name in _INS:
        arrays[f"in_{name}"] = np.ascontiguousarray(inputs[name])
    arrays["in_tables"] = shape_tables()
    for name, v in arrays.items():
        ins[name[3:]] = nc.dram_tensor(name, v.shape, mybir.dt.from_np(v.dtype), kind="ExternalInput").ap()
    outs = {name: nc.dram_tensor(f"out_{name}", shape, F32, kind="ExternalOutput").ap()
            for name, shape in _OUTS.items()}
    build(nc, ins, outs)
    r = _run(nc, [arrays], core_ids=[0])
    return tuple(r.results[0][f"out_{name}"] for name in _OUTS)
```

```python
from contextlib import ExitStack

import numpy as np

import concourse.bass as bass
from concourse import mybir

F32 = mybir.dt.float32
F32R = mybir.dt.float32r
ALU = mybir.AluOpType
ACT = mybir.ActivationFunctionType
AX = mybir.AxisListType

P = 128
D = 1024
KD = D // P
LAT, CTX = 512, 128
T = LAT + CTX
TT = T // P
LT = LAT // P
PAST = 128
GRID_W = 64
HD = 128
NH, NKV = D // HD, D // HD // 4
G = NH // NKV
KEYS = LAT + PAST
NE = 16
CAP_L, CAP_C = 2 * LAT // NE, 2 * CTX // NE
CAP = CAP_L + CAP_C
NP = NE // 2
SEL_L, SEL_C = 2 * CAP_L, 2 * CAP_C
NMOD = 6
MC = NMOD * KD
EPS = 1e-6
THETA = 10000.0
WINDOWS = (2, 4, 8, 16)
PADZ = 8
Z_L, Z_C = PADZ, PADZ + LAT + 2 * PADZ
ZW = Z_C + CTX + PADZ
UC = 512
KH = KD // 2
FRING = 8
ADA_UNITS = NMOD * D // UC
RRING, SRING = 4, 4
ROWS = (CAP, P)
SH1, SC1, G1, SH2, SC2, G2 = (KD * m for m in range(NMOD))

V_C, V_CTX, V_N1, V_N2, V_PS, V_Q, V_K, V_ROWS = 0, 8, 16, 32, 48, 56, 57, 58
T_ID, T_SWAP, T_IOTA, T_INV, T_COS, T_SIN, T_COLS = 0, 128, 256, 320, 832, 1344, 1856


def shape_tables():
    f = np.float32
    tab = np.zeros((P, T_COLS), f)
    tab[:, T_ID:T_ID + P] = np.eye(P, dtype=f)
    p = np.arange(P)
    tab[p ^ 32, T_SWAP + p] = 1.0
    tab[:, T_IOTA:T_IOTA + CAP_L] = np.arange(1, CAP_L + 1, dtype=f)
    t = np.arange(CTX)
    for g, w in enumerate(WINDOWS):
        n = np.clip(t + w - w // 2, 0, CTX) - np.clip(t - w // 2, 0, CTX)
        tab[:, T_INV + CTX * g:T_INV + CTX * (g + 1)] = f(1) / n.astype(f)
    n = HD // 4
    inv_freq = np.power(f(THETA), -np.arange(n, dtype=f) / f(n)).astype(f)
    tok = np.arange(LAT)
    pos = np.stack([tok // GRID_W, tok % GRID_W]).astype(f)
    ang = pos[p // (2 * n)] * inv_freq[p % n][:, None]
    sign = np.where(p % (2 * n) < n, f(-1), f(1))[:, None]
    tab[:, T_COS:T_COS + LAT] = np.cos(ang)
    tab[:, T_SIN:T_SIN + LAT] = np.sin(ang) * sign
    return tab


def weight_order():
    u = [("ada0", n) for n in range(6)] + [("qkv", 2), ("qkv", 0)]
    u += [("ada0", n) for n in range(6, 9)] + [("qkv", 1)]
    u += [("ada0", n) for n in range(9, 12)] + [("ada1", n) for n in range(12)] + [("wo", 0), ("wo", 1)]
    return u


class PsumUses:

    def __init__(self):
        self.opened, self.filled = [0] * 8, [0] * 8
        self.at = {}

    def take(self, name, bank, unit=None):
        self.at[name] = (bank, self.opened[bank], 0, self.filled[bank], 0, unit, 0)
        self.opened[bank] += 1
        self.filled[bank] += unit is None

    def loop(self, prefix, uses, trips, base):
        opens = [sum(b == bank for _, b, _ in uses) for bank in range(8)]
        fills = [sum(b == bank and u is None for _, b, u in uses) for bank in range(8)]
        o, f = list(self.opened), list(self.filled)
        for name, b, u in uses:
            unit = None if u is None else ("split", base + u)
            self.at[prefix + name] = (b, o[b], opens[b], f[b], fills[b], unit, UNITS // SRING)
            o[b] += 1
            f[b] += u is None
        self.opened = [c + trips * n for c, n in zip(self.opened, opens)]
        self.filled = [c + trips * n for c, n in zip(self.filled, fills)]


HEADS = [("k", 0), ("k", 1)] + [("q", h) for h in range(NH)]
ADA_AFTER_HEAD = {2: (0, 6), 3: (0, 7), 4: (0, 8), 7: (0, 9), 8: (0, 10), 10: (0, 11)}
TURN_AFTER_HEAD = {1: (0, 5), **{n + 1: unit for n, unit in ADA_AFTER_HEAD.items()}}
ADA_AHEAD = 0
EXPERT_UNITS = ([(w, c, r) for c in range(2) for w in "gu" for r in range(2)]
                + [("d", c, r) for r in range(2) for c in range(2)])
UNITS = 2 * len(EXPERT_UNITS)
GATHER_USES = [("XE0", 0, None), ("XE1", 1, None), ("XEc", 2, None)]


SPLITS = UNITS * NP
POOL_UNIT = SPLITS


def pair_uses(gather):
    uses = []
    for e in range(2):
        n = UNITS // 2 * e
        uses += [(f"G{e}0", 0, n + 1), (f"U{e}0", 1, n + 3)]
        if e == 0:
            uses += [("PT", 6, None), ("PTc", 7, None)]
        uses += [(f"G{e}1", 2, n + 5), (f"T{e}0", 4, None), (f"U{e}1", 3, n + 7)]
        uses += [(f"D{e}0", 5, n + 10), (f"T{e}1", 7, None), (f"D{e}1", 6, n + 11)]
    uses += GATHER_USES if gather else []
    uses += [(f"C{d}", b, None) for d, b in enumerate((4, 7, 3, 1, 2, 4, 7, 3))]
    return uses + [("Cc0", 5, None), ("Cc1", 6, None)]


def plan_psum(unit_of, base):
    u = PsumUses()

    def last_of(kind, n):
        return "front", unit_of[(kind, n)] + 1

    u.take("vec", 7)
    u.take("bada", 6)
    for n in range(2 * TT):
        u.take(f"x{n}", n % 6)

    def norm(i):
        u.take(f"ssl{i}", 0)
        u.take(f"ssc{i}", 1)

    norm(0)
    for lay in range(2):
        for n in range(NMOD * D // UC):
            u.take(f"row{lay}_{n}", 7, ("ada", 2 * (ADA_UNITS * lay + n) + 1))
            if lay == 1:
                u.take(f"col1_{n}", 7)
    for n in range(5):
        u.take(f"col0_{n}", 5)
    for n in range(len(HEADS) + 2):
        if n < len(HEADS):
            u.take(f"hl{n}", 2 * (n % 2))
            last = {5: ("qkv", 0), 9: ("qkv", 1)}.get(n)
            u.take(f"hc{n}", 2 * (n % 2) + 1, last_of(*last) if last else None)
        if n == 1:
            for m, b in enumerate((6, 0, 6)):
                u.take(f"v{m}", b, last_of("qkv", 2) if m == 2 else None)
        if 1 <= n <= len(HEADS):
            u.take(f"hsl{n - 1}", 4)
            u.take(f"hsc{n - 1}", 5)
        if n in TURN_AFTER_HEAD and TURN_AFTER_HEAD[n][0] == 0:
            u.take(f"col0_{TURN_AFTER_HEAD[n][1]}", 5)
        if n >= 2:
            u.take(f"rot{n - 2}", 6)
    u.take("cachek", 5)
    u.take("newk", 4)
    for n in range(NH * TT + 3):
        if n < NH * TT:
            u.take(f"S{n}", 2 * (n % 2))
        if 2 <= n < NH * TT + 2:
            u.take(f"T{n - 2}", 4)
        if n >= 3 and (n - 3) % TT >= TT - 2:
            u.take(f"O{n - 3}", 6)
    for d in range(KD):
        u.take(f"wol{d}", 2 * (d % 2))
        u.take(f"woc{d}", 2 * (d % 2) + 1, last_of("wo", d // 4) if d % 4 == 3 else None)
    for lay in range(2):
        if lay == 1:
            norm(2)
            for d in range(KD):
                u.take(f"pl{d}", 2 * (d % 2))
                u.take(f"pc{d}", 2 * (d % 2) + 1, ("raw", POOL_UNIT) if d == KD - 1 else None)
        norm(2 * lay + 1)
        u.take(f"rl{lay}", 6)
        u.take(f"rc{lay}", 7)
        u.take(f"rt{lay}", 2)
        for n in range(2 * TT):
            u.take(f"ht{lay}_{n}", 3 + n % 3)
        u.take(f"afl{lay}", 6)
        u.take(f"afc{lay}", 7)
        u.take(f"sl{lay}", 2)
        for name, b, _ in GATHER_USES:
            u.take(f"L{lay}g{name}", b)
        u.loop(f"L{lay}", pair_uses(True), NP - 1, SPLITS * lay)
        for name, b, n in pair_uses(False):
            u.take(f"L{lay}z{name}", b, None if n is None else ("split", SPLITS * (lay + 1) - UNITS + n))
    for n in range(2 * TT):
        u.take(f"y{n}", n % 8)
    return u.at


def build(nc, a, out):
    front = weight_order()
    unit_of = {u: 2 * n for n, u in enumerate(front)}
    base = {0: 0, 1: POOL_UNIT + 1}
    use = plan_psum(unit_of, base)

    with ExitStack() as ctx:
        def sb(name, *shape):
            return ctx.enter_context(nc.sbuf_tensor(name, [P, *shape], F32))

        def sem(name):
            return ctx.enter_context(nc.semaphore(name))

        xT = sb("xT", KD, T)
        bufH = sb("bufH", KD * ZW)
        tab = sb("tab", T_COS)
        vec_rows = sb("vec_rows", P)
        bada_rows = sb("bada_rows", P)
        vec = sb("vec", V_ROWS)
        bada = sb("bada", 2 * MC)
        cond = sb("cond", KD, 2)
        cond_parts = ctx.enter_context(nc.sbuf_tensor("cond_parts", [P, KD, 4], F32R))
        add_parts = sb("add_parts", 2)
        mod = [sb(f"mod{i}", MC, 2) for i in range(2)]
        amp = [sb(f"amp{i}", KD, 2) for i in range(4)]
        gate_pool = sb("gate_pool", KD, 2)
        wr = sb("wr", 2, KD, NE)
        ones = sb("ones", P)
        eps = sb("eps", 1)
        new_k = sb("new_k", NKV * HD)
        stat = sb("stat", 16)
        ada_row = sb("ada_row", 2, UC)
        rmax = sb("rmax", 3, TT)
        aff = sb("aff", TT, NE)
        slot = sb("slot", TT, NE)
        top8 = sb("top8", 8)

        free = [-(-nc.sbuf_base // 64) * 64]

        def place(name, at, *shape, dtype=F32):
            return nc.alloc_sbuf_tensor_at(name, [P, *shape], dtype, offset=at), at + 4 * int(np.prod(shape))

        slots_at = free[0]
        unit_bytes = 4 * KH * UC
        fring = [place(f"front{n}", slots_at + unit_bytes * n, KH, UC)[0] for n in range(FRING)]
        raw_w = [place(f"raw_w{n}", slots_at + unit_bytes * n, KH, UC)[0] for n in range(RRING)]
        split_w = [place(f"split_w{n}", slots_at + unit_bytes * (RRING + 2 * n), 2, KH, UC, dtype=F32R)[0]
                   for n in range(SRING)]
        ada_w = split_w[2:4]
        shared_at = slots_at + unit_bytes * (RRING + 2 * SRING)
        bufQ, at = place("bufQ", shared_at, KD * T)
        bufS, at = place("bufS", at, 8704)
        xe, at = place("xe", shared_at, 2, 2 * KD * P + P, dtype=F32R)
        hT, at = place("hT", at, 2, KD, P, dtype=F32R)
        ye, at = place("ye", at, 2, D, dtype=F32R)
        ye_c, at = place("ye_c", at, 2, D, dtype=F32R)
        put, at = place("put", at, LAT, dtype=F32R)
        put_c, at = place("put_c", at, CTX, dtype=F32R)
        hid, at = place("hid", at, 2, UC)
        pick, at = place("pick", at, LT, 2, CAP_L)
        pick_c, at = place("pick_c", at, 2, CAP_C)
        pick_w, at = place("pick_w", at, 2, CAP_L)
        gates, at = place("gates", at, 4)

        ident, swap = tab[:, T_ID:T_ID + P], tab[:, T_SWAP:T_SWAP + P]

        def view(buf, at, *shape):
            n = int(np.prod(shape))
            v = buf[:, at:at + n]
            names = "abcd"[:len(shape)]
            if len(shape) == 1:
                return v
            return v.rearrange(f"p ({' '.join(names)}) -> p {' '.join(names)}",
                               **{k: s for k, s in zip(names, shape)})

        x_rows = view(bufH, 0, TT, D)
        hA = view(bufH, 0, KD, T)
        oT = hA
        h_rows = x_rows
        y_rows = x_rows
        Z = view(bufH, 0, KD, ZW)
        qT = view(bufQ, 0, NH, T)
        h2T = view(bufQ, 0, KD, T)
        pooled = view(bufQ, 0, KD, T)
        V = view(bufS, 0, TT + 1, NKV * HD)
        kT = view(bufS, 1536, NKV, KEYS)
        kTc = view(bufS, 2816, NKV, CTX)
        cos, sin = view(bufS, 3072, LAT), view(bufS, 3584, LAT)
        raw = view(bufS, 4096, 2, T)
        sqh = view(bufS, 5376, 2, T)
        rrh = view(bufS, 6656, 2, T)
        cache_rows = view(bufS, 7936, NKV * HD)
        probs = view(bufS, 4096, 3, KEYS)
        pT = view(bufS, 6016, TT, LAT)
        pTc = view(bufS, 8576, CTX)
        sq = view(bufS, 4096, 2, T)
        rstd = view(bufS, 5376, T)
        win = [view(bufS, n * 2 * ZW, 2, ZW) for n in range(2)]
        work = view(bufS, 6016, T)
        mask = view(bufS, 6656, T)
        cum = view(bufS, 7296, T)
        zeros = view(bufS, 7936, T)
        psum = ctx.enter_context(nc.psum_tensor("psum", [P, 8 * 512], F32))

        def bank(name, lo, hi, rows=P):
            b = use[name][0]
            return psum[0:rows, 512 * b + lo:512 * b + hi]

        def xe_lat(part, half):
            v = xe[:, part, 0:2 * (KD * P + CAP_L)].rearrange("p (e x) -> p e x", e=2)
            return v[:, :, 4 * P * half:4 * P * (half + 1)].rearrange("p e (k c) -> p e k c", c=P)[:, :, :, 0:CAP_L]

        def xe_ctx(part):
            full_rows = xe[:, part, :]
            return [full_rows[:, CAP_L:CAP_L + KD * P].rearrange("p (k c) -> p k c", c=P)[:, :, 0:CAP_C],
                    full_rows[:, KD * P:2 * KD * P].rearrange("p (k c) -> p k c", c=P)[:, :, 0:CAP_C]]

        def out_rows(e):
            if e == 0:
                return ((0, CAP_L, ye, 0), (CAP_L, CAP, ye_c, 2))
            return ((CAP_L, P, ye, 1), (0, CAP_C, ye_c, 3))

        x_loaded = [sem(f"x_loaded{t}") for t in range(TT)]
        ident_loaded = sem("ident_loaded")
        tab_loaded = sem("tab_loaded")
        trig_loaded = sem("trig_loaded")
        vec_loaded = sem("vec_loaded")
        bada_loaded = sem("bada_loaded")
        wr_loaded = sem("wr_loaded")
        cache_loaded = sem("cache_loaded")
        front_full = [sem(f"front_full{n}") for n in range(FRING)]
        front_used = [sem(f"front_used{n}") for n in range(FRING)]
        raw_full = [sem(f"raw_full{n}") for n in range(RRING)]
        raw_used = [sem(f"raw_used{n}") for n in range(RRING)]
        split_used = [sem(f"split_used{n}") for n in range(SRING)]
        ada_rounded = sem("ada_rounded")
        ada_used = [sem(f"ada_used{r}") for r in range(2)]
        rounded = sem("rounded")
        xeh_ready = sem("xeh_ready")
        zeros_set = sem("zeros_set")
        out_zeros_set = sem("out_zeros_set")
        hTh_ready = sem("hTh_ready")
        yeh_ready = sem("yeh_ready")
        bank_full = [sem(f"bank_full{b}") for b in range(8)]
        bank_empty = [sem(f"bank_empty{b}") for b in range(8)]
        dve_step = sem("dve_step")
        consts_set = sem("consts_set")
        cond_ready = sem("cond_ready")
        nsq_ready = sem("nsq_ready")
        nsq_used = sem("nsq_used")
        nscaled = sem("nscaled")
        h_ready = sem("h_ready")
        raw_ready = sem("raw_ready")
        hsq_ready = sem("hsq_ready")
        hnorm_ready = sem("hnorm_ready")
        head_ready = sem("head_ready")
        nmax_ready = sem("nmax_ready")
        probs_ready = sem("probs_ready")
        pooled_ready = sem("pooled_ready")
        aexp_ready = sem("aexp_ready")
        aff_ready = sem("aff_ready")
        slots_ready = sem("slots_ready")
        pick_ready = sem("pick_ready")
        new_v_stored = sem("new_v_stored")
        new_k_stored = sem("new_k_stored")
        stored = sem("stored")

        def full(name, i=0):
            _, _, _, n, per, unit, per_unit = use[name]
            if unit is None:
                return bank_full[use[name][0]], n + 1 + (per * i if per else 0)
            kind, u = unit
            sems = {"front": front_used, "ada": ada_used, "raw": raw_used, "split": split_used}[kind]
            return sems[u % len(sems)], u // len(sems) + 1 + (per_unit * i if per_unit else 0)

        def empty(name, i=0):
            b, n, per = use[name][:3]
            return bank_empty[b], n + (per * i if per else 0)

        def fills(name):
            return full(name)[0], 1

        def empties(name):
            return bank_empty[use[name][0]], 1

        def taken(name, i=0):
            s, v = empty(name, i)
            return s, v + 1

        def wait_empty(eng, name, i=0):
            s, v = empty(name, i)
            if not isinstance(v, int) or v > 0:
                eng.wait_ge(s, v)

        unit_cols = {
            "ada0": lambda n: a["w_ada"][0, :, UC * n:UC * (n + 1)],
            "ada1": lambda n: a["w_ada"][1, :, UC * n:UC * (n + 1)],
            "qkv": lambda n: a["w_qkv"][0, :, UC * n:UC * (n + 1)],
            "wo": lambda n: a["w_o"][0, :, UC * n:UC * (n + 1)],
        }

        block = ctx.enter_context(nc.Block())

        @block.sync
        def _(sp):
            for t in range(TT):
                src = a["x_sample"][0, P * t:P * (t + 1), :] if t < LT else a["x_prompt"][0, :, :]
                sp.dma_start(x_rows[:, t, :], src).then_inc(x_loaded[t], 16)
            sp.wait_ge(vec_loaded, 16 * 7)
            sp.wait_ge(bada_loaded, 16)
            for n, (kind, m) in enumerate(front):
                for r in range(2):
                    u = 2 * n + r
                    if u >= FRING:
                        sp.wait_ge(front_used[u % FRING], u // FRING)
                    sp.dma_start(fring[u % FRING][:, :, :],
                                 unit_cols[kind](m)[P * KH * r:P * KH * (r + 1), :]
                                 .rearrange("(k p) n -> p k n", p=P)).then_inc(front_full[u % FRING], 16)

            def expert_units(lay, e0, first, i=0):
                for e in range(2):
                    for m, (w, c, r) in enumerate(EXPERT_UNITS):
                        u = base[lay] + UNITS // 2 * e + m + first
                        src = {"g": a["w_e_gate"], "u": a["w_e_up"], "d": a["w_e_down"]}[w]
                        if isinstance(i, int) and u < RRING:
                            last = (2 * len(front) - 1 - u) // FRING * FRING + u
                            sp.wait_ge(front_used[u], last // FRING + 1)
                        else:
                            sp.wait_ge(raw_used[u % RRING], u // RRING + (0 if isinstance(i, int) else UNITS // RRING * i))
                        sp.dma_start(raw_w[u % RRING][:, :, :],
                                     src[lay, bass.ds(e0 + e, 1), P * KH * r:P * KH * (r + 1), UC * c:UC * (c + 1)]
                                     .rearrange("e (k p) n -> p (e k) n", p=P)
                                     ).then_inc(raw_full[u % RRING], 16)

            for lay in range(2):
                expert_units(lay, 0, 0)
                with sp.Fori(0, NP - 1) as i:
                    expert_units(lay, 2 * i + 2, UNITS, i)
                if lay == 0:
                    sp.wait_ge(raw_used[POOL_UNIT % RRING], POOL_UNIT // RRING)
                    sp.dma_start(raw_w[POOL_UNIT % RRING][:, :, :].rearrange("p k (h n) -> p (k h) n", h=2),
                                 a["w_pool"][0].rearrange("g (c p) n -> p (g c) n", p=P)
                                 ).then_inc(raw_full[POOL_UNIT % RRING], 16)
            for t in range(TT):
                sp.wait_ge(*taken(f"y{2 * t}"))
                sp.wait_ge(*taken(f"y{2 * t + 1}"))
                dst = out["y_sample"][0, P * t:P * (t + 1), :] if t < LT else out["y_prompt"][0, :, :]
                sp.dma_start(dst, y_rows[:, t, :]).then_inc(stored, 16)
            sp.wait_ge(stored, 16 * TT)

        @block.gpsimd
        def _(pool):
            def low_ada(idx):
                u = unit_of[(f"ada{idx // ADA_UNITS}", idx % ADA_UNITS)]
                for r in range(2):
                    pool.wait_ge(ada_rounded, 2 * idx + r + 1)
                    nc.gpsimd.tensor_tensor(ada_w[r][:, 1, :, :], fring[(u + r) % FRING][:, :, :],
                                            ada_w[r][:, 0, :, :].bitcast(F32),
                                            ALU.subtract).then_inc(front_used[(u + r) % FRING], 1)

            low_ada(4)
            low_ada(5)
            pool.wait_ge(*taken("v2"))
            pool.dma_start(out["new_v"][0, 0].rearrange("t h d -> t (h d)"),
                           V[:, TT, :]).then_inc(new_v_stored, 16)
            for idx in range(6, 2 * ADA_UNITS):
                low_ada(idx)
            pool.wait_ge(*taken("newk"))
            pool.dma_start(out["new_k"][0, 0].rearrange("t h d -> t (h d)"),
                           new_k[:, :]).then_inc(new_k_stored, 16)

            def low_unit(lay, m, i=0, looped=False):
                s, r = SPLITS * lay + m, base[lay] + m
                pool.wait_ge(rounded, s + 1 + (UNITS * i if looped else 0))
                w = split_w[s % SRING]
                nc.gpsimd.tensor_tensor(w[:, 1, :, :], raw_w[r % RRING][:, :, :], w[:, 0, :, :].bitcast(F32),
                                        ALU.subtract).then_inc(raw_used[r % RRING], 1)

            for lay in range(2):
                for m in range(3):
                    low_unit(lay, m)
                pool.wait_ge(*taken(f"sl{lay}"))
                nc.gpsimd.memset(ye_c[:, :, :].bitcast(F32), 0.0).then_inc(out_zeros_set, 1)
                with pool.Fori(0, NP) as i:
                    for m in range(3, UNITS, 4):
                        low_unit(lay, m, i, True)
            pool.wait_ge(new_v_stored, 16)
            pool.wait_ge(new_k_stored, 16)

        @block.tensor
        def _(pe):
            def landed(kind, n, r):
                u = unit_of[(kind, n)] + r
                pe.wait_ge(front_full[u % FRING], 16 * (u // FRING + 1))

            def front_unit(kind, n, halves=(0, 1)):
                u = unit_of[(kind, n)]
                for r in halves:
                    landed(kind, n, r)
                return lambda k: fring[(u + k // KH) % FRING][:, k % KH, :]

            def first_half_used(kind, n):
                return front_used[unit_of[(kind, n)] % FRING], 1

            pe.wait_ge(ident_loaded, 16)
            pe.wait_ge(vec_loaded, 16 * 7)
            pe.transpose(bank("vec", 0, V_ROWS), vec_rows[0:V_ROWS, :],
                         ident[0:V_ROWS, 0:V_ROWS]).then_inc(*fills("vec"))
            pe.wait_ge(bada_loaded, 16)
            pe.transpose(bank("bada", 0, 2 * MC), bada_rows[0:2 * MC, :],
                         ident[0:2 * MC, 0:2 * MC]).then_inc(*fills("bada"))
            for t in range(TT):
                pe.wait_ge(x_loaded[t], 16)
                for half in range(2):
                    name = f"x{2 * t + half}"
                    wait_empty(pe, name)
                    for k in range(4):
                        kk = 4 * half + k
                        mm = pe.transpose(bank(name, P * k, P * (k + 1)),
                                          x_rows[:, t, P * kk:P * (kk + 1)], ident)
                    mm.then_inc(*fills(name))

            def norm_stats(i):
                wait_empty(pe, f"ssl{i}")
                wait_empty(pe, f"ssc{i}")
                for k in range(KD):
                    pe.wait_ge(nsq_ready, KD * i + k + 1)
                    ml = pe.matmul(bank(f"ssl{i}", 0, LAT), ones[:, :], sq[:, k % 2, 0:LAT],
                                   start=(k == 0), stop=(k == KD - 1))
                    mc = pe.matmul(bank(f"ssc{i}", 0, CTX), ones[:, :], sq[:, k % 2, LAT:T],
                                   start=(k == 0), stop=(k == KD - 1))
                    if k == KD - 1:
                        ml.then_inc(*fills(f"ssl{i}"))
                        mc.then_inc(*fills(f"ssc{i}"))
                    else:
                        mc.then_inc(nsq_used, 1)

            def ada_rows(lay, n, halves=(0, 1)):
                name, u = f"row{lay}_{n}", unit_of[(f"ada{lay}", n)]
                if halves[0] == 0:
                    wait_empty(pe, name)
                for r in halves:
                    pe.wait_ge(front_used[(u + r) % FRING], (u + r) // FRING + 1)
                    for k in range(KH):
                        for part in range(2):
                            mm = pe.matmul(bank(name, 0, UC, 4), cond_parts[:, KH * r + k, :],
                                           ada_w[r][:, part, k, :], start=(r == 0 and k == 0 and part == 0),
                                           stop=(r == 1 and k == KH - 1 and part == 1))
                    mm.then_inc(ada_used[r], 1)

            def ada_turn(lay, n):
                name = f"col{lay}_{n}"
                wait_empty(pe, name)
                pe.wait_ge(*taken(f"row{lay}_{n}"))
                for c in range(UC // P):
                    mm = pe.matmul(bank(name, 2 * c, 2 * c + 2), ada_row[0:4, n % 2, P * c:P * (c + 1)],
                                   add_parts[0:4, :], start=True, stop=True)
                mm.then_inc(*fills(name))

            pe.wait_ge(consts_set, 2)
            norm_stats(0)
            pe.wait_ge(cond_ready, 3)
            for n in range(6):
                ada_rows(0, n)
                if n in (1, 2, 3, 5):
                    ada_turn(0, n - 1)
                if n == 3:
                    ada_turn(0, 3)

            def project(n):
                kind, h = HEADS[n]
                m = 2 if kind == "k" else h // 4
                c = h if kind == "k" else h % 4
                w = front_unit("qkv", m, (0,))
                wait_empty(pe, f"hl{n}")
                wait_empty(pe, f"hc{n}")
                for k in range(KD):
                    if k == KH:
                        landed("qkv", m, 1)
                    if n == 0:
                        pe.wait_ge(h_ready, k + 1)
                    ml = pe.matmul(bank(f"hl{n}", 0, LAT), w(k)[:, P * c:P * (c + 1)],
                                   hA[:, k, 0:LAT], start=(k == 0), stop=(k == KD - 1))
                    mc = pe.matmul(bank(f"hc{n}", 0, CTX), w(k)[:, P * c:P * (c + 1)],
                                   hA[:, k, LAT:T], start=(k == 0), stop=(k == KD - 1))
                    if kind == "q" and c == 3 and k == KH - 1:
                        mc.then_inc(*first_half_used("qkv", m))
                ml.then_inc(*fills(f"hl{n}"))
                mc.then_inc(*fills(f"hc{n}"))

            def values():
                w = front_unit("qkv", 2)
                for t in range(TT):
                    name = f"v{t // 2}"
                    if t % 2 == 0:
                        wait_empty(pe, name)
                    o = NKV * HD * (t % 2)
                    for k in range(KD):
                        mm = pe.matmul(bank(name, o, o + NKV * HD), hA[:, k, P * t:P * (t + 1)],
                                       w(k)[:, NKV * HD:2 * NKV * HD], start=(k == 0), stop=(k == KD - 1))
                        if t == TT - 1 and k == KH - 1:
                            mm.then_inc(*first_half_used("qkv", 2))
                    if t % 2 == 1 or t == TT - 1:
                        mm.then_inc(*fills(name))

            def head_stats(n):
                wait_empty(pe, f"hsl{n}")
                wait_empty(pe, f"hsc{n}")
                pe.wait_ge(hsq_ready, n + 1)
                pe.matmul(bank(f"hsl{n}", 0, LAT), ones[:, :], sqh[:, n % 2, 0:LAT],
                          start=True, stop=True).then_inc(*fills(f"hsl{n}"))
                pe.matmul(bank(f"hsc{n}", 0, CTX), ones[:, :], sqh[:, n % 2, LAT:T],
                          start=True, stop=True).then_inc(*fills(f"hsc{n}"))

            def rotate(n):
                wait_empty(pe, f"rot{n}")
                pe.wait_ge(hnorm_ready, n + 1)
                if n == 0:
                    pe.wait_ge(tab_loaded, 16)
                pe.matmul(bank(f"rot{n}", 0, LAT), swap, raw[:, n % 2, 0:LAT],
                          start=True, stop=True).then_inc(*fills(f"rot{n}"))

            for n in range(len(HEADS) + 2):
                if n < len(HEADS):
                    project(n)
                if n == 1:
                    values()
                if 1 <= n <= len(HEADS):
                    head_stats(n - 1)
                if n >= 2:
                    rotate(n - 2)
                if n in TURN_AFTER_HEAD:
                    ada_turn(*TURN_AFTER_HEAD[n])
                if n in ADA_AFTER_HEAD:
                    ada_rows(*ADA_AFTER_HEAD[n])

            pe.wait_ge(cache_loaded, 32)
            wait_empty(pe, "cachek")
            for g in range(NKV):
                mm = pe.transpose(bank("cachek", P * g, P * (g + 1)),
                                  cache_rows[:, HD * g:HD * (g + 1)], ident)
            mm.then_inc(*fills("cachek"))
            wait_empty(pe, "newk")
            pe.wait_ge(head_ready, NKV)
            for g in range(NKV):
                mm = pe.transpose(bank("newk", P * g, P * (g + 1)), kTc[:, g, :], ident)
            mm.then_inc(*fills("newk"))

            def scores(n):
                h, t = n // TT, n % TT
                g = h // G
                wait_empty(pe, f"S{n}")
                if t == 0:
                    pe.wait_ge(head_ready, NKV + h + 1)
                q = qT[:, h, P * t:P * (t + 1)]
                if t < LT:
                    if n == 0:
                        pe.wait_ge(*taken("cachek"))
                        pe.wait_ge(*taken("v2"))
                    pe.matmul(bank(f"S{n}", 0, LAT), q, kT[:, g, 0:LAT], start=True, stop=True)
                    mm = pe.matmul(bank(f"S{n}", LAT, KEYS), q, kT[:, g, LAT:KEYS], start=True, stop=True)
                else:
                    mm = pe.matmul(bank(f"S{n}", 0, CTX), q, kTc[:, g, :], start=True, stop=True)
                mm.then_inc(*fills(f"S{n}"))

            def probs_turn(n):
                wait_empty(pe, f"T{n}")
                pe.wait_ge(probs_ready, n + 1)
                for c in range(TT if n % TT < LT else 1):
                    mm = pe.transpose(bank(f"T{n}", P * c, P * (c + 1)),
                                      probs[:, n % 3, P * c:P * (c + 1)], ident)
                mm.then_inc(*fills(f"T{n}"))

            def weigh(n):
                h, t = n // TT, n % TT
                g = h // G
                wait_empty(pe, f"O{n}")
                pe.wait_ge(*taken(f"T{n}"))
                if t == LT - 1:
                    for c in range(TT):
                        mm = pe.matmul(bank(f"O{n}", 0, LAT), V[:, c, HD * g:HD * (g + 1)],
                                       pT[:, c, :], start=(c == 0), stop=(c == TT - 1))
                else:
                    mm = pe.matmul(bank(f"O{n}", 0, CTX), V[:, TT, HD * g:HD * (g + 1)], pTc[:, :],
                                   start=True, stop=True)
                mm.then_inc(*fills(f"O{n}"))

            for n in range(NH * TT + 3):
                if n < NH * TT:
                    scores(n)
                unit, part = ADA_AHEAD + n // 3, n % 3
                if part == 0 and ADA_AHEAD < unit <= 12:
                    ada_turn(1, unit - 1)
                if 2 <= n < NH * TT + 2:
                    probs_turn(n - 2)
                if unit < ADA_UNITS and part < 2:
                    ada_rows(1, unit, (part,))
                if n >= 3 and (n - 3) % TT >= TT - 2:
                    weigh(n - 3)

            pe.wait_ge(*taken(f"O{NH * TT - 1}"))
            for d in range(KD):
                w = front_unit("wo", d // 4)
                c = d % 4
                wait_empty(pe, f"wol{d}")
                wait_empty(pe, f"woc{d}")
                for h in range(NH):
                    ml = pe.matmul(bank(f"wol{d}", 0, LAT), w(h)[:, P * c:P * (c + 1)],
                                   oT[:, h, 0:LAT], start=(h == 0), stop=(h == NH - 1))
                    mc = pe.matmul(bank(f"woc{d}", 0, CTX), w(h)[:, P * c:P * (c + 1)],
                                   oT[:, h, LAT:T], start=(h == 0), stop=(h == NH - 1))
                    if c == 3 and h == KH - 1:
                        mc.then_inc(*first_half_used("wo", d // 4))
                ml.then_inc(*fills(f"wol{d}"))
                mc.then_inc(*fills(f"woc{d}"))

            def pool_products():
                norm_stats(2)
                pe.wait_ge(raw_full[POOL_UNIT % RRING], 16 * (POOL_UNIT // RRING + 1))
                w = raw_w[POOL_UNIT % RRING][:, :, :].rearrange("p k (h n) -> p (k h) n", h=2)
                for k in range(KD):
                    g = k // 2
                    wait_empty(pe, f"pl{k}")
                    wait_empty(pe, f"pc{k}")
                    pe.wait_ge(pooled_ready, g + 1)
                    for c in range(2):
                        wc = w[:, 2 * g + c, P * (k % 2):P * (k % 2 + 1)]
                        ml = pe.matmul(bank(f"pl{k}", 0, LAT), wc, pooled[:, 2 * g + c, 0:LAT],
                                       start=(c == 0), stop=(c == 1))
                        mc = pe.matmul(bank(f"pc{k}", 0, CTX), wc, pooled[:, 2 * g + c, LAT:T],
                                       start=(c == 0), stop=(c == 1))
                    ml.then_inc(*fills(f"pl{k}"))
                    mc.then_inc(*fills(f"pc{k}"))

            def route(lay):
                norm_stats(2 * lay + 1)
                if lay == 0:
                    pe.wait_ge(wr_loaded, 32)
                wait_empty(pe, f"rl{lay}")
                wait_empty(pe, f"rc{lay}")
                for k in range(KD):
                    pe.wait_ge(h_ready, KD * (2 * lay + 1) + k + 1)
                    ml = pe.matmul(bank(f"rl{lay}", 0, LAT, NE), wr[:, lay, k, :], h2T[:, k, 0:LAT],
                                   start=(k == 0), stop=(k == KD - 1))
                    mc = pe.matmul(bank(f"rc{lay}", 0, CTX, NE), wr[:, lay, k, :], h2T[:, k, LAT:T],
                                   start=(k == 0), stop=(k == KD - 1))
                ml.then_inc(*fills(f"rl{lay}"))
                mc.then_inc(*fills(f"rc{lay}"))
                def turn_h(n):
                    t, half = n // 2, n % 2
                    name = f"ht{lay}_{n}"
                    wait_empty(pe, name)
                    for k in range(4):
                        mm = pe.transpose(bank(name, P * k, P * (k + 1)),
                                          h2T[:, 4 * half + k, P * t:P * (t + 1)], ident)
                    mm.then_inc(*fills(name))

                turn_h(0)
                wait_empty(pe, f"rt{lay}")
                pe.wait_ge(*taken(f"rl{lay}"))
                pe.wait_ge(*taken(f"rc{lay}"))
                for t in range(TT):
                    mm = pe.transpose(bank(f"rt{lay}", NE * t, NE * (t + 1)), work[0:NE, P * t:P * (t + 1)],
                                      ident[0:NE, 0:NE])
                mm.then_inc(*fills(f"rt{lay}"))
                turn_h(1)
                turn_h(2)
                wait_empty(pe, f"afl{lay}")
                wait_empty(pe, f"afc{lay}")
                pe.wait_ge(aff_ready, lay + 1)
                for t in range(LT):
                    mm = pe.transpose(bank(f"afl{lay}", P * t, P * (t + 1), NE), aff[:, t, :], ident)
                mm.then_inc(*fills(f"afl{lay}"))
                pe.transpose(bank(f"afc{lay}", 0, P, NE), aff[:, LT, :], ident).then_inc(*fills(f"afc{lay}"))
                for n in range(3, 2 * TT):
                    turn_h(n)
                wait_empty(pe, f"sl{lay}")
                pe.wait_ge(slots_ready, lay + 1)
                for t in range(TT):
                    mm = pe.transpose(bank(f"sl{lay}", NE * t, NE * (t + 1)),
                                      cum[0:NE, P * t:P * (t + 1)], ident[0:NE, 0:NE])
                mm.then_inc(*fills(f"sl{lay}"))
                pe.wait_ge(*taken(f"ht{lay}_{2 * TT - 1}"))

            def gather_latent(L, half, n_pick, i=0):
                if half == 1:
                    pe.wait_ge(pick_ready, n_pick)
                name = L + f"XE{half}"
                wait_empty(pe, name, i)
                for k in range(4):
                    kk = 4 * half + k
                    for c in range(LT):
                        mm = pe.matmul(bank(name, P * k, P * (k + 1)),
                                       h_rows[:, c, P * kk:P * (kk + 1)],
                                       pick[:, c, :, :].rearrange("p e s -> p (e s)"),
                                       start=(c == 0), stop=(c == LT - 1))
                mm.then_inc(*fills(name))

            def gather_context(L, i=0):
                wait_empty(pe, L + "XEc", i)
                for k in range(KD):
                    mm = pe.matmul(bank(L + "XEc", SEL_C * k, SEL_C * (k + 1)),
                                   h_rows[:, LT, P * k:P * (k + 1)],
                                   pick_c[:, :, :].rearrange("p e s -> p (e s)"), start=True, stop=True)
                mm.then_inc(*fills(L + "XEc"))

            def expert_pair(lay, L, pair, i, last):
                per_s, per_r = ((0, 0) if last else (UNITS // SRING * i, UNITS // RRING * i))
                gp = NP * lay + pair
                first_s = SPLITS * lay + (SPLITS - UNITS if last else 0)
                first_r = base[lay] + (SPLITS - UNITS if last else 0)

                def split_unit(m):
                    r = first_r + m
                    pe.wait_ge(raw_used[r % RRING], r // RRING + 1 + per_r)
                    return split_w[(first_s + m) % SRING]

                def three_passes(name, e, m, high, low, half, closes, between=None):
                    w = split_unit(m)
                    for k in range(KH):
                        if between and k == KH // 2:
                            between()
                        kk = KH * half + k
                        for j, (x, part) in enumerate(((high, 0), (high, 1), (low, 0))):
                            mm = pe.matmul(bank(name, 0, UC, ROWS[e]), x(kk), w[:, part, k, :],
                                           start=(half == 0 and k == 0 and j == 0),
                                           stop=(half == 1 and k == KH - 1 and j == 2))
                    if closes:
                        mm.then_inc(*fills(name))
                    else:
                        mm.then_inc(split_used[(first_s + m) % SRING], 1)

                def turn_hidden(e, half):
                    name = L + f"T{e}{half}"
                    wait_empty(pe, name, i)
                    pe.wait_ge(*taken(L + f"U{e}{half}", i))
                    for k in range(4):
                        mm = pe.transpose(bank(name, ROWS[e] * k, ROWS[e] * (k + 1)),
                                          hid[0:ROWS[e], half, P * k:P * (k + 1)], ident[0:ROWS[e], 0:ROWS[e]])
                    mm.then_inc(*fills(name))

                for e in range(2):
                    n0 = UNITS // 2 * e

                    def tokens(part):
                        return lambda k: xe[:, part, KD * P * e + P * k:KD * P * e + P * k + ROWS[e]]

                    def hidden(part):
                        return lambda k: hT[:, part, k, 0:ROWS[e]]

                    def gate_up(m, kind, c):
                        name = L + f"{kind}{e}{c}"
                        wait_empty(pe, name, i)
                        for r in range(2):
                            three_passes(name, e, n0 + m + r, tokens(0), tokens(1), r, r == 1)

                    gate_up(0, "G", 0)
                    gate_up(2, "U", 0)
                    if e == 0:
                        wait_empty(pe, L + "PT", i)
                        wait_empty(pe, L + "PTc", i)
                        for c in range(LT):
                            mm = pe.transpose(bank(L + "PT", P * c, P * (c + 1)),
                                              pick[:, c, :, :].rearrange("p e s -> p (e s)"), ident)
                        mm.then_inc(*fills(L + "PT"))
                        wide = pick_w[:, :, :].rearrange("p e s -> p (e s)")
                        es = bass.ds(2 * pair, 2)
                        pe.transpose(bank(L + "PTc", 0, CTX), wide, ident)
                        for c in range(LT):
                            pe.matmul(bank(L + "PTc", CTX, CTX + 2), pick[:, c, :, :].rearrange("p e s -> p (e s)"),
                                      aff[:, c, es], start=(c == 0), stop=(c == LT - 1))
                        pe.matmul(bank(L + "PTc", CTX + 2, CTX + 4), wide, aff[:, LT, es],
                                  start=True, stop=True).then_inc(*fills(L + "PTc"))
                    gate_up(4, "G", 1)
                    turn_hidden(e, 0)
                    gate_up(6, "U", 1)
                    if e == 1 and not last:
                        gather_latent(L, 1, 3 * gp + 6, i)
                    for c in range(2):
                        wait_empty(pe, L + f"D{e}{c}", i)
                        if c == 0:
                            pe.wait_ge(*taken(L + f"T{e}0", i))
                        three_passes(L + f"D{e}{c}", e, n0 + 8 + c, hidden(0), hidden(1), 0, False,
                                     (lambda: turn_hidden(e, 1)) if c == 1 else None)
                    if e == 1 and not last:
                        gather_context(L, i)
                    pe.wait_ge(*taken(L + f"T{e}1", i))
                    for c in range(2):
                        three_passes(L + f"D{e}{c}", e, n0 + 10 + c, hidden(0), hidden(1), 1, True)

                if not last:
                    gather_latent(L, 0, 3 * gp + 6, i)

                pe.wait_ge(*taken(L + "PTc", i))
                for d in range(KD):
                    name = L + f"C{d}"
                    wait_empty(pe, name, i)
                    if d % 4 == 0:
                        pe.wait_ge(*taken(L + f"D1{d // 4}", i))
                    pe.matmul(bank(name, 0, LAT), ye[:, 0, P * d:P * (d + 1)], put[:, :], start=True, stop=False)
                    pe.matmul(bank(name, 0, LAT), ye[:, 1, P * d:P * (d + 1)], put[:, :],
                              start=False, stop=True).then_inc(*fills(name))
                for half in range(2):
                    name = L + f"Cc{half}"
                    wait_empty(pe, name, i)
                    for k in range(4):
                        d = 4 * half + k
                        pe.matmul(bank(name, P * k, P * (k + 1)), ye_c[0:CAP, 0, P * d:P * (d + 1)],
                                  put_c[0:CAP, :], start=True, stop=False)
                        mm = pe.matmul(bank(name, P * k, P * (k + 1)), ye_c[0:CAP, 1, P * d:P * (d + 1)],
                                       put_c[0:CAP, :], start=False, stop=True)
                    mm.then_inc(*fills(name))

            for lay in range(2):
                if lay == 1:
                    pool_products()
                route(lay)
                for half in (1, 0):
                    gather_latent(f"L{lay}g", half, 3 * NP * lay + 3)
                gather_context(f"L{lay}g")
                with pe.Fori(0, NP - 1) as i:
                    expert_pair(lay, f"L{lay}", i, i, False)
                expert_pair(lay, f"L{lay}z", NP - 1, 0, True)

            pe.wait_ge(*taken("L1zCc1"))
            for n in range(2 * TT):
                t, half = n // 2, n % 2
                name = f"y{n}"
                wait_empty(pe, name)
                for k in range(4):
                    mm = pe.transpose(bank(name, P * k, P * (k + 1)),
                                      xT[:, 4 * half + k, P * t:P * (t + 1)], ident)
                mm.then_inc(*fills(name))

        @block.scalar
        def _(act):
            act.dma_start(ident, a["tables"][:, T_ID:T_ID + P]).then_inc(ident_loaded, 16)
            rows = [(V_C, V_CTX, a["c"].rearrange("a (k p) -> (a k) p", p=P)),
                    (V_CTX, V_N1, a["c_ctx"].rearrange("(k p) -> k p", p=P)),
                    (V_N1, V_N2, a["norm1"].rearrange("a (k p) -> (a k) p", p=P)),
                    (V_N2, V_PS, a["norm2"].rearrange("a (k p) -> (a k) p", p=P)),
                    (V_PS, V_Q, a["pool_scale"].rearrange("a (k p) -> (a k) p", p=P)),
                    (V_Q, V_K, a["q_norm"]), (V_K, V_ROWS, a["k_norm"])]
            for lo, hi, src in rows:
                act.dma_start(vec_rows[lo:hi, :], src).then_inc(vec_loaded, 16)
            act.dma_start(bada_rows[0:2 * MC, :],
                          a["b_ada"].rearrange("l (m p) -> (l m) p", p=P)).then_inc(bada_loaded, 16)
            act.dma_start(tab[:, T_SWAP:T_COS], a["tables"][:, T_SWAP:T_COS]).then_inc(tab_loaded, 16)
            act.dma_start(cos, a["tables"][:, T_COS:T_SIN]).then_inc(trig_loaded, 16)
            act.dma_start(sin, a["tables"][:, T_SIN:T_COLS]).then_inc(trig_loaded, 16)
            act.dma_start(cache_rows, a["cache_k"][0, 0].rearrange("t h d -> t (h d)")).then_inc(cache_loaded, 16)
            act.dma_start(V[:, LT, :], a["cache_v"][0, 0].rearrange("t h d -> t (h d)")).then_inc(cache_loaded, 16)
            for lay in range(2):
                act.dma_start(wr[:, lay, :, :],
                              a["w_router"][lay].rearrange("(k p) e -> p k e", p=P)).then_inc(wr_loaded, 16)

            act.wait_ge(*taken("vec"))
            nc.scalar.activation(cond[:, :, :].rearrange("p k t -> p t k"),
                                 vec[:, V_C:V_N1].rearrange("p (t k) -> p t k", t=2),
                                 ACT.Silu).then_inc(cond_ready, 1)
            act.wait_ge(cond_ready, 1)
            nc.scalar.copy(cond_parts[:, :, 0:2], cond[:, :, :]).then_inc(cond_ready, 1)
            for n in range(1, 2 * TT, 2):
                act.wait_ge(*full(f"x{n}"))
                nc.scalar.copy(xT[:, 4:8, P * (n // 2):P * (n // 2 + 1)],
                               bank(f"x{n}", 0, 512).rearrange("p (k t) -> p k t", k=4)
                               ).then_inc(*empties(f"x{n}"))

            def round_ada(idx, halves=(0, 1)):
                u = unit_of[(f"ada{idx // ADA_UNITS}", idx % ADA_UNITS)]
                for r in halves:
                    act.wait_ge(front_full[(u + r) % FRING], 16 * ((u + r) // FRING + 1))
                    if idx > 0:
                        act.wait_ge(ada_used[r], idx)
                    nc.scalar.copy(ada_w[r][:, 0, :, :], fring[(u + r) % FRING][:, :, :]).then_inc(ada_rounded, 1)

            def keep_row(idx):
                lay, n = idx // ADA_UNITS, idx % ADA_UNITS
                name = f"row{lay}_{n}"
                act.wait_ge(*full(name))
                nc.scalar.copy(ada_row[0:4, n % 2, :], bank(name, 0, UC, 4)).then_inc(*empties(name))

            def norm(i, dst):
                lay, second = i // 2, i % 2
                for k in range(KD):
                    if k >= 2:
                        act.wait_ge(nsq_used, (KD - 1) * i + k - 1)
                    if i == 0 and k == 0:
                        act.wait_ge(*taken("x8"))
                        act.wait_ge(*taken("x9"))
                    if i == 1:
                        act.wait_ge(*taken(f"woc{k}"))
                    if i == 2 and k == 0:
                        act.wait_ge(*taken("L0zCc1"))
                    if i == 3:
                        act.wait_ge(*taken(f"pc{k}"))
                    nc.scalar.activation(sq[:, k % 2, :], xT[:, k, :], ACT.Square).then_inc(nsq_ready, 1)
                act.wait_ge(*full(f"ssl{i}"))
                if i == 0:
                    act.wait_ge(consts_set, 2)
                nc.scalar.activation(rstd[:, 0:LAT], bank(f"ssl{i}", 0, LAT), ACT.Sqrt,
                                     bias=eps[:, :], scale=1.0 / D).then_inc(*empties(f"ssl{i}"))
                act.wait_ge(*full(f"ssc{i}"))
                nc.scalar.activation(rstd[:, LAT:T], bank(f"ssc{i}", 0, CTX), ACT.Sqrt,
                                     bias=eps[:, :], scale=1.0 / D).then_inc(*empties(f"ssc{i}"))
                if i == 0:
                    for idx in range(5):
                        round_ada(idx)
                    keep_row(4)
                    round_ada(5)
                sh = SH2 if second else SH1
                for k in range(KD):
                    act.wait_ge(nscaled, KD * i + k + 1)
                    lat, ctx_ = dst(k)
                    nc.scalar.activation(lat, lat, ACT.Identity, bias=mod[lay][:, sh + k, 0:1])
                    nc.scalar.activation(ctx_, ctx_, ACT.Identity,
                                         bias=mod[lay][:, sh + k, 1:2]).then_inc(h_ready, 1)

            norm(0, lambda k: (hA[:, k, 0:LAT], hA[:, k, LAT:T]))
            keep_row(5)

            for n in range(len(HEADS) + 2):
                if n == 1:
                    for m in range(3):
                        name = f"v{m}"
                        act.wait_ge(*full(name))
                        if m < 2:
                            nc.scalar.copy(V[:, 2 * m:2 * m + 2, :],
                                           bank(name, 0, 512).rearrange("p (t c) -> p t c", t=2)
                                           ).then_inc(*empties(name))
                        else:
                            nc.scalar.copy(V[:, TT, :], bank(name, 0, NKV * HD)).then_inc(*empties(name))
                if 1 <= n <= len(HEADS):
                    m = n - 1
                    act.wait_ge(*full(f"hsl{m}"))
                    nc.scalar.activation(rrh[:, m % 2, 0:LAT], bank(f"hsl{m}", 0, LAT), ACT.Sqrt,
                                         bias=eps[:, :], scale=1.0 / HD).then_inc(*empties(f"hsl{m}"))
                    act.wait_ge(*full(f"hsc{m}"))
                    nc.scalar.activation(rrh[:, m % 2, LAT:T], bank(f"hsc{m}", 0, CTX), ACT.Sqrt,
                                         bias=eps[:, :], scale=1.0 / HD).then_inc(*empties(f"hsc{m}"))
                if n < len(HEADS):
                    act.wait_ge(raw_ready, n + 1)
                    nc.scalar.activation(sqh[:, n % 2, :], raw[:, n % 2, :], ACT.Square).then_inc(hsq_ready, 1)
                if n in ADA_AFTER_HEAD:
                    idx = ADA_UNITS * ADA_AFTER_HEAD[n][0] + ADA_AFTER_HEAD[n][1]
                    keep_row(idx)
                if n + 1 in ADA_AFTER_HEAD:
                    round_ada(ADA_UNITS * ADA_AFTER_HEAD[n + 1][0] + ADA_AFTER_HEAD[n + 1][1])
                if n == max(ADA_AFTER_HEAD):
                    round_ada(idx + 1)

            def expo(n):
                w = KEYS if n % TT < LT else CTX
                act.wait_ge(nmax_ready, n + 1)
                nc.scalar.activation(probs[:, n % 3, 0:w], bank(f"S{n}", 0, w), ACT.Exp,
                                     bias=stat[:, 4 + n % 4:5 + n % 4], scale=HD ** -0.5,
                                     accum_out=stat[:, 8 + n % 4:9 + n % 4]).then_inc(*empties(f"S{n}"))

            def keep_turned(n):
                act.wait_ge(*full(f"T{n}"))
                t = n % TT
                if t < LT:
                    nc.scalar.copy(pT[:, :, P * t:P * (t + 1)],
                                   bank(f"T{n}", 0, KEYS).rearrange("p (c q) -> p c q", q=P)
                                   ).then_inc(*empties(f"T{n}"))
                else:
                    nc.scalar.copy(pTc[:, :], bank(f"T{n}", 0, CTX)).then_inc(*empties(f"T{n}"))

            for n in range(NH * TT + 2):
                if n < NH * TT:
                    expo(n)
                if n >= 2:
                    keep_turned(n - 2)
                unit = ADA_AHEAD + n // 3
                if n % 3 < 2 and unit + 1 < ADA_UNITS:
                    round_ada(ADA_UNITS + unit + 1, (n % 3,))
                if n % 3 == 1 and unit < ADA_UNITS:
                    keep_row(ADA_UNITS + unit)

            def round_unit(lay, m, i=0, looped=False):
                s, r = SPLITS * lay + m, base[lay] + m
                act.wait_ge(raw_full[r % RRING], 16 * (r // RRING + 1) + (16 * (UNITS // RRING) * i if looped else 0))
                if looped or s >= SRING:
                    act.wait_ge(split_used[s % SRING], s // SRING + (UNITS // SRING * i if looped else 0))
                nc.scalar.copy(split_w[s % SRING][:, 0, :, :], raw_w[r % RRING][:, :, :]).then_inc(rounded, 1)

            def keep_tokens(L, i=0):
                act.wait_ge(*full(L + "XEc", i))
                for e, dst in enumerate(xe_ctx(0)):
                    ins = nc.scalar.copy(dst, bank(L + "XEc", 0, KD * SEL_C)
                                         .rearrange("p (k e s) -> p k e s", e=2, k=KD)[:, :, e, :])
                ins.then_inc(xeh_ready, 1)
                keep_latent(L, 1, i)

            def keep_latent(L, half, i=0):
                act.wait_ge(*full(L + f"XE{half}", i))
                nc.scalar.copy(xe_lat(0, half), bank(L + f"XE{half}", 0, 512)
                               .rearrange("p (k e s) -> p e k s", e=2, k=4)).then_inc(xeh_ready, 1)

            def after_unit(lay, L, pair, m, i, last):
                e, j = m // (UNITS // 2), m % (UNITS // 2)
                if j in (1, 5):
                    name = L + f"G{e}{j // 5}"
                    act.wait_ge(*full(name, i))
                    nc.scalar.activation(hid[0:ROWS[e], j // 5, :], bank(name, 0, UC, ROWS[e]),
                                         ACT.Silu).then_inc(*empties(name))
                if m == 3:
                    act.wait_ge(*full(L + "PT", i))
                    nc.scalar.copy(put[:, :], bank(L + "PT", 0, LAT)).then_inc(*empties(L + "PT"))
                    act.wait_ge(*full(L + "PTc", i))
                    nc.scalar.copy(gates[:, :], bank(L + "PTc", CTX, CTX + 4))
                    nc.scalar.copy(put_c[:, :], bank(L + "PTc", 0, CTX)).then_inc(*empties(L + "PTc"))
                if j in (5, 8):
                    half = int(j == 8)
                    name = L + f"T{e}{half}"
                    act.wait_ge(*full(name, i))
                    nc.scalar.copy(hT[:, 0, 4 * half:4 * half + 4, 0:ROWS[e]], bank(name, 0, 4 * ROWS[e])
                                   .rearrange("p (k s) -> p k s", k=4)).then_inc(hTh_ready, 1)
                if m == 21 and not last:
                    keep_tokens(L, i)
                if j in (10, 11):
                    c = j - 10
                    name = L + f"D{e}{c}"
                    act.wait_ge(*full(name, i))
                    if j == 10 and e == 0:
                        act.wait_ge(*taken(L + "PTc", i))
                    for lo, hi, dst, g in out_rows(e):
                        ins = nc.scalar.activation(dst[lo:hi, 0, UC * c:UC * (c + 1)],
                                                   psum[lo:hi, 512 * use[name][0]:512 * use[name][0] + UC],
                                                   ACT.Copy, scale=gates[lo:hi, g:g + 1])
                    ins.then_inc(yeh_ready, 1)

            def experts(lay):
                keep_tokens(f"L{lay}g")
                keep_latent(f"L{lay}g", 0)
                with act.Fori(0, NP - 1) as i:
                    for m in range(UNITS):
                        after_unit(lay, f"L{lay}", i, m, i, False)
                        if m < UNITS - 3:
                            round_unit(lay, m + SRING, i, True)
                        elif m > UNITS - 3:
                            round_unit(lay, m - 1 + SRING, i, True)
                    keep_latent(f"L{lay}", 0, i)
                    round_unit(lay, UNITS - 1 + SRING, i, True)
                for m in range(UNITS):
                    after_unit(lay, f"L{lay}z", NP - 1, m, 0, True)
                    if m + SRING < UNITS:
                        round_unit(lay, SPLITS - UNITS + m + SRING)

            for lay in range(2):
                if lay == 1:
                    norm(2, lambda k: (Z[:, k, Z_L:Z_L + LAT], Z[:, k, Z_C:Z_C + CTX]))
                norm(2 * lay + 1, lambda k: (h2T[:, k, 0:LAT], h2T[:, k, LAT:T]))
                act.wait_ge(*taken(f"rt{lay}"))
                nc.scalar.activation(slot[:, :, :], aff[:, :, :], ACT.Exp).then_inc(aexp_ready, 1)
                for n in range(2 * TT):
                    name = f"ht{lay}_{n}"
                    act.wait_ge(*full(name))
                    nc.scalar.copy(h_rows[:, n // 2, 512 * (n % 2):512 * (n % 2 + 1)],
                                   bank(name, 0, 512)).then_inc(*empties(name))
                for m in range(SRING):
                    round_unit(lay, m)
                if lay == 0:
                    act.wait_ge(new_v_stored, 16)
                act.wait_ge(zeros_set, lay + 1)
                act.wait_ge(out_zeros_set, lay + 1)
                experts(lay)
            for n in range(1, 2 * TT, 2):
                act.wait_ge(*full(f"y{n}"))
                nc.scalar.copy(y_rows[:, n // 2, 512:1024], bank(f"y{n}", 0, 512)).then_inc(*empties(f"y{n}"))

        @block.vector
        def _(dve):
            dve_steps = [0]

            def own(ins):
                dve_steps[0] += 1
                ins.then_inc(dve_step, 1)
                dve.wait_ge(dve_step, dve_steps[0])

            nc.vector.memset(ones[:, :], 1.0).then_inc(consts_set, 1)
            nc.vector.memset(eps[:, :], EPS).then_inc(consts_set, 1)
            dve.wait_ge(*full("vec"))
            nc.vector.tensor_copy(vec[:, :], bank("vec", 0, V_ROWS)).then_inc(*empties("vec"))
            dve.wait_ge(*full("bada"))
            nc.vector.tensor_copy(bada[:, :], bank("bada", 0, 2 * MC)).then_inc(*empties("bada"))
            dve.wait_ge(ident_loaded, 16)
            nc.vector.tensor_tensor(add_parts[0:4, :], ident[0:4, 0:2], ident[0:4, 2:4], ALU.add)
            dve.wait_ge(cond_ready, 2)
            nc.vector.tensor_tensor(cond_parts[:, :, 2:4], cond[:, :, :], cond_parts[:, :, 0:2].bitcast(F32),
                                    ALU.subtract).then_inc(cond_ready, 1)
            for n in range(0, 2 * TT, 2):
                dve.wait_ge(*full(f"x{n}"))
                nc.vector.tensor_copy(xT[:, 0:4, P * (n // 2):P * (n // 2 + 1)],
                                      bank(f"x{n}", 0, 512).rearrange("p (k t) -> p k t", k=4)
                                      ).then_inc(*empties(f"x{n}"))

            def take_mod(lay, n):
                name, c0 = f"col{lay}_{n}", UC // P * n
                c1 = c0 + UC // P
                dve.wait_ge(*full(name))
                nc.vector.tensor_tensor(
                    mod[lay][:, c0:c1, :], bank(name, 0, 2 * UC // P).rearrange("p (c t) -> p c t", t=2),
                    bada[:, MC * lay + c0:MC * lay + c1].unsqueeze(2).to_broadcast([P, c1 - c0, 2]),
                    ALU.add).then_inc(*empties(name))

            def set_amp(i):
                lay, second = i // 2, i % 2
                sc = SC2 if second else SC1
                g = (V_N2 if second else V_N1) + KD * lay
                own(nc.vector.scalar_tensor_tensor(
                    out=amp[i][:, :, :], in0=mod[lay][:, sc:sc + KD, :], scalar=1.0,
                    in1=vec[:, g:g + KD].unsqueeze(2).to_broadcast([P, KD, 2]), op0=ALU.add, op1=ALU.mult))

            def set_rstd(i):
                dve.wait_ge(*taken(f"ssl{i}"))
                dve.wait_ge(*taken(f"ssc{i}"))
                own(nc.vector.reciprocal(rstd[:, :], rstd[:, :]))

            def norm(i, dst):
                if i > 0:
                    set_rstd(i)
                for k in range(KD):
                    lat, ctx_ = dst(k)
                    nc.vector.scalar_tensor_tensor(out=lat, in0=xT[:, k, 0:LAT], scalar=amp[i][:, k, 0:1],
                                                   in1=rstd[:, 0:LAT], op0=ALU.mult, op1=ALU.mult)
                    nc.vector.scalar_tensor_tensor(out=ctx_, in0=xT[:, k, LAT:T], scalar=amp[i][:, k, 1:2],
                                                   in1=rstd[:, LAT:T], op0=ALU.mult, op1=ALU.mult
                                                   ).then_inc(nscaled, 1)

            def low_ada(n, r):
                u = unit_of[("ada0", n)] + r
                dve.wait_ge(ada_rounded, 2 * n + r + 1)
                nc.vector.tensor_tensor(ada_w[r][:, 1, :, :], fring[u % FRING][:, :, :],
                                        ada_w[r][:, 0, :, :].bitcast(F32),
                                        ALU.subtract).then_inc(front_used[u % FRING], 1)

            dve.wait_ge(*taken("bada"))
            low_ada(0, 0)
            low_ada(0, 1)
            for n in range(4):
                if n < 3:
                    low_ada(n + 1, 0)
                name = f"row0_{n}"
                dve.wait_ge(*full(name))
                nc.vector.tensor_copy(ada_row[0:4, n % 2, :], bank(name, 0, UC, 4)).then_inc(*empties(name))
                if n < 3:
                    low_ada(n + 1, 1)
                if n == 2:
                    set_rstd(0)
                if n > 0:
                    take_mod(0, n - 1)
            take_mod(0, 3)
            dve.wait_ge(*taken("col0_3"))
            set_amp(0)
            dve.wait_ge(*taken("x9"))
            norm(0, lambda k: (hA[:, k, 0:LAT], hA[:, k, LAT:T]))
            take_mod(0, 4)

            def head_dst(n):
                kind, h = HEADS[n]
                return (kT[:, h, 0:LAT], kTc[:, h, :]) if kind == "k" else (qT[:, h, 0:LAT], qT[:, h, LAT:T])

            def take_head(n):
                dve.wait_ge(*full(f"hl{n}"))
                nc.vector.tensor_copy(raw[:, n % 2, 0:LAT], bank(f"hl{n}", 0, LAT)).then_inc(*empties(f"hl{n}"))
                dve.wait_ge(*full(f"hc{n}"))
                nc.vector.tensor_copy(raw[:, n % 2, LAT:T], bank(f"hc{n}", 0, CTX)).then_inc(*empties(f"hc{n}"))
                nc.vector.engine_nop().then_inc(raw_ready, 1)

            def norm_head(n):
                g = V_K if HEADS[n][0] == "k" else V_Q
                dve.wait_ge(*taken(f"hsl{n}"))
                dve.wait_ge(*taken(f"hsc{n}"))
                own(nc.vector.reciprocal(rrh[:, n % 2, :], rrh[:, n % 2, :]))
                nc.vector.scalar_tensor_tensor(out=raw[:, n % 2, 0:LAT], in0=raw[:, n % 2, 0:LAT],
                                               scalar=vec[:, g:g + 1], in1=rrh[:, n % 2, 0:LAT],
                                               op0=ALU.mult, op1=ALU.mult).then_inc(hnorm_ready, 1)
                nc.vector.scalar_tensor_tensor(out=head_dst(n)[1], in0=raw[:, n % 2, LAT:T],
                                               scalar=vec[:, g:g + 1], in1=rrh[:, n % 2, LAT:T],
                                               op0=ALU.mult, op1=ALU.mult)

            def finish_head(n):
                if n == 0:
                    dve.wait_ge(trig_loaded, 32)
                dst = head_dst(n)[0]
                dve.wait_ge(*full(f"rot{n}"))
                dve.wait_ge(hnorm_ready, n + 1)
                nc.vector.tensor_tensor(dst, raw[:, n % 2, 0:LAT], cos, ALU.mult)
                nc.vector.tensor_tensor(sqh[:, n % 2, 0:LAT], bank(f"rot{n}", 0, LAT), sin,
                                        ALU.mult).then_inc(*empties(f"rot{n}"))
                dve.wait_ge(*taken(f"rot{n}"))
                nc.vector.tensor_tensor(dst, dst, sqh[:, n % 2, 0:LAT], ALU.add).then_inc(head_ready, 1)

            for n in range(len(HEADS) + 2):
                if n >= 2:
                    finish_head(n - 2)
                if n < len(HEADS):
                    take_head(n)
                if 1 <= n <= len(HEADS):
                    norm_head(n - 1)
                if n in TURN_AFTER_HEAD:
                    take_mod(*TURN_AFTER_HEAD[n])

            dve.wait_ge(*taken("col0_11"))
            set_amp(1)
            dve.wait_ge(*full("cachek"))
            nc.vector.tensor_copy(kT[:, :, LAT:KEYS], bank("cachek", 0, NKV * HD)
                                  .rearrange("p (g t) -> p g t", g=NKV)).then_inc(*empties("cachek"))
            dve.wait_ge(*full("newk"))
            nc.vector.tensor_copy(new_k[:, :], bank("newk", 0, NKV * HD)).then_inc(*empties("newk"))

            def tile_max(n):
                w = KEYS if n % TT < LT else CTX
                dve.wait_ge(*full(f"S{n}"))
                own(nc.vector.tensor_reduce(stat[:, n % 4:n % 4 + 1], bank(f"S{n}", 0, w), AX.X, ALU.max))
                nc.vector.tensor_scalar(stat[:, 4 + n % 4:5 + n % 4], stat[:, n % 4:n % 4 + 1], -HD ** -0.5,
                                        None, ALU.mult).then_inc(nmax_ready, 1)

            def tile_probs(n):
                w = KEYS if n % TT < LT else CTX
                dve.wait_ge(*taken(f"S{n}"))
                own(nc.vector.reciprocal(stat[:, 12 + n % 4:13 + n % 4], stat[:, 8 + n % 4:9 + n % 4]))
                nc.vector.tensor_scalar(probs[:, n % 3, 0:w], probs[:, n % 3, 0:w],
                                        stat[:, 12 + n % 4:13 + n % 4], None, ALU.mult
                                        ).then_inc(probs_ready, 1)

            for n in range(NH * TT + 4):
                if n < NH * TT:
                    tile_max(n)
                if n % 3 == 0 and 1 <= n // 3 <= 12 - ADA_AHEAD:
                    take_mod(1, ADA_AHEAD + n // 3 - 1)
                if 1 <= n <= NH * TT:
                    tile_probs(n - 1)
                m = n - 4
                if m >= 0 and m % TT >= LT - 1:
                    lo, hi = (0, LAT) if m % TT == LT - 1 else (LAT, T)
                    dve.wait_ge(*full(f"O{m}"))
                    nc.vector.tensor_copy(oT[:, m // TT, lo:hi],
                                          bank(f"O{m}", 0, hi - lo)).then_inc(*empties(f"O{m}"))
            dve.wait_ge(*taken("col1_11"))
            set_amp(2)
            set_amp(3)
            own(nc.vector.tensor_tensor(gate_pool[:, :, :], mod[1][:, G1:G1 + KD, :],
                                        vec[:, V_PS:V_PS + KD].unsqueeze(2).to_broadcast([P, KD, 2]), ALU.mult))

            def add_mixed(k, lat, ctx_, gate):
                dve.wait_ge(*full(lat))
                nc.vector.scalar_tensor_tensor(out=xT[:, k, 0:LAT], in0=bank(lat, 0, LAT), scalar=gate[:, k, 0:1],
                                               in1=xT[:, k, 0:LAT], op0=ALU.mult, op1=ALU.add
                                               ).then_inc(*empties(lat))
                dve.wait_ge(*full(ctx_))
                nc.vector.scalar_tensor_tensor(out=xT[:, k, LAT:T], in0=bank(ctx_, 0, CTX),
                                               scalar=gate[:, k, 1:2], in1=xT[:, k, LAT:T],
                                               op0=ALU.mult, op1=ALU.add).then_inc(*empties(ctx_))

            for k in range(KD):
                add_mixed(k, f"wol{k}", f"woc{k}", mod[0][:, G1:G1 + KD, :])

            def pool_windows():
                for lo, hi in ((0, Z_L), (Z_L + LAT, Z_C), (Z_C + CTX, ZW)):
                    nc.vector.memset(Z[:, :, lo:hi], 0.0)
                norm(2, lambda k: (Z[:, k, Z_L:Z_L + LAT], Z[:, k, Z_C:Z_C + CTX]))
                for g, w in enumerate(WINDOWS):
                    dve.wait_ge(h_ready, 2 * KD + 2 * g + 2)
                    if g > 0:
                        dve.wait_ge(pooled_ready, g)
                    z = Z[:, 2 * g:2 * g + 2, :]
                    src, lo, hi, reach = z, 1, ZW, 0
                    for s in range(g + 1):
                        dst = win[s % 2]
                        left, right = (1, 0) if s == 0 else (reach, reach)
                        own(nc.vector.tensor_tensor(dst[:, :, lo:hi], src[:, :, lo - left:hi - left],
                                                    src[:, :, lo + right:hi + right], ALU.add))
                        src, reach = dst, max(1, 2 * reach)
                        lo, hi = lo + reach, hi - reach
                    inv = T_INV + CTX * g
                    d = pooled[:, 2 * g:2 * g + 2, :]
                    half = CTX // 2
                    for at, n, tcol in ((Z_L, half, 0), (Z_L + LAT - half, half, half), (Z_C, CTX, 0)):
                        ins = nc.vector.tensor_tensor(
                            src[:, :, at:at + n], src[:, :, at:at + n],
                            tab[:, inv + tcol:inv + tcol + n].unsqueeze(1).to_broadcast([P, 2, n]), ALU.mult)
                    nc.vector.scalar_tensor_tensor(
                        out=d[:, :, half:LAT - half], in0=src[:, :, Z_L + half:Z_L + LAT - half], scalar=1.0 / w,
                        in1=z[:, :, Z_L + half:Z_L + LAT - half], op0=ALU.mult, op1=ALU.subtract)
                    own(ins)
                    for at, n, o in ((Z_L, half, 0), (Z_L + LAT - half, half, LAT - half), (Z_C, CTX, LAT)):
                        ins = nc.vector.tensor_tensor(d[:, :, o:o + n], src[:, :, at:at + n],
                                                      z[:, :, at:at + n], ALU.subtract)
                    ins.then_inc(pooled_ready, 1)

            def route(lay):
                dve.wait_ge(*full(f"rl{lay}"))
                nc.vector.tensor_copy(work[0:NE, 0:LAT], bank(f"rl{lay}", 0, LAT, NE)).then_inc(*empties(f"rl{lay}"))
                dve.wait_ge(*full(f"rc{lay}"))
                nc.vector.tensor_copy(work[0:NE, LAT:T], bank(f"rc{lay}", 0, CTX, NE)).then_inc(*empties(f"rc{lay}"))
                logits = bank(f"rt{lay}", 0, TT * NE).rearrange("p (t e) -> p t e", e=NE)
                dve.wait_ge(*full(f"rt{lay}"))
                own(nc.vector.tensor_reduce(rmax[:, 0, :], logits, AX.X, ALU.max))
                nc.vector.tensor_tensor(aff[:, :, :], logits, rmax[:, 0, :].unsqueeze(2).to_broadcast([P, TT, NE]),
                                        ALU.subtract).then_inc(*empties(f"rt{lay}"))
                dve.wait_ge(aexp_ready, lay + 1)
                own(nc.vector.tensor_reduce(rmax[:, 1, :], slot[:, :, :], AX.X, ALU.add))
                own(nc.vector.reciprocal(rmax[:, 2, :], rmax[:, 1, :]))
                nc.vector.tensor_tensor(aff[:, :, :], slot[:, :, :],
                                        rmax[:, 2, :].unsqueeze(2).to_broadcast([P, TT, NE]),
                                        ALU.mult).then_inc(aff_ready, 1)
                dve.wait_ge(*full(f"afl{lay}"))
                nc.vector.tensor_copy(work[0:NE, 0:LAT], bank(f"afl{lay}", 0, LAT, NE)).then_inc(*empties(f"afl{lay}"))
                dve.wait_ge(*full(f"afc{lay}"))
                nc.vector.tensor_copy(work[0:NE, LAT:T], bank(f"afc{lay}", 0, CTX, NE)).then_inc(*empties(f"afc{lay}"))
                dve.wait_ge(*taken(f"afl{lay}"))
                dve.wait_ge(*taken(f"afc{lay}"))
                for lo, hi, cap in ((0, LAT, CAP_L), (LAT, T, CAP_C)):
                    for _ in range(cap // 8):
                        own(nc.vector.max(top8[0:NE, :], work[0:NE, lo:hi]))
                        own(nc.vector.match_replace(work[0:NE, lo:hi], top8[0:NE, :], work[0:NE, lo:hi], -1.0))
                own(nc.vector.tensor_scalar(mask[0:NE, :], work[0:NE, :], 0.0, None, ALU.is_lt))
                for lo, hi in ((0, LAT), (LAT, T)):
                    own(nc.vector.tensor_tensor_scan(cum[0:NE, lo:hi], mask[0:NE, lo:hi], mask[0:NE, lo:hi],
                                                     0.0, ALU.add, ALU.max))
                nc.vector.tensor_tensor(cum[0:NE, :], cum[0:NE, :], mask[0:NE, :], ALU.mult).then_inc(slots_ready, 1)
                dve.wait_ge(*full(f"sl{lay}"))
                nc.vector.tensor_copy(slot[:, :, :], bank(f"sl{lay}", 0, TT * NE)
                                      .rearrange("p (t e) -> p t e", e=NE)).then_inc(*empties(f"sl{lay}"))
                dve.wait_ge(*taken(f"sl{lay}"))

            def set_picks(pair):
                es = bass.ds(2 * pair, 2)
                iota = tab[:, T_IOTA:T_IOTA + CAP_L]
                nc.vector.tensor_tensor(
                    pick[:, :, :, :], slot[:, 0:LT, es].unsqueeze(3).to_broadcast([P, LT, 2, CAP_L]),
                    iota.unsqueeze(1).unsqueeze(1).to_broadcast([P, LT, 2, CAP_L]),
                    ALU.is_equal).then_inc(pick_ready, 1)
                nc.vector.tensor_tensor(
                    pick_c[:, :, :], slot[:, LT, es].unsqueeze(2).to_broadcast([P, 2, CAP_C]),
                    iota[:, 0:CAP_C].unsqueeze(1).to_broadcast([P, 2, CAP_C]),
                    ALU.is_equal).then_inc(pick_ready, 1)
                for e in range(2):
                    ins = nc.vector.tensor_tensor(
                        pick_w[:, 1 - e, 0:CAP_C], slot[:, LT, bass.ds(2 * pair + e, 1)].to_broadcast([P, CAP_C]),
                        iota[:, 0:CAP_C], ALU.is_equal)
                ins.then_inc(pick_ready, 1)

            def low_unit(lay, m, i=0, looped=False):
                s, r = SPLITS * lay + m, base[lay] + m
                if m % 4 == 3:
                    return
                dve.wait_ge(rounded, s + 1 + (UNITS * i if looped else 0))
                w = split_w[s % SRING]
                nc.vector.tensor_tensor(w[:, 1, :, :], raw_w[r % RRING][:, :, :], w[:, 0, :, :].bitcast(F32),
                                        ALU.subtract).then_inc(raw_used[r % RRING], 1)

            def keep_tokens(L, n, i=0):
                dve.wait_ge(xeh_ready, n + 1)
                for e, (dst, high) in enumerate(zip(xe_ctx(1), xe_ctx(0))):
                    ins = nc.vector.tensor_tensor(dst, bank(L + "XEc", 0, KD * SEL_C)
                                                  .rearrange("p (k e s) -> p k e s", e=2, k=KD)[:, :, e, :],
                                                  high.bitcast(F32), ALU.subtract)
                ins.then_inc(*empties(L + "XEc"))
                keep_latent(L, 1, n + 1, i)

            def keep_latent(L, half, n, i=0):
                dve.wait_ge(xeh_ready, n + 1)
                name = L + f"XE{half}"
                nc.vector.tensor_tensor(xe_lat(1, half), bank(name, 0, 512)
                                        .rearrange("p (k e s) -> p e k s", e=2, k=4),
                                        xe_lat(0, half).bitcast(F32), ALU.subtract).then_inc(*empties(name))

            def after_unit(lay, L, pair, m, i, last):
                e, j = m // (UNITS // 2), m % (UNITS // 2)
                gp = NP * lay + pair
                if j in (3, 7):
                    half = j // 7
                    name = L + f"U{e}{half}"
                    dve.wait_ge(*full(name, i))
                    dve.wait_ge(*taken(L + f"G{e}{half}", i))
                    h = hid[0:ROWS[e], half, :]
                    nc.vector.tensor_tensor(h, bank(name, 0, UC, ROWS[e]), h, ALU.mult).then_inc(*empties(name))
                if j in (5, 8):
                    half = int(j == 8)
                    name = L + f"T{e}{half}"
                    dve.wait_ge(hTh_ready, 4 * gp + 2 * e + half + 1)
                    nc.vector.tensor_tensor(hT[:, 1, 4 * half:4 * half + 4, 0:ROWS[e]],
                                            bank(name, 0, 4 * ROWS[e]).rearrange("p (k s) -> p k s", k=4),
                                            hT[:, 0, 4 * half:4 * half + 4, 0:ROWS[e]].bitcast(F32),
                                            ALU.subtract).then_inc(*empties(name))
                if m == 9 and not last:
                    dve.wait_ge(*full(L + "PTc", i))
                    set_picks(pair + 1)
                if m == 21 and not last:
                    keep_tokens(L, 3 * gp + 3, i)
                if j in (10, 11):
                    c = j - 10
                    name = L + f"D{e}{c}"
                    dve.wait_ge(yeh_ready, 4 * gp + 2 * e + c + 1)
                    for lo, hi, dst, g in out_rows(e):
                        ins = nc.vector.scalar_tensor_tensor(
                            out=dst[lo:hi, 1, UC * c:UC * (c + 1)],
                            in0=psum[lo:hi, 512 * use[name][0]:512 * use[name][0] + UC],
                            scalar=gates[lo:hi, g:g + 1], in1=dst[lo:hi, 0, UC * c:UC * (c + 1)].bitcast(F32),
                            op0=ALU.mult, op1=ALU.subtract)
                    ins.then_inc(*empties(name))

            def add_outputs(lay, L, i=0, between=None):
                for d in range(KD):
                    if between and d == KD // 2:
                        between()
                    name = L + f"C{d}"
                    dve.wait_ge(*full(name, i))
                    nc.vector.scalar_tensor_tensor(
                        out=xT[:, d, 0:LAT], in0=bank(name, 0, LAT), scalar=mod[lay][:, G2 + d, 0:1],
                        in1=xT[:, d, 0:LAT], op0=ALU.mult, op1=ALU.add).then_inc(*empties(name))
                for half in range(2):
                    name = L + f"Cc{half}"
                    dve.wait_ge(*full(name, i))
                    for k in range(4):
                        d = 4 * half + k
                        ins = nc.vector.scalar_tensor_tensor(
                            out=xT[:, d, LAT:T], in0=bank(name, P * k, P * (k + 1)),
                            scalar=mod[lay][:, G2 + d, 1:2], in1=xT[:, d, LAT:T], op0=ALU.mult, op1=ALU.add)
                    ins.then_inc(*empties(name))

            def experts(lay):
                nc.vector.memset(pick_w[:, :, :], 0.0)
                for part in range(2):
                    ins = nc.vector.memset(xe[:, part, KD * P:2 * KD * P].rearrange("p (k c) -> p k c", c=P)
                                           [:, :, CAP_C:CAP_L].bitcast(F32), 0.0)
                own(ins)
                nc.vector.engine_nop().then_inc(zeros_set, 1)
                set_picks(0)
                keep_tokens(f"L{lay}g", 3 * NP * lay)
                keep_latent(f"L{lay}g", 0, 3 * NP * lay + 2)
                with dve.Fori(0, NP - 1) as i:
                    for m in range(UNITS):
                        after_unit(lay, f"L{lay}", i, m, i, False)
                        if m < UNITS - 3:
                            low_unit(lay, m + SRING, i, True)
                    low_unit(lay, UNITS - 3 + SRING, i, True)
                    keep_latent(f"L{lay}", 0, 3 * (NP * lay + i) + 5, i)
                    add_outputs(lay, f"L{lay}", i, lambda: low_unit(lay, UNITS - 2 + SRING, i, True))
                    low_unit(lay, UNITS - 1 + SRING, i, True)
                for m in range(UNITS):
                    after_unit(lay, f"L{lay}z", NP - 1, m, 0, True)
                    if m + SRING < UNITS:
                        low_unit(lay, SPLITS - UNITS + m + SRING)
                add_outputs(lay, f"L{lay}z")

            for lay in range(2):
                if lay == 1:
                    pool_windows()
                    for k in range(KD):
                        add_mixed(k, f"pl{k}", f"pc{k}", gate_pool)
                norm(2 * lay + 1, lambda k: (h2T[:, k, 0:LAT], h2T[:, k, LAT:T]))
                route(lay)
                if lay == 0:
                    dve.wait_ge(new_v_stored, 16)
                experts(lay)
            for n in range(0, 2 * TT, 2):
                dve.wait_ge(*full(f"y{n}"))
                nc.vector.tensor_copy(y_rows[:, n // 2, 0:512], bank(f"y{n}", 0, 512)).then_inc(*empties(f"y{n}"))


_INS = ["x_prompt", "x_sample", "cache_k", "cache_v", "c", "c_ctx", "norm1", "norm2", "w_ada", "b_ada",
        "w_qkv", "q_norm", "k_norm", "w_o", "w_pool", "pool_scale", "w_router", "w_e_gate", "w_e_up", "w_e_down"]
_OUTS = {"y_prompt": (1, CTX, D), "y_sample": (1, LAT, D), "new_k": (1, 1, CTX, NKV, HD),
         "new_v": (1, 1, CTX, NKV, HD)}


def kernel(**inputs):
    import concourse.bacc as _bacc
    from concourse.bass_utils import run_bass_kernel_spmd as _run

    nc = _bacc.Bacc("TRN2", target_bir_lowering=False, num_devices=1)
    arrays, ins = {}, {}
    for name in _INS:
        arrays[f"in_{name}"] = np.ascontiguousarray(inputs[name])
    arrays["in_tables"] = shape_tables()
    for name, v in arrays.items():
        ins[name[3:]] = nc.dram_tensor(name, v.shape, mybir.dt.from_np(v.dtype), kind="ExternalInput").ap()
    outs = {name: nc.dram_tensor(f"out_{name}", shape, F32, kind="ExternalOutput").ap()
            for name, shape in _OUTS.items()}
    build(nc, ins, outs)
    r = _run(nc, [arrays], core_ids=[0])
    return tuple(r.results[0][f"out_{name}"] for name in _OUTS)
```
